# Optimizing a Trainium2 kernel written in Bass

```python
import jax, jax.numpy as jnp
from jax import lax
import numpy as np

D_MODEL = 1024
BATCH = 1
SEQ = 256
DEPTH = 1
DEC_BATCH = 1
DEC_SEQ = 1024
PAST_LEN = 512

GRID_W = 64
HEAD_DIM = 64
ATTN_SCALE = HEAD_DIM ** -0.5
EPS = 1e-6
NA_HEADS = 8
NA_WIDTH = NA_HEADS * HEAD_DIM
NA_KH = 8
NA_KW = 16
NA_QCB = 16
NA_KCB = 32
NA_NCB = GRID_W // NA_QCB
WA_Q_HEADS = 8
WA_KV_HEADS = 2
WA_GROUP = WA_Q_HEADS // WA_KV_HEADS
WA_WIDTH = WA_Q_HEADS * HEAD_DIM
WA_KV_WIDTH = WA_KV_HEADS * HEAD_DIM
WINDOW = 128
WA_BLOCK = 128
ROPE_HALF = HEAD_DIM // 2
ROPE_BASE = 10000.0
IN_SPLITS = (NA_WIDTH, NA_WIDTH, NA_WIDTH, NA_WIDTH,
             WA_WIDTH, WA_KV_WIDTH, WA_KV_WIDTH, WA_WIDTH,
             D_MODEL, D_MODEL)
D_IN = 4 * NA_WIDTH + 2 * WA_WIDTH + 2 * WA_KV_WIDTH + 2 * D_MODEL

kernel_name = "hybrid_natten_swa_diffusion_step"

def _rmsnorm(x):
    xf = x.astype(jnp.float32)
    return (xf * lax.rsqrt(jnp.mean(xf * xf, axis=-1, keepdims=True) + EPS)).astype(x.dtype)

def _modulation(cvec, w_ada, b_ada):
    m = jax.nn.silu(cvec) @ w_ada + b_ada
    return m[..., :D_MODEL], m[..., D_MODEL:2 * D_MODEL], m[..., 2 * D_MODEL:]

def _project(x, shift, scale, w_in):
    h = _rmsnorm(x) * (1.0 + scale) + shift
    p = h @ w_in
    outs, off = [], 0
    for w in IN_SPLITS:
        outs.append(p[..., off:off + w])
        off += w
    return outs

def _merge(x, oa, za, ob, zb, ga, gb, gate, w_br_a, w_br_b, w_out):
    ya = (oa * jax.nn.silu(za)) @ w_br_a
    yb = (ob * jax.nn.silu(zb)) @ w_br_b
    h = jax.nn.sigmoid(ga) * ya + jax.nn.sigmoid(gb) * yb
    return x + gate * (h @ w_out)

def _softmax_f32(s):
    return jax.nn.softmax(s.astype(jnp.float32), axis=-1)

def _axial_rope(x):
    T = x.shape[1]
    t = jnp.arange(T)
    row = (t // GRID_W).astype(jnp.float32)
    col = (t % GRID_W).astype(jnp.float32)
    inv = ROPE_BASE ** (-jnp.arange(0, ROPE_HALF, 2, dtype=jnp.float32) / ROPE_HALF)
    n = ROPE_HALF // 2

    def rot(xh, pos):
        ang = pos[:, None] * inv[None, :]
        cos = jnp.cos(ang)[:, None, :].astype(x.dtype)
        sin = jnp.sin(ang)[:, None, :].astype(x.dtype)
        x1, x2 = xh[..., :n], xh[..., n:]
        return jnp.concatenate([x1 * cos - x2 * sin, x1 * sin + x2 * cos], axis=-1)

    return jnp.concatenate([rot(x[..., :ROPE_HALF], row), rot(x[..., ROPE_HALF:], col)], axis=-1)

def _dense_attn(q, k, v):
    s = jnp.einsum('bqhd,bkhd->bhqk', q, k).astype(jnp.float32) * ATTN_SCALE
    p = _softmax_f32(s).astype(v.dtype)
    o = jnp.einsum('bhqk,bkhd->bqhd', p, v)
    return o.reshape(q.shape[0], q.shape[1], -1)

def _dense_sink_gqa(q, k, v, sink):
    s = jnp.einsum('bqkgd,bskd->bkgqs', q, k).astype(jnp.float32) * ATTN_SCALE
    sink_col = jnp.broadcast_to(sink.reshape(WA_KV_HEADS, WA_GROUP)[None, :, :, None, None].astype(jnp.float32),
                                s.shape[:-1] + (1,))
    p = _softmax_f32(jnp.concatenate([s, sink_col], axis=-1))[..., :-1].astype(v.dtype)
    o = jnp.einsum('bkgqs,bskd->bqkgd', p, v)
    return o.reshape(q.shape[0], q.shape[1], -1)

def _neighbourhood_attn(q, k, v, ck, cv, rpb):
    B, T, H, Dh = q.shape
    rows = T // GRID_W
    kh = min(NA_KH, rows)
    r = jnp.arange(rows)
    row_start = jnp.clip(r - kh // 2, 0, rows - kh)
    row_idx = row_start[:, None] + jnp.arange(kh)
    j = jnp.arange(NA_NCB)
    kcol_start = jnp.clip(j * NA_QCB - (NA_KCB - NA_QCB) // 2, 0, GRID_W - NA_KCB)
    kcol_idx = kcol_start[:, None] + jnp.arange(NA_KCB)
    qcol = j[:, None] * NA_QCB + jnp.arange(NA_QCB)
    win_start = jnp.clip(qcol - NA_KW // 2, 0, GRID_W - NA_KW)
    kc = kcol_idx[:, None, :]
    col_ok = (kc >= win_start[..., None]) & (kc < win_start[..., None] + NA_KW)
    dr = row_idx - r[:, None]
    dc = jnp.clip(kc - qcol[..., None], -(NA_KW - 1), NA_KW - 1)
    bias = rpb[:, dr[:, None, None, :, None] + NA_KH - 1, dc[None, :, :, None, :] + NA_KW - 1]
    bias = bias.astype(jnp.float32)
    bias = jnp.where(col_ok[None, None, :, :, None, :], bias, -jnp.inf)
    bias = bias.transpose(1, 2, 0, 3, 4, 5).reshape(rows, NA_NCB, H, NA_QCB, kh * NA_KCB)

    qg = q.reshape(B, rows, NA_NCB, NA_QCB, H, Dh)
    kgrid = k.reshape(B, rows, GRID_W, H, Dh)
    vgrid = v.reshape(B, rows, GRID_W, H, Dh)
    ri = row_idx[:, None, :, None]
    ci = kcol_idx[None, :, None, :]
    kb = kgrid[:, ri, ci].reshape(B, rows, NA_NCB, kh * NA_KCB, H, Dh)
    vb = vgrid[:, ri, ci].reshape(B, rows, NA_NCB, kh * NA_KCB, H, Dh)

    s_nb = jnp.einsum('brjqhd,brjkhd->brjhqk', qg, kb).astype(jnp.float32) * ATTN_SCALE + bias[None]
    s_ctx = jnp.einsum('brjqhd,bshd->brjhqs', qg, ck).astype(jnp.float32) * ATTN_SCALE
    p = _softmax_f32(jnp.concatenate([s_nb, s_ctx], axis=-1)).astype(v.dtype)
    nk = kh * NA_KCB
    o = (jnp.einsum('brjhqk,brjkhd->brjqhd', p[..., :nk], vb)
         + jnp.einsum('brjhqs,bshd->brjqhd', p[..., nk:], cv))
    return o.reshape(B, T, H * Dh)

def _window_sink_gqa(q, k, v, ck, cv, sink):
    B, T = q.shape[0], q.shape[1]
    nb = T // WA_BLOCK
    P = ck.shape[1]
    qb = q.reshape(B, nb, WA_BLOCK, WA_KV_HEADS, WA_GROUP, HEAD_DIM)
    pad = ((0, 0), (WA_BLOCK, WA_BLOCK), (0, 0), (0, 0))
    kp = jnp.pad(k, pad).reshape(B, nb + 2, WA_BLOCK, WA_KV_HEADS, HEAD_DIM)
    vp = jnp.pad(v, pad).reshape(B, nb + 2, WA_BLOCK, WA_KV_HEADS, HEAD_DIM)
    kband = jnp.concatenate([kp[:, :-2], kp[:, 1:-1], kp[:, 2:]], axis=2)
    vband = jnp.concatenate([vp[:, :-2], vp[:, 1:-1], vp[:, 2:]], axis=2)
    blk = jnp.arange(nb)
    qpos = blk[:, None] * WA_BLOCK + jnp.arange(WA_BLOCK)
    kpos = blk[:, None] * WA_BLOCK - WA_BLOCK + jnp.arange(3 * WA_BLOCK)
    ok = ((jnp.abs(kpos[:, None, :] - qpos[:, :, None]) <= WINDOW)
          & (kpos >= 0)[:, None, :] & (kpos < T)[:, None, :])
    s_nb = jnp.einsum('bnqkgd,bnskd->bnkgqs', qb, kband).astype(jnp.float32) * ATTN_SCALE
    s_nb = jnp.where(ok[None, :, None, None], s_nb, -jnp.inf)
    s_ctx = jnp.einsum('bnqkgd,bskd->bnkgqs', qb, ck).astype(jnp.float32) * ATTN_SCALE
    sink_col = jnp.broadcast_to(sink.reshape(WA_KV_HEADS, WA_GROUP)[None, None, :, :, None, None].astype(jnp.float32),
                                s_nb.shape[:-1] + (1,))
    p = _softmax_f32(jnp.concatenate([s_nb, s_ctx, sink_col], axis=-1)).astype(v.dtype)
    nk = 3 * WA_BLOCK
    o = (jnp.einsum('bnkgqs,bnskd->bnqkgd', p[..., :nk], vband)
         + jnp.einsum('bnkgqs,bskd->bnqkgd', p[..., nk:nk + P], cv))
    return o.reshape(B, T, WA_WIDTH)

def _context_layer(x, c_ctx, w_ada, b_ada, w_in, sink, w_br_a, w_br_b, w_out):
    B, S, _ = x.shape
    shift, scale, gate = _modulation(c_ctx, w_ada, b_ada)
    qa, ka, va, za, qb, kb, vb, zb, ga, gb = _project(x, shift, scale, w_in)
    qa = qa.reshape(B, S, NA_HEADS, HEAD_DIM)
    ka = ka.reshape(B, S, NA_HEADS, HEAD_DIM)
    va = va.reshape(B, S, NA_HEADS, HEAD_DIM)
    qb = qb.reshape(B, S, WA_KV_HEADS, WA_GROUP, HEAD_DIM)
    kb = kb.reshape(B, S, WA_KV_HEADS, HEAD_DIM)
    vb = vb.reshape(B, S, WA_KV_HEADS, HEAD_DIM)
    oa = _dense_attn(qa, ka, va)
    ob = _dense_sink_gqa(qb, kb, vb, sink)
    y = _merge(x, oa, za, ob, zb, ga, gb, gate, w_br_a, w_br_b, w_out)
    return y, ka, va, kb, vb

def _latent_layer(x, c, ck_a, cv_a, ck_b, cv_b, w_ada, b_ada, w_in, rpb, sink, w_br_a, w_br_b, w_out):
    B, T, _ = x.shape
    shift, scale, gate = _modulation(c, w_ada, b_ada)
    qa, ka, va, za, qb, kb, vb, zb, ga, gb = _project(x, shift[:, None], scale[:, None], w_in)
    qa = qa.reshape(B, T, NA_HEADS, HEAD_DIM)
    ka = ka.reshape(B, T, NA_HEADS, HEAD_DIM)
    va = va.reshape(B, T, NA_HEADS, HEAD_DIM)
    qb = _axial_rope(qb.reshape(B, T, WA_Q_HEADS, HEAD_DIM)).reshape(B, T, WA_KV_HEADS, WA_GROUP, HEAD_DIM)
    kb = _axial_rope(kb.reshape(B, T, WA_KV_HEADS, HEAD_DIM))
    vb = vb.reshape(B, T, WA_KV_HEADS, HEAD_DIM)
    oa = _neighbourhood_attn(qa, ka, va, ck_a, cv_a, rpb)
    ob = _window_sink_gqa(qb, kb, vb, ck_b, cv_b, sink)
    return _merge(x, oa, za, ob, zb, ga, gb, gate[:, None], w_br_a, w_br_b, w_out)

def setup_inputs(seed: int = 0) -> dict:
    key = jax.random.key(seed)
    ks = jax.random.split(key, 20)
    f32 = jnp.float32
    nrm = lambda k, shp, s: jax.random.normal(k, shp, f32) * s
    return {
        "x_prompt": nrm(ks[0], (BATCH, SEQ, D_MODEL), 1.0),
        "x_sample": nrm(ks[1], (DEC_BATCH, DEC_SEQ, D_MODEL), 1.0),
        "cache_a_k": nrm(ks[2], (DEC_BATCH, DEPTH, PAST_LEN, NA_HEADS, HEAD_DIM), 1.0),
        "cache_a_v": nrm(ks[3], (DEC_BATCH, DEPTH, PAST_LEN, NA_HEADS, HEAD_DIM), 1.0),
        "cache_b_k": nrm(ks[4], (DEC_BATCH, DEPTH, PAST_LEN, WA_KV_HEADS, HEAD_DIM), 1.0),
        "cache_b_v": nrm(ks[5], (DEC_BATCH, DEPTH, PAST_LEN, WA_KV_HEADS, HEAD_DIM), 1.0),
        "c": nrm(ks[6], (DEC_BATCH, D_MODEL), 1.0),
        "c_ctx": nrm(ks[7], (D_MODEL,), 1.0),
        "w_ada": nrm(ks[8], (DEPTH, D_MODEL, 3 * D_MODEL), D_MODEL ** -0.5),
        "b_ada": nrm(ks[9], (DEPTH, 3 * D_MODEL), 0.02),
        "w_in": nrm(ks[10], (DEPTH, D_MODEL, D_IN), D_MODEL ** -0.5),
        "rpb_a": nrm(ks[11], (DEPTH, NA_HEADS, 2 * NA_KH - 1, 2 * NA_KW - 1), 0.1),
        "sink_b": nrm(ks[12], (DEPTH, WA_Q_HEADS), 0.5),
        "w_br_a": nrm(ks[13], (DEPTH, NA_WIDTH, D_MODEL), NA_WIDTH ** -0.5),
        "w_br_b": nrm(ks[14], (DEPTH, WA_WIDTH, D_MODEL), WA_WIDTH ** -0.5),
        "w_out": nrm(ks[15], (DEPTH, D_MODEL, D_MODEL), D_MODEL ** -0.5),
        "final_norm_g": 1.0 + nrm(ks[16], (D_MODEL,), 0.02),
    }

def reference(x_prompt, x_sample, cache_a_k, cache_a_v, cache_b_k, cache_b_v, c, c_ctx,
              w_ada, b_ada, w_in, rpb_a, sink_b, w_br_a, w_br_b, w_out, final_norm_g):
    xp, xs = x_prompt, x_sample
    new_ak, new_av, new_bk, new_bv = [], [], [], []
    for l in range(DEPTH):
        xp, ka, va, kb, vb = _context_layer(xp, c_ctx, w_ada[l], b_ada[l], w_in[l], sink_b[l],
                                            w_br_a[l], w_br_b[l], w_out[l])
        new_ak.append(ka)
        new_av.append(va)
        new_bk.append(kb)
        new_bv.append(vb)
        xs = _latent_layer(xs, c, cache_a_k[:, l], cache_a_v[:, l], cache_b_k[:, l], cache_b_v[:, l],
                           w_ada[l], b_ada[l], w_in[l], rpb_a[l], sink_b[l], w_br_a[l], w_br_b[l], w_out[l])
    y_prompt = _rmsnorm(xp) * final_norm_g
    y_sample = _rmsnorm(xs) * final_norm_g
    new_a_k = jnp.stack(new_ak, axis=1)
    new_a_v = jnp.stack(new_av, axis=1)
    new_b_k = jnp.stack(new_bk, axis=1)
    new_b_v = jnp.stack(new_bv, axis=1)
    return (y_prompt, y_sample, new_a_k, new_a_v, new_b_k, new_b_v)


_drawn_inputs = setup_inputs


def setup_inputs(seed=0):
    import zlib

    import numpy as np

    out = dict(_drawn_inputs(seed))
    spreads = {}
    factors = {'cache_a_k': 3.364,
     'cache_a_v': 3.015,
     'cache_b_k': 3.808,
     'cache_b_v': 3.406,
     'rpb_a': 64.0,
     'sink_b': 28.856,
     'final_norm_g': 8.197}
    for name, (base, spread) in spreads.items():
        noise = np.random.default_rng([zlib.crc32(name.encode()), seed]).standard_normal(out[name].shape)
        drawn = base * np.exp(spread * noise) if base else spread * noise
        out[name] = __import__('jax').numpy.asarray(drawn.astype(out[name].dtype))
    for name, factor in factors.items():
        out[name] = (out[name] * factor).astype(out[name].dtype)
    return out
```

```python
from contextlib import ExitStack

import numpy as np

import concourse.bass as bass
from concourse import mybir

F32 = mybir.dt.float32
F32R = mybir.dt.float32r
ALU = mybir.AluOpType
ACT = mybir.ActivationFunctionType
AX = mybir.AxisListType

P = 128
D = 1024
KD = D // P
LAT, PROMPT = 1024, 256
TOK = LAT + PROMPT
PAST = 512
HD = 64
GRID_W = 64
ROWS = LAT // GRID_W
NA_HEADS, NA_KH, NA_KW = 8, 8, 16
QR, QC = 8, 16
KR, KC = 12, 32
NCB = GRID_W // QC
KC0 = [min(max(j * QC - (KC - QC) // 2, 0), GRID_W - KC) for j in range(NCB)]
BIAS_TYPE = [0, 1, 1, 2]
TYPE_BLOCK = [0, 1, 3]
TYPE_OFF = [KC0[j] - j * QC for j in TYPE_BLOCK]
BR, BC = 16, 48
WINDOW = 128
NB = KR * KC
SW = PAST + NB
PAIRS = 4
EPS = 1e-6
QSCALE = -(HD ** -0.5)
BIG = 1e30
VH = 10
UNIT = 320
UNITS = TOK // UNIT
GROUPS = [(0, 512), (512, 512), (1024, 256)]
GATE_BLOCKS = 24
GPP = 3
STEPS = 10
CHUNKS = [1, 1] + [4] * 8
CHUNK0 = [sum(CHUNKS[:s]) for s in range(STEPS)]
NCHUNK = sum(CHUNKS)


def split_mm(eng, out, lhs, rhs, n_k, begun=None):
    for k in range(n_k):
        for i, (a, b) in enumerate(((0, 0), (0, 1), (1, 0))):
            mm = eng.matmul(out, lhs(a, k), rhs(b, k), start=(k == 0 and i == 0), stop=(k == n_k - 1 and i == 2))
            if begun is not None and k == 0 and i == 0:
                mm.then_inc(begun, 1)
    return mm


def split(eng, hi, lo, src, one, hi_sem, hi_value, lo_sem):
    eng.tensor_tensor(hi, src, one[:, :].to_broadcast(list(src.shape)), ALU.mult).then_inc(hi_sem, 1)
    eng.wait_ge(hi_sem, hi_value)
    eng.tensor_tensor(lo, src, hi.bitcast(F32), ALU.subtract).then_inc(lo_sem, 1)


def startup(nc, io, hm, ident, wv, wkb):
    with ExitStack() as ctx:
        def sb(name, shape, dt=F32):
            return ctx.enter_context(nc.sbuf_tensor(name, shape, dt))

        def ps(name, shape):
            return ctx.enter_context(nc.psum_tensor(name, shape, F32))

        def sem(name):
            return nc.alloc_semaphore(name=name)

        XG = [(0, 4), (4, 4), (8, 2)]
        x = sb("x", [P, 2, 4, D])
        wada = sb("wada", [P, 4, D])
        vraw = sb("vraw", [P, 2, VH * HD])
        kraw = sb("kraw", [P, D])
        h32 = sb("h32", [P, 2, 512])
        modrow = sb("modrow", [2, 2 * D])
        ccol = sb("ccol", [P, KD, 2])
        scol = sb("scol", [P, KD, 2])
        bcol = sb("bcol", [P, 2 * KD])
        modc = sb("modc", [P, 2 * KD, 2])
        modf = sb("modf", [P, 2 * KD, 2])
        ss = sb("ss", [P, 12])
        rms = sb("rms", [P, 12])
        rstd = sb("rstd", [P, 12])
        epsc = sb("epsc", [P, 1])
        one = sb("one", [P, 1])
        mod_ps = ps("mod_ps", [P, 4, 512])
        t_ps = ps("t_ps", [P, 2, 512])
        junk = ps("junk", [P, D])

        small_in, ident_in, kraw_in, eps_set = sem("small_in"), sem("ident_in"), sem("kraw_in"), sem("eps_set")
        x_in = [sem(f"x_in{g}") for g in range(3)]
        wada_in = [sem(f"wada_in{i}") for i in range(4)]
        vraw_in = [sem(f"vraw_in{i}") for i in range(2)]
        silu_done, wada_used, mod_row, mod_t, mod_c, mod_ready = (
            sem(n) for n in ("silu_done", "wada_used", "mod_row", "mod_t", "mod_c", "mod_ready"))
        sq_done, rms_done, rstd_done, xn_done, xt_done = (
            sem(n) for n in ("sq_done", "rms_done", "rstd_done", "xn_done", "xt_done"))
        h_done, hi_done, lo_done, v_hi, v_lo, k_hi, k_lo = (
            sem(n) for n in ("h_done", "hi_done", "lo_done", "v_hi", "v_lo", "k_hi", "k_lo"))

        block = ctx.enter_context(nc.Block())
        chunks = [(g, k) for g in range(3) for k in range(KD)]

        @block.sync
        def _(sp):
            def load_x(g):
                t0, n = XG[g]
                if g == 2:
                    sp.wait_ge(xt_done, KD)
                sp.dma_start(x[:, g % 2, 0:n, :], io["x"][t0 * P:(t0 + n) * P, :].rearrange("(t p) d -> p t d", p=P)
                             ).then_inc(x_in[g], 16)

            def load_wada(i):
                if i >= 4:
                    sp.wait_ge(wada_used, i - 3)
                k, half = i // 2, i % 2
                sp.dma_start(wada[:, i % 4, :], io["w_ada"][k * P:(k + 1) * P, half * D:(half + 1) * D]
                             ).then_inc(wada_in[i % 4], 16)

            sp.dma_start(ccol[:, :, :], io["c_col"]).then_inc(small_in, 16)
            sp.dma_start(bcol[:, :], io["b_col"]).then_inc(small_in, 16)
            sp.dma_start(ident[:, :], io["ident"]).then_inc(ident_in, 16)
            load_x(0)
            for i in range(2 * KD):
                load_wada(i)
                if i == 7:
                    load_x(1)
            for k in range(KD):
                if k >= 2:
                    sp.wait_ge(v_lo, k - 1)
                sp.dma_start(vraw[:, k % 2, :], io["w_v"][:, k, :]).then_inc(vraw_in[k % 2], 16)
            sp.dma_start(kraw[:, :], io["w_kb"]).then_inc(kraw_in, 16)
            load_x(2)

        @block.gpsimd
        def _(pool):
            pool.memset(epsc[:, :], EPS).then_inc(eps_set, 1)
            pool.memset(one[:, :], 1.0).then_inc(eps_set, 1)
            pool.wait_ge(eps_set, 2)
            for k in range(KD):
                pool.wait_ge(vraw_in[k % 2], 16 * (k // 2 + 1))
                split(pool, wv[:, 0, k, :], wv[:, 1, k, :], vraw[:, k % 2, :], one, v_hi, k + 1, v_lo)
            pool.wait_ge(kraw_in, 16)
            split(pool, wkb[:, 0, :], wkb[:, 1, :], kraw[:, :], one, k_hi, 1, k_lo)

        @block.scalar
        def _(act):
            act.wait_ge(small_in, 32)
            act.activation(scol[:, :, :], ccol[:, :, :], ACT.Silu).then_inc(silu_done, 1)
            act.wait_ge(eps_set, 1)

            def norms(g):
                t0, n = XG[g]
                act.wait_ge(x_in[g], 16)
                for t in range(n):
                    if t0 + t > 0:
                        act.wait_ge(sq_done, t0 + t)
                    act.activation(junk[:, :], x[:, g % 2, t, :], ACT.Square, accum_out=ss[:, t0 + t:t0 + t + 1]
                                   ).then_inc(sq_done, 1)
                act.wait_ge(sq_done, t0 + n)
                act.activation(rms[:, t0:t0 + n], ss[:, t0:t0 + n], ACT.Sqrt, bias=epsc[:, 0:1], scale=1.0 / D
                               ).then_inc(rms_done, 1)

            norms(0)
            norms(1)
            act.wait_ge(mod_ready, 1)
            for i, (g, k) in enumerate(chunks):
                if i == KD + 2:
                    norms(2)
                n, stream = XG[g][1] * P, int(g == 2)
                act.wait_ge(xt_done, i + 1)
                if i >= 2:
                    act.wait_ge(lo_done, i - 1)
                act.activation(h32[:, i % 2, 0:n], t_ps[:, i % 2, 0:n], ACT.Identity,
                               bias=modf[:, k, stream:stream + 1], scale=modf[:, KD + k, stream:stream + 1]
                               ).then_inc(h_done, 1)

        @block.tensor
        def _(pe):
            pe.wait_ge(silu_done, 1)
            for i in range(2 * KD):
                k, half = i // 2, i % 2
                pe.wait_ge(wada_in[i % 4], 16 * (i // 4 + 1))
                for c in range(2):
                    mm = pe.matmul(mod_ps[0:2, 2 * half + c, :], scol[:, k, :], wada[:, i % 4, c * 512:(c + 1) * 512],
                                   start=(k == 0), stop=(k == KD - 1))
                mm.then_inc(wada_used, 1)
            pe.wait_ge(ident_in, 16)
            pe.wait_ge(mod_row, 1)
            for b in range(2 * KD):
                mm = pe.transpose(mod_ps[:, 0, 2 * b:2 * b + 2], modrow[0:2, b * P:(b + 1) * P], ident[0:2, 0:2])
            mm.then_inc(mod_t, 1)
            for i, (g, k) in enumerate(chunks):
                pe.wait_ge(xn_done, XG[g][0] + XG[g][1])
                if i >= 2:
                    pe.wait_ge(h_done, i - 1)
                for t in range(XG[g][1]):
                    mm = pe.transpose(t_ps[:, i % 2, t * P:(t + 1) * P], x[:, g % 2, t, k * P:(k + 1) * P], ident[:, :])
                mm.then_inc(xt_done, 1)

        @block.vector
        def _(dve):
            def normalise(g):
                t0, n = XG[g]
                dve.wait_ge(rms_done, g + 1)
                dve.reciprocal(rstd[:, t0:t0 + n], rms[:, t0:t0 + n]).then_inc(rstd_done, 1)
                dve.wait_ge(rstd_done, g + 1)
                for t in range(n):
                    dve.tensor_scalar(x[:, g % 2, t, :], x[:, g % 2, t, :], rstd[:, t0 + t:t0 + t + 1], None, ALU.mult
                                      ).then_inc(xn_done, 1)

            normalise(0)
            normalise(1)
            dve.wait_ge(wada_used, 2 * KD)
            dve.tensor_copy(modrow[:, :], mod_ps[0:2, :, :].rearrange("p a b -> p (a b)")).then_inc(mod_row, 1)
            dve.wait_ge(mod_t, 1)
            dve.wait_ge(small_in, 32)
            for s in range(2):
                dve.tensor_tensor(modc[:, :, s], mod_ps[:, 0, 0:4 * KD].rearrange("p (b s) -> p b s", s=2)[:, :, s],
                                  bcol[:, :], ALU.add).then_inc(mod_c, 1)
            dve.wait_ge(mod_c, 2)
            dve.tensor_copy(modf[:, 0:KD, :], modc[:, 0:KD, :]).then_inc(mod_c, 1)
            dve.tensor_scalar(modf[:, KD:, :], modc[:, KD:, :], 1.0, None, ALU.add).then_inc(mod_ready, 1)
            for i, (g, k) in enumerate(chunks):
                if i == KD + 2:
                    normalise(2)
                t0, n = XG[g][0] * P, XG[g][1] * P
                dve.wait_ge(h_done, i + 1)
                dve.tensor_copy(hm[:, 0, k, t0:t0 + n], h32[:, i % 2, 0:n]).then_inc(hi_done, 1)
                dve.wait_ge(hi_done, i + 1)
                dve.tensor_tensor(hm[:, 1, k, t0:t0 + n], h32[:, i % 2, 0:n], hm[:, 0, k, t0:t0 + n].bitcast(F32),
                                  ALU.subtract).then_inc(lo_done, 1)


SWAP16 = [(i + 16) % 32 for i in range(32)]


def values(nc, io, hm, wv, wkb):
    with ExitStack() as ctx:
        def sb(name, shape, dt=F32):
            return ctx.enter_context(nc.sbuf_tensor(name, shape, dt))

        def ps(name, shape):
            return ctx.enter_context(nc.psum_tensor(name, shape, F32))

        def sem(name):
            return nc.alloc_semaphore(name=name)

        vst = sb("vst", [P, 2, VH, 2 * HD], F32R)
        vout = sb("vout", [P, 2, VH * HD])
        kst = sb("kst", [P, 2, TOK], F32R)
        kout = sb("kout", [P, PROMPT])
        cos, sin = sb("cos_v", [P, LAT]), sb("sin_v", [P, LAT])
        raw, swp, rot = sb("raw_v", [P, 512]), sb("swp_v", [P, 512]), sb("rot_v", [P, 512])
        wgate = sb("wgate", [P, 2, D])
        gcc, gsc = sb("gcc", [P, KD, 2]), sb("gsc", [P, KD, 2])
        gb, grow = sb("gb", [2, D]), sb("grow", [2, D])
        v_ps = ps("v_ps", [P, 4, 512])
        g_ps = ps("g_ps", [P, 2, 512])

        small_in, table_in, silu_done = sem("v_small_in"), sem("v_table_in"), sem("v_silu")
        wg_in = [sem(f"wg_in{i}") for i in range(2)]
        wg_used, g_row, g_out = sem("wg_used"), sem("g_row"), sem("g_out")
        mm_done, v_hi, v_lo, v_copy = sem("v_mm"), sem("v_hi2"), sem("v_lo2"), sem("v_copy")
        v_out = [sem(f"v_out{i}") for i in range(2)]
        vo_out = sem("vo_out")
        k_raw, k_swp, k_cos, k_sin, k_rot, k_hi, k_lo, k_copy, k_out = (
            sem(n) for n in ("k_raw", "k_swp", "k_cos", "k_sin", "k_rot", "kv_hi", "kv_lo", "k_copy", "k_out"))
        block = ctx.enter_context(nc.Block())
        TT = TOK // P
        NU = 2 * TT
        HW = VH * HD // 2

        @block.sync
        def _(sp):
            sp.dma_start(gcc[:, :, :], io["c_col"]).then_inc(small_in, 16)
            sp.dma_start(gb[:, :], io["b_gate"].to_broadcast([2, D])).then_inc(small_in, 16)
            sp.dma_start(cos[:, :], io["cos"]).then_inc(table_in, 16)
            sp.dma_start(sin[:, :], io["sin"]).then_inc(table_in, 16)

            def load_gate_weights(k):
                sp.dma_start(wgate[:, k % 2, :], io["w_ada"][k * P:(k + 1) * P, 2 * D:3 * D]).then_inc(wg_in[k % 2], 16)

            load_gate_weights(0)
            load_gate_weights(1)
            for t in range(TT):
                sp.wait_ge(v_lo, 2 * t + 2)
                sp.dma_start(io["v_d"][t * P:(t + 1) * P, :], vst[:, t % 2, :, :].rearrange("p h c -> p (h c)").bitcast(F32)
                             ).then_inc(v_out[t % 2], 16)
                if 2 <= t < KD:
                    sp.wait_ge(wg_used, t - 1)
                    load_gate_weights(t)
                if t * P >= LAT:
                    s = t - LAT // P
                    sp.wait_ge(v_copy, 2 * s + 2)
                    sp.dma_start(io["new_av"][s * P:(s + 1) * P, :], vout[:, s, 0:8 * HD]).then_inc(vo_out, 16)
                    sp.dma_start(io["new_bv"][s * P:(s + 1) * P, :], vout[:, s, 8 * HD:]).then_inc(vo_out, 16)
            sp.wait_ge(g_row, 1)
            sp.dma_start(io["gate_d"], grow[:, :]).then_inc(g_out, 16)
            sp.wait_ge(k_copy, 1)
            sp.dma_start(io["new_bk"], kout[:, :]).then_inc(k_out, 16)
            sp.wait_ge(k_lo, 3)
            for part in range(2):
                for kv in range(2):
                    sp.dma_start(io["kb_d"][kv, part], kst[kv * HD:(kv + 1) * HD, part, :].bitcast(F32)).then_inc(k_out, 16)
            sp.wait_ge(v_out[0], 16 * (TT // 2))
            sp.wait_ge(v_out[1], 16 * (TT // 2))
            sp.wait_ge(vo_out, 64)
            sp.wait_ge(g_out, 16)
            sp.wait_ge(k_out, 80)

        @block.tensor
        def _(pe):
            for u in range(NU):
                t, n = u // 2, u % 2
                if u >= 4:
                    pe.wait_ge(v_lo, u - 3)
                split_mm(pe, v_ps[:, u % 4, 0:HW], lambda a, k: hm[:, a, k, t * P:(t + 1) * P],
                         lambda b, k: wv[:, b, k, n * HW:(n + 1) * HW], KD).then_inc(mm_done, 1)
                if n == 0 and 2 <= t < KD + 2:
                    k = t - 2
                    if k == 0:
                        pe.wait_ge(silu_done, 1)
                    pe.wait_ge(wg_in[k % 2], 16 * (k // 2 + 1))
                    for c in range(2):
                        mm = pe.matmul(g_ps[0:2, c, :], gsc[:, k, :], wgate[:, k % 2, c * 512:(c + 1) * 512],
                                       start=(k == 0), stop=(k == KD - 1))
                    mm.then_inc(wg_used, 1)
            for g, (t0, n) in enumerate(GROUPS):
                u = NU + g
                pe.wait_ge(v_lo, u - 3)
                split_mm(pe, v_ps[:, u % 4, 0:n], lambda a, k: wkb[:, a, k * P:(k + 1) * P],
                         lambda b, k: hm[:, b, k, t0:t0 + n], KD).then_inc(mm_done, 1)

        @block.scalar
        def _(act):
            act.wait_ge(small_in, 32)
            act.activation(gsc[:, :, :], gcc[:, :, :], ACT.Silu).then_inc(silu_done, 1)
            for u in range(NU):
                t, n = u // 2, u % 2
                act.wait_ge(mm_done, u + 1)
                if t >= 2 and n == 0:
                    act.wait_ge(v_out[t % 2], 16 * (t // 2))
                if t * P >= LAT:
                    act.activation(vout[:, t - LAT // P, n * HW:(n + 1) * HW], v_ps[:, u % 4, 0:HW], ACT.Copy
                                   ).then_inc(v_copy, 1)
                act.activation(vst[:, t % 2, 5 * n:5 * n + 5, 0:HD],
                               v_ps[:, u % 4, 0:HW].rearrange("p (h c) -> p h c", c=HD), ACT.Copy).then_inc(v_hi, 1)
            for g, (t0, n) in enumerate(GROUPS):
                act.wait_ge(mm_done, NU + g + 1)
                if g == 1:
                    act.wait_ge(k_lo, 1)
                if g == 2:
                    act.wait_ge(k_lo, 2)
                act.activation((rot if g == 2 else raw)[:, 0:n], v_ps[:, (NU + g) % 4, 0:n], ACT.Copy).then_inc(k_raw, 1)

        @block.gpsimd
        def _(pool):
            pool.wait_ge(table_in, 32)
            for g, (t0, n) in enumerate(GROUPS[:2]):
                pool.wait_ge(k_swp, g + 1)
                pool.tensor_tensor(swp[:, :], swp[:, :], sin[:, t0:t0 + n], ALU.mult).then_inc(k_sin, 1)

        @block.vector
        def _(dve):
            for u in range(NU):
                t, n = u // 2, u % 2
                hi = vst[:, t % 2, 5 * n:5 * n + 5, 0:HD]
                dve.wait_ge(v_hi, u + 1)
                dve.tensor_tensor(vst[:, t % 2, 5 * n:5 * n + 5, HD:],
                                  v_ps[:, u % 4, 0:HW].rearrange("p (h c) -> p h c", c=HD), hi.bitcast(F32),
                                  ALU.subtract).then_inc(v_lo, 1)
            dve.wait_ge(table_in, 32)
            for g, (t0, n) in enumerate(GROUPS):
                dve.wait_ge(k_raw, g + 1)
                if g < 2:
                    dve.tensor_tensor(rot[:, :], raw[:, :], cos[:, t0:t0 + n], ALU.mult).then_inc(k_cos, 1)
                    dve.stream_shuffle(swp[:, :], raw[:, :], SWAP16).then_inc(k_swp, 1)
                    dve.wait_ge(k_sin, g + 1)
                    dve.wait_ge(k_cos, g + 1)
                    dve.tensor_tensor(rot[:, :], rot[:, :], swp[:, :], ALU.add).then_inc(k_rot, 1)
                    dve.wait_ge(k_rot, g + 1)
                else:
                    dve.tensor_copy(kout[:, :], rot[:, 0:n]).then_inc(k_copy, 1)
                dve.tensor_copy(kst[:, 0, t0:t0 + n], rot[:, 0:n]).then_inc(k_hi, 1)
                dve.wait_ge(k_hi, g + 1)
                dve.tensor_tensor(kst[:, 1, t0:t0 + n], rot[:, 0:n], kst[:, 0, t0:t0 + n].bitcast(F32), ALU.subtract
                                  ).then_inc(k_lo, 1)
            dve.wait_ge(small_in, 32)
            dve.wait_ge(wg_used, KD)
            dve.tensor_tensor(grow[:, :], g_ps[0:2, :, :].rearrange("p a b -> p (a b)"), gb[:, :], ALU.add
                              ).then_inc(g_row, 1)


def pairs(nc, io, hm, ident, branch):
    A = branch == "a"
    with ExitStack() as ctx:
        def sb(name, shape, dt=F32):
            return ctx.enter_context(nc.sbuf_tensor(f"{name}_{branch}", shape, dt))

        def ps(name, shape):
            return ctx.enter_context(nc.psum_tensor(f"{name}_{branch}", shape, F32))

        def sem(name):
            return nc.alloc_semaphore(name=f"{name}_{branch}")

        w = sb("w", [P, 3, 2, D], F32R)
        wraw = sb("wraw", [P, D])
        craw = sb("craw", [P, D])
        q1 = sb("q1", [P, 2, TOK], F32R)
        q2 = sb("q2", [P, TOK], F32R)
        kk = sb("kk", [P, 2, TOK], F32R)
        kc = sb("kc", [P, 2, PAST], F32R)
        CH = 2 if A else 1
        vc = sb("vc", [P, PAST // P, CH, 2 * HD], F32R)
        vw = sb("vw", [P, 16 if A else 8, CH * 2 * HD], F32R)
        vp = sb("vp", [P, 2, CH * 2 * HD], F32R)
        pr = sb("pr", [P, 2, NB + PAST + NB])
        pt = sb("pt", [P, 2, 14 * P], F32R)
        ost = sb("ost", [P, TOK])
        gst = sb("gst", [P, 2, UNIT])
        otmp = sb("otmp", [HD, 2 * P])
        one, qscale = sb("one", [P, 1]), sb("qscale", [P, 1])
        mn = sb("mn", [P, 2])
        nm = sb("nm", [P, 2])
        mx = sb("mx", [P, 2])
        den = sb("den", [P, 2])
        rden = sb("rden", [P, 2])
        if A:
            rb = sb("rb", [P, BR, BC])
            comb = sb("comb", [P, 2, 2, NB])
            rowm = sb("rowm", [P, 2, KR])
            colm = sb("colm", [P, 3, KC])
            kout = sb("kout", [P, PROMPT])
        else:
            band = sb("band", [P, 3, NB])
            cos, sin = sb("cos", [P, LAT]), sb("sin", [P, LAT])
            raw, swp, rot = sb("raw", [P, 512]), sb("swp", [P, 512]), sb("rot", [P, 512])
            sink = sb("sink", [P, 8])
            nsink = sb("nsink", [P, 8])
            nsk = sb("nsk", [P, 2])
            esk = sb("esk", [P, 2])
            den2 = sb("den2", [P, 2])
        s_ps = ps("s_ps", [P, 4, 512])
        t_ps = ps("t_ps", [P, 2, 512])
        o_ps = ps("o_ps", [P, 512])
        d_ps = ps("d_ps", [P, 512])

        PROJ = 2 if A else 1
        TILES = PROJ + GPP
        SLOT = [0, 1, 2, 0, 1] if A else [0, 1, 2, 1]
        NG = PROJ * 3

        def slot_free(i):
            last = max([k for k in range(i) if SLOT[k] == SLOT[i]] or
                       [k - TILES for k in range(TILES) if SLOT[k] == SLOT[i]])
            return max(last + 2, 0)

        w_in, q_in = sem("w_in"), sem("q_in")
        craw_in, w_hi, w_lo = sem("craw_in"), sem("w_hi"), sem("w_lo")
        w_begun, w_scaled = sem("w_begun"), sem("w_scaled")
        c_split = sem("c_split")
        const_in, vw_in, kk_in = sem("const_in"), sem("vw_in"), sem("kk_in")
        rb_in, comb_t, comb_done = sem("rb_in"), sem("comb_t"), sem("comb_done")
        ckh, cvh = sem("ckh"), sem("cvh")
        proj_done, xa, xd, x_used = sem("proj_done"), sem("xa"), sem("xd"), sem("x_used")
        ko_done, ko_out = sem("ko_done"), sem("ko_out")
        s_done, m1_done, m2_done, m3_done, m_done, exp_done = (
            sem(n) for n in ("s_done", "m1_done", "m2_done", "m3_done", "m_done", "exp_done"))
        esk_done, den_done, r_done, p_done = sem("esk_done"), sem("den_done"), sem("r_done"), sem("p_done")
        t_done, hi_done, lo_done, pva_done, pvb_done, ot_done, o_done = (
            sem(n) for n in ("t_done", "hi_done", "lo_done", "pva_done", "pvb_done", "ot_done", "o_done"))
        d_done, g_done = sem("d_done"), sem("g_done")
        g_out = [sem("g_out0"), sem("g_out1")]
        o_out = sem("o_out")
        r_raw, r_swp, r_cos, r_sin, r_rot = (sem(n) for n in ("r_raw", "r_swp", "r_cos", "r_sin", "r_rot"))
        nsk_done, ones_set = sem("nsk_done"), sem("ones_set")

        block = ctx.enter_context(nc.Block())
        base = 0 if A else PAIRS

        def grid(ap, r0, nr, c0, ncol):
            return ap[..., 0:LAT].rearrange("p (r c) -> p r c", c=GRID_W)[:, r0:r0 + nr, c0:c0 + ncol]

        def rows(ap):
            return ap.rearrange("p (r j c) -> p r j c", r=QR, c=QC) if ap.shape[-1] == 512 else ap

        def tiled(ap):
            return ap.rearrange("p (j r c) -> p r j c", r=QR, c=QC) if ap.shape[-1] == 512 else ap

        def near_bank(s, t):
            return s_ps[:, 2 * t, PAST - NB:PAST] if s % 2 else s_ps[:, 2 * t + 1, 0:NB]

        def scores_run(s, t):
            both = s_ps[:, 2 * t:2 * t + 2, :].rearrange("p a b -> p (a b)")
            return both[:, 0:PROMPT] if s < 2 else both[:, PAST - NB:] if s % 2 else both[:, 0:SW]

        def probs_run(s, t):
            return pr[:, t, NB:NB + PROMPT] if s < 2 else pr[:, t, 0:SW] if s % 2 else pr[:, t, NB:]

        def probs_block(s, t, kb):
            c0 = NB + kb * P if kb < 4 or s % 2 == 0 else (kb - 4) * P
            return pr[:, t, c0:c0 + P]

        def chunk_blocks(s):
            if s < 2:
                return [[(0, 0), (0, 1), (1, 0), (1, 1)]]
            if A:
                near = [(4, 0), (5, 0), (4, 1), (6, 0), (5, 1), (6, 1)]
            else:
                near = [(kb, t) for kb in (4, 5, 6) for t in (0, 1)]
            ctx_ = [(kb, t) for kb in range(4) for t in (0, 1)]
            return [ctx_[0:4], ctx_[4:8], near[0:4], near[4:6]]

        @block.sync
        def _(sp):
            if A:
                sp.dma_start(rowm[:, :, :], io["rowmask"]).then_inc(const_in, 16)
                sp.dma_start(colm[:, :, :], io["colmask"]).then_inc(const_in, 16)
            else:
                sp.dma_start(band[:, :, :], io["band"]).then_inc(const_in, 16)
                sp.dma_start(cos[:, :], io["cos"]).then_inc(const_in, 16)
                sp.dma_start(sin[:, :], io["sin"]).then_inc(const_in, 16)
                sp.dma_start(sink[:, :], io["sink"].to_broadcast([P, 8])).then_inc(const_in, 16)
            with sp.Fori(0, PAIRS) as p:
                def load_tile(i):
                    if i < PROJ:
                        src = io["w_k" + branch][p]
                    else:
                        src = io["w_gate"][(p + base) * GPP + (i - PROJ)]
                    sp.wait_ge(w_lo, p * TILES + i)
                    sp.dma_start(wraw[:, :], src).then_inc(w_in, 16)

                sp.wait_ge(c_split, p * 3)
                sp.dma_start(craw[:, :], io["w_q" + branch][p]).then_inc(q_in, 16)
                sp.wait_ge(w_lo, p * TILES + 1)
                sp.dma_start(craw[:, 0:PAST], io["ck" + branch][p]).then_inc(craw_in, 16)
                sp.dma_start(craw[:, PAST:PAST + 4 * CH * HD], io["cv" + branch][p]).then_inc(craw_in, 16)
                if A:
                    load_tile(1)
                sp.wait_ge(pvb_done, p * (STEPS - 2))
                if A:
                    for rg in range(4):
                        for j in range(NCB):
                            v = io["v_d"][0:LAT, :].rearrange("(r c) n -> r c n", c=GRID_W)
                            sp.dma_start(vw[:, rg * NCB + j, :].bitcast(F32),
                                         v[4 * rg:4 * rg + 4, KC0[j]:KC0[j] + KC, bass.ds(p * 256, 256)]
                                         ).then_inc(vw_in, 16)
                    sp.dma_start(vp[:, :, :].bitcast(F32),
                                 io["v_d"][LAT:TOK, bass.ds(p * 256, 256)].rearrange("(t p) n -> p t n", p=P)
                                 ).then_inc(vw_in, 16)
                else:
                    kv = p // 2
                    v = io["v_d"][:, bass.ds(kv * 128 + 1024, 128)]
                    sp.dma_start(vw[:, :, :].bitcast(F32), v[0:LAT, :].rearrange("(t p) n -> p t n", p=P)).then_inc(vw_in, 16)
                    sp.dma_start(vp[:, :, :].bitcast(F32), v[LAT:TOK, :].rearrange("(t p) n -> p t n", p=P)).then_inc(vw_in, 16)
                    sp.wait_ge(exp_done, p * 2 * STEPS)
                    for h in range(2):
                        for part in range(2):
                            r0 = HD * ((h + part) % 2)
                            sp.dma_start(kk[r0:r0 + HD, h, :].bitcast(F32), io["kb_d"][kv, part]).then_inc(kk_in, 16)
                if A:
                    sp.wait_ge(comb_done, p * 12)
                    sp.dma_start(rb[:, :, :], io["bias"][p * 2]).then_inc(rb_in, 16)
                for i in range(PROJ, TILES):
                    load_tile(i)
                if A:
                    sp.wait_ge(comb_done, p * 12 + 6)
                    sp.dma_start(rb[:, :, :], io["bias"][p * 2 + 1]).then_inc(rb_in, 16)

        @block.gpsimd
        def _(pool):
            pool.memset(one[:, :], 1.0).then_inc(ones_set, 1)
            pool.memset(qscale[:, :], QSCALE).then_inc(ones_set, 1)
            pool.wait_ge(ones_set, 2)
            pool.wait_ge(const_in, 32 if A else 64)
            with pool.Fori(0, PAIRS) as p:
                def split_tile(i):
                    slot = SLOT[i]
                    if i > 0:
                        raw_w = wraw[:, :]
                        pool.wait_ge(w_in, (p * (TILES - 1) + i) * 16)
                    else:
                        raw_w = craw[:, :]
                        pool.wait_ge(q_in, (p + 1) * 16)
                        pool.tensor_tensor(raw_w, raw_w, qscale[:, :].to_broadcast([P, D]), ALU.mult
                                           ).then_inc(w_scaled, 1)
                        pool.wait_ge(w_scaled, p + 1)
                    pool.wait_ge(w_begun, p * TILES + slot_free(i))
                    split(pool, w[:, slot, 0, :], w[:, slot, 1, :], raw_w, one, w_hi, p * TILES + i + 1, w_lo)

                def bias(h, ty):
                    n = 3 * h + ty
                    if ty == 0:
                        pool.wait_ge(rb_in, (p * 2 + h + 1) * 16)
                    if n >= 2:
                        pool.wait_ge(m_done, p * 2 * STEPS + 4 + [2, 6, 8, 10][n - 2])
                    for t in range(2):
                        b = rb[:, (4 if t == 0 else 0):(4 if t == 0 else 0) + KR, TYPE_OFF[ty] + 16:TYPE_OFF[ty] + 16 + KC]
                        c = comb[:, n % 2, t, :].rearrange("p (r c) -> p r c", c=KC)
                        rm = rowm[:, t, :].rearrange("p (r o) -> p r o", o=1).to_broadcast([P, KR, KC])
                        cm = colm[:, ty:ty + 1, :].to_broadcast([P, KR, KC])
                        pool.tensor_tensor(c, rm, b, ALU.subtract).then_inc(comb_t, 1)
                        pool.wait_ge(comb_t, p * 12 + 2 * n + t + 1)
                        pool.tensor_tensor(c, c, cm, ALU.add).then_inc(comb_done, 1)

                for i in range(PROJ):
                    split_tile(i)
                if A:
                    pool.wait_ge(m_done, p * 2 * STEPS)
                    bias(0, 0)
                    bias(0, 1)
                    split_tile(2)
                    split_tile(3)
                    bias(0, 2)
                    bias(1, 0)
                    bias(1, 1)
                    split_tile(4)
                    bias(1, 2)
                else:
                    for g in range(2):
                        pool.wait_ge(r_swp, p * 2 + g + 1)
                        pool.tensor_tensor(swp[:, :], swp[:, :], sin[:, g * 512:(g + 1) * 512], ALU.mult).then_inc(r_sin, 1)
                    for i in range(PROJ, TILES):
                        split_tile(i)

        @block.tensor
        def _(pe):
            with pe.Fori(0, PAIRS) as p:
                pe.wait_ge(exp_done, p * 2 * STEPS)
                for n in range(NG):
                    i, (t0, tn) = n // 3, GROUPS[n % 3]
                    if n % 3 == 0:
                        pe.wait_ge(w_lo, p * TILES + i + 1)
                    if n >= 4:
                        pe.wait_ge(x_used, p * NG + n - 3)
                    mm = split_mm(pe, s_ps[:, n % 4, 0:tn], lambda a, k: w[:, SLOT[i], a, k * P:(k + 1) * P],
                                  lambda b, k: hm[:, b, k, t0:t0 + tn], KD, w_begun if n % 3 == 0 else None)
                    mm.then_inc(proj_done, 1)

                def unit(u):
                    i, t0 = PROJ + u // UNITS, (u % UNITS) * UNIT
                    if u % UNITS == 0:
                        pe.wait_ge(w_lo, p * TILES + i + 1)
                    pe.wait_ge(g_done, p * GPP * UNITS + u)
                    mm = split_mm(pe, d_ps[:, 0:UNIT], lambda a, k: w[:, SLOT[i], a, k * P:(k + 1) * P],
                                  lambda b, k: hm[:, b, k, t0:t0 + UNIT], KD, w_begun if u % UNITS == 0 else None)
                    mm.then_inc(d_done, 1)

                def score(s, t, out, rhs):
                    if s < 2:
                        h, cols = s, lambda ap: ap[..., LAT + t * P:LAT + (t + 1) * P]
                    elif A:
                        h, cols = (s - 2) // 4, lambda ap: ap[..., (4 * t + (s - 2) % 4) * P:(4 * t + (s - 2) % 4 + 1) * P]
                    else:
                        h, cols = t, lambda ap: ap[..., (s - 2) * P:(s - 1) * P]
                    r0 = HD * h
                    pe.matmul(out, cols(q1[:, h, :]), rhs(h, slice(0, P)), start=True, stop=False)
                    return pe.matmul(out, cols(q2[r0:r0 + HD, :]), rhs(h, slice(r0, r0 + HD)), start=False, stop=True)

                def scores(s):
                    if s == 0:
                        pe.wait_ge(x_used, p * NG + NG)
                        pe.wait_ge(c_split, p * 3 + 3)
                        if not A:
                            pe.wait_ge(kk_in, (p + 1) * 64)
                    else:
                        pe.wait_ge(exp_done, p * 2 * STEPS + 2 * s)
                    for t in range(2):
                        if s < 2:
                            mm = score(s, t, s_ps[:, 2 * t, 0:PROMPT], lambda h, r: kk[r, h, LAT:TOK])
                            continue
                        score(s, t, s_ps[:, 2 * t + s % 2, :], lambda h, r: kc[r, h, :])
                        if A:
                            j = (s - 2) % 4
                            mm = score(s, t, near_bank(s, t),
                                       lambda h, r: grid(kk[r, h, :], 4 * t, KR, KC0[j], KC))
                        else:
                            w0 = min(max(s - 3, 0), 5) * P
                            mm = score(s, t, near_bank(s, t), lambda h, r: kk[r, h, w0:w0 + NB])
                    mm.then_inc(s_done, 1)

                def transposes(s, c):
                    n = CHUNK0[s] + c
                    if c == 0:
                        pe.wait_ge(p_done, p * 2 * STEPS + 2 * s + 2)
                    if n >= 2:
                        pe.wait_ge(lo_done, p * NCHUNK + n - 1)
                    for b, (kb, t) in enumerate(chunk_blocks(s)[c]):
                        mm = pe.transpose(t_ps[:, n % 2, b * P:(b + 1) * P], probs_block(s, t, kb), ident[:, :])
                    mm.then_inc(t_done, 1)

                def weighted(s, half):
                    if s == 0:
                        pe.wait_ge(vw_in, (p + 1) * 16 * (17 if A else 2))
                    last_chunk = CHUNKS[s] if half or s < 2 else 2
                    pe.wait_ge(lo_done, p * NCHUNK + CHUNK0[s] + last_chunk)
                    if half == 0:
                        pe.wait_ge(o_done, p * STEPS + s)
                    if s < 2:
                        h = s if A else 0
                        work = [(vp[:, kb, h * P:(h + 1) * P], 2 * kb, 0, 2) for kb in range(2)]
                    elif half == 0:
                        h = (s - 2) // 4 if A else 0
                        work = [(vc[:, kb, h, :], 2 * kb, 0, 2) for kb in range(4)]
                    elif A:
                        h, j = (s - 2) // 4, (s - 2) % 4
                        work = [(vw[:, rg * NCB + j, h * P:(h + 1) * P], b0, c0, nb)
                                for rg, b0, c0, nb in ((0, 8, 0, 1), (1, 9, 0, 2), (2, 11, 0, 2), (3, 13, 1, 1))]
                    else:
                        w0 = min(max(s - 3, 0), 5)
                        work = [(vw[:, w0 + kb, :], 8 + 2 * kb, 0, 2) for kb in range(3)]
                    for n, (v, b0, c0, nb) in enumerate(work):
                        for part in range(2):
                            mm = pe.matmul(o_ps[:, c0 * P:(c0 + nb) * P], v, pt[:, part, b0 * P:(b0 + nb) * P],
                                           start=(half == 0 and n == 0 and part == 0),
                                           stop=((half == 1 or s < 2) and n == len(work) - 1 and part == 1),
                                           skip_group_check=True)
                    mm.then_inc(pvb_done if half else pva_done, 1)

                for s in range(STEPS + 1):
                    if s < STEPS:
                        scores(s)
                    if s >= 4:
                        weighted(s - 2, 1)
                    if s > 0:
                        for c in range(min(2, CHUNKS[s - 1])):
                            transposes(s - 1, c)
                    unit(s)
                    if s > 0:
                        for c in range(2, CHUNKS[s - 1]):
                            transposes(s - 1, c)
                        weighted(s - 1, 0)
                unit(STEPS + 1)
                weighted(STEPS - 1, 1)

        @block.scalar
        def _(act):
            with act.Fori(0, PAIRS) as p:
                act.wait_ge(craw_in, (p + 1) * 32)
                for h in range(2):
                    r0 = HD * h
                    act.activation(kc[r0:r0 + HD, h, :], craw[r0:r0 + HD, 0:PAST], ACT.Copy).then_inc(ckh, 1)
                act.activation(vc[:, :, :, 0:HD],
                               craw[:, PAST:PAST + 4 * CH * HD].rearrange("p (b h c) -> p b h c", h=CH, c=HD),
                               ACT.Copy).then_inc(cvh, 1)
                for n in range(NG):
                    t0, tn = GROUPS[n % 3]
                    tok, bank = slice(t0, t0 + tn), s_ps[:, n % 4, 0:tn]
                    act.wait_ge(proj_done, p * NG + n + 1)
                    if A and n < 3:
                        act.activation(tiled(q1[0:HD, 0, tok]), rows(bank[0:HD, :]), ACT.Copy).then_inc(xa, 1)
                        act.wait_ge(xd, p * 9 + 2 * n + 1)
                        act.activation(tiled(q1[0:HD, 1, tok]), rows(bank[HD:P, :]), ACT.Copy).then_inc(xa, 1)
                    elif A:
                        act.activation(kk[0:HD, 0, tok], bank[0:HD, :], ACT.Copy).then_inc(xa, 1)
                    else:
                        act.wait_ge(x_used, p * NG + n)
                        act.activation((rot if n == 2 else raw)[:, 0:tn], bank, ACT.Copy).then_inc(r_raw, 1)
                        if n < 2:
                            act.wait_ge(r_rot, p * 2 + n + 1)
                        else:
                            act.wait_ge(r_raw, p * 3 + 3)
                        for h in range(2):
                            act.activation(q1[0:HD, h, tok], rot[h * HD:(h + 1) * HD, 0:tn], ACT.Copy
                                           ).then_inc(xa, 1)

                if A:
                    act.wait_ge(ko_done, p + 1)
                    act.dma_start(io["new_ak"][p], kout[:, :]).then_inc(ko_out, 16)

                def high(s, chunks):
                    for c in chunks:
                        n = CHUNK0[s] + c
                        cols = len(chunk_blocks(s)[c]) * P
                        act.wait_ge(t_done, p * NCHUNK + n + 1)
                        if c == 0:
                            act.wait_ge(pva_done, p * STEPS + s)
                        if c == 2:
                            act.wait_ge(pvb_done, p * (STEPS - 2) + s - 2)
                        act.activation(pt[:, 0, c * 512:c * 512 + cols], t_ps[:, n % 2, 0:cols], ACT.Copy
                                       ).then_inc(hi_done, 1)

                def exps(s):
                    for t in range(2):
                        n = p * 2 * STEPS + 2 * s + t + 1
                        act.wait_ge(m_done, n)
                        if t == 0:
                            act.wait_ge(t_done, p * NCHUNK + (CHUNK0[s - 1] + min(2, CHUNKS[s - 1]) if s > 0 else 0))
                            act.wait_ge(r_done, p * STEPS + s)
                        act.activation(probs_run(s, t), scores_run(s, t), ACT.Exp, bias=mx[:, t:t + 1], scale=-1.0,
                                       accum_out=den[:, t:t + 1]).then_inc(exp_done, 1)
                        if not A:
                            h = s if s < 2 else t
                            act.activation(esk[:, t:t + 1], nsk[:, h:h + 1], ACT.Exp, bias=mx[:, t:t + 1], scale=-1.0
                                           ).then_inc(esk_done, 1)

                def gate_out(u):
                    act.wait_ge(g_done, p * GPP * UNITS + u + 1)
                    blk = (p + base) * GPP + u // UNITS
                    act.dma_start(io["gates_d"][blk, :, (u % UNITS) * UNIT:(u % UNITS + 1) * UNIT], gst[:, u % 2, :]
                                  ).then_inc(g_out[u % 2], 16)

                def gate(u):
                    act.wait_ge(d_done, p * GPP * UNITS + u + 1)
                    act.wait_ge(g_out[u % 2], (p * (GPP * UNITS // 2) + u // 2) * 16)
                    act.activation(gst[:, u % 2, :], d_ps[:, 0:UNIT], ACT.Copy).then_inc(g_done, 1)
                    if u > 0:
                        gate_out(u - 1)

                def low_half(s):
                    if s < 2:
                        act.wait_ge(pva_done, p * STEPS + s + 1)
                    else:
                        act.wait_ge(pvb_done, p * (STEPS - 2) + s - 1)
                    act.wait_ge(o_done, p * STEPS + s)
                    act.activation(otmp[:, :], o_ps[HD:P, 0:2 * P], ACT.Copy).then_inc(ot_done, 1)

                for s in range(STEPS + 1):
                    if s >= 2:
                        low_half(s - 2)
                    if s > 0:
                        high(s - 1, range(min(2, CHUNKS[s - 1])))
                    if s < STEPS:
                        exps(s)
                    gate(s)
                    if s > 0:
                        high(s - 1, range(2, CHUNKS[s - 1]))
                gate(STEPS + 1)
                gate_out(STEPS + 1)
                low_half(STEPS - 1)
                act.wait_ge(o_done, (p + 1) * STEPS)
                act.dma_start(io["o_d"][p + base], ost[:, :]).then_inc(o_out, 16)
            act.wait_ge(g_out[0], PAIRS * GPP * UNITS // 2 * 16)
            act.wait_ge(g_out[1], PAIRS * GPP * UNITS // 2 * 16)
            act.wait_ge(o_out, PAIRS * 16)
            if A:
                act.wait_ge(ko_out, PAIRS * 16)

        @block.vector
        def _(dve):
            if not A:
                dve.wait_ge(const_in, 64)
                dve.tensor_scalar(nsink[:, :], sink[:, :], -1.0, None, ALU.mult).then_inc(nsk_done, 1)
                dve.wait_ge(nsk_done, 1)
            with dve.Fori(0, PAIRS) as p:
                if not A:
                    dve.tensor_copy(nsk[:, :], nsink[:, bass.ds(p * 2, 2)]).then_inc(nsk_done, 1)
                for h in range(2):
                    r0, r1 = HD * h, HD * (1 - h)
                    dve.wait_ge(ckh, p * 2 + h + 1)
                    dve.tensor_tensor(kc[r1:r1 + HD, h, :], craw[r0:r0 + HD, 0:PAST],
                                      kc[r0:r0 + HD, h, :].bitcast(F32), ALU.subtract).then_inc(c_split, 1)
                dve.wait_ge(cvh, p + 1)
                dve.tensor_tensor(vc[:, :, :, HD:],
                                  craw[:, PAST:PAST + 4 * CH * HD].rearrange("p (b h c) -> p b h c", h=CH, c=HD),
                                  vc[:, :, :, 0:HD].bitcast(F32), ALU.subtract).then_inc(c_split, 1)
                for n in range(NG):
                    t0, tn = GROUPS[n % 3]
                    tok, bank = slice(t0, t0 + tn), s_ps[:, n % 4, 0:tn]
                    if A:
                        dve.wait_ge(proj_done, p * NG + n + 1)
                    if A and n < 3:
                        dve.tensor_copy(tiled(q1[HD:P, 1, tok]), rows(bank[HD:P, :])).then_inc(xd, 1)
                        dve.wait_ge(xa, p * 9 + 2 * n + 1)
                        dve.tensor_copy(tiled(q1[HD:P, 0, tok]), rows(bank[0:HD, :])).then_inc(xd, 1)
                        dve.tensor_tensor(tiled(q2[0:HD, tok]), rows(bank[0:HD, :]), tiled(q1[0:HD, 0, tok]).bitcast(F32),
                                          ALU.subtract)
                        dve.wait_ge(xa, p * 9 + 2 * n + 2)
                        dve.wait_ge(xd, p * 9 + 2 * n + 1)
                        dve.tensor_tensor(tiled(q2[HD:P, tok]), rows(bank[HD:P, :]), tiled(q1[HD:P, 1, tok]).bitcast(F32),
                                          ALU.subtract).then_inc(x_used, 1)
                    elif A:
                        dve.tensor_copy(kk[HD:P, 1, tok], bank[HD:P, :]).then_inc(xd, 1)
                        dve.wait_ge(xa, p * 9 + n + 4)
                        dve.wait_ge(xd, p * 9 + n + 4)
                        if n == 5:
                            dve.wait_ge(ko_out, p * 16)
                            dve.tensor_copy(kout[:, :], bank).then_inc(ko_done, 1)
                        dve.tensor_tensor(kk[HD:P, 0, tok], bank[0:HD, :], kk[0:HD, 0, tok].bitcast(F32), ALU.subtract)
                        dve.tensor_tensor(kk[0:HD, 1, tok], bank[HD:P, :], kk[HD:P, 1, tok].bitcast(F32), ALU.subtract
                                          ).then_inc(x_used, 1)
                    else:
                        dve.wait_ge(r_raw, p * 3 + n + 1)
                        if n < 2:
                            dve.tensor_tensor(rot[:, :], raw[:, :], cos[:, tok], ALU.mult).then_inc(r_cos, 1)
                            dve.stream_shuffle(swp[:, :], raw[:, :], SWAP16).then_inc(r_swp, 1)
                            dve.wait_ge(r_sin, p * 2 + n + 1)
                            dve.wait_ge(r_cos, p * 2 + n + 1)
                            dve.tensor_tensor(rot[:, :], rot[:, :], swp[:, :], ALU.add).then_inc(r_rot, 1)
                            dve.wait_ge(r_rot, p * 2 + n + 1)
                        for h in range(2):
                            dve.tensor_copy(q1[HD:P, h, tok], rot[h * HD:(h + 1) * HD, 0:tn]).then_inc(xd, 1)
                        dve.wait_ge(xa, p * 6 + 2 * n + 2)
                        dve.wait_ge(xd, p * 6 + 2 * n + 2)
                        for h in range(2):
                            r = slice(h * HD, (h + 1) * HD)
                            last = dve.tensor_tensor(q2[r, tok], rot[r, 0:tn], q1[r, h, tok].bitcast(F32), ALU.subtract)
                        last.then_inc(x_used, 1)

                def low(s, chunks):
                    for c in chunks:
                        n = CHUNK0[s] + c
                        cols = len(chunk_blocks(s)[c]) * P
                        dve.wait_ge(hi_done, p * NCHUNK + n + 1)
                        dve.tensor_tensor(pt[:, 1, c * 512:c * 512 + cols], t_ps[:, n % 2, 0:cols],
                                          pt[:, 0, c * 512:c * 512 + cols].bitcast(F32), ALU.subtract).then_inc(lo_done, 1)

                def minima(s):
                    width = PROMPT if s < 2 else PAST
                    dve.wait_ge(s_done, p * STEPS + s + 1)
                    ctx_min = mx if A and s < 2 else mn
                    if A and s >= 2:
                        h, j = (s - 2) // 4, (s - 2) % 4
                        n = 3 * h + BIAS_TYPE[j]
                        dve.wait_ge(comb_done, p * 12 + 2 * n + 2)
                    red = dve.tensor_reduce(ctx_min[:, :],
                                            s_ps[:, :, :].rearrange("p (t b) c -> p t b c", b=2)[:, :, s % 2 if s >= 2 else 0, 0:width],
                                            AX.X, ALU.min)
                    if A and s < 2:
                        red.then_inc(m_done, 2)
                        return
                    red.then_inc(m1_done, 1)
                    if s >= 2:
                        for t in range(2):
                            near = comb[:, n % 2, t, :] if A else \
                                band[:, 0 if s == 2 else 2 if s == STEPS - 1 else 1, :]
                            bank = near_bank(s, t)
                            red = dve.tensor_tensor_reduce(bank, bank, near, 1.0, BIG, ALU.add, ALU.min, nm[:, t:t + 1])
                        red.then_inc(m2_done, 1)
                    if A:
                        dve.wait_ge(m1_done, p * (STEPS - 2) + s - 1)
                        dve.wait_ge(m2_done, p * (STEPS - 2) + s - 1)
                        dve.tensor_tensor(mx[:, :], mn[:, :], nm[:, :], ALU.min).then_inc(m_done, 2)
                        return
                    dve.wait_ge(m1_done, p * STEPS + s + 1)
                    if s < 2:
                        sk = nsk[:, s:s + 1].to_broadcast([P, 2])
                    else:
                        sk = nsk[:, :]
                        dve.wait_ge(m2_done, p * (STEPS - 2) + s - 1)
                        dve.tensor_tensor(nm[:, :], mn[:, :], nm[:, :], ALU.min).then_inc(m3_done, 1)
                        dve.wait_ge(m3_done, p * (STEPS - 2) + s - 1)
                    if s == 0:
                        dve.wait_ge(nsk_done, p + 2)
                    dve.tensor_tensor(mx[:, :], (mn if s < 2 else nm)[:, :], sk, ALU.min).then_inc(m_done, 2)

                def normalise(s):
                    dve.wait_ge(exp_done, p * 2 * STEPS + 2 * s + 2)
                    if s > 0:
                        dve.wait_ge(p_done, p * 2 * STEPS + 2 * s)
                    if A:
                        dve.reciprocal(rden[:, :], den[:, :]).then_inc(r_done, 1)
                    else:
                        dve.wait_ge(esk_done, p * 2 * STEPS + 2 * s + 2)
                        dve.tensor_tensor(den2[:, :], den[:, :], esk[:, :], ALU.add).then_inc(den_done, 1)
                        dve.wait_ge(den_done, p * STEPS + s + 1)
                        dve.reciprocal(rden[:, :], den2[:, :]).then_inc(r_done, 1)
                    dve.wait_ge(r_done, p * STEPS + s + 1)
                    for t in range(2):
                        dve.tensor_scalar(probs_run(s, t), probs_run(s, t), rden[:, t:t + 1], None, ALU.mult
                                          ).then_inc(p_done, 1)

                def add_halves(s):
                    dve.wait_ge(ot_done, p * STEPS + s + 1)
                    if s == 0:
                        dve.wait_ge(o_out, p * 16)
                    if s < 2:
                        dve.tensor_tensor(ost[HD * s:HD * s + HD, LAT:TOK], o_ps[0:HD, 0:2 * P], otmp[:, :], ALU.add
                                          ).then_inc(o_done, 1)
                    elif A:
                        h, j = (s - 2) // 4, (s - 2) % 4
                        dst = grid(ost[HD * h:HD * h + HD, :], 0, ROWS, QC * j, QC)
                        dve.tensor_tensor(dst, o_ps[0:HD, 0:2 * P].rearrange("p (r c) -> p r c", c=QC),
                                          otmp[:, :].rearrange("p (r c) -> p r c", c=QC), ALU.add).then_inc(o_done, 1)
                    else:
                        for t in range(2):
                            last = dve.tensor_tensor(ost[HD * t:HD * t + HD, (s - 2) * P:(s - 1) * P],
                                                     o_ps[0:HD, t * P:(t + 1) * P], otmp[:, t * P:(t + 1) * P], ALU.add)
                        last.then_inc(o_done, 1)

                for s in range(STEPS + 1):
                    if s < STEPS:
                        minima(s)
                    if s >= 2:
                        add_halves(s - 2)
                    if s > 0:
                        low(s - 1, range(min(2, CHUNKS[s - 1])))
                    if s < STEPS:
                        normalise(s)
                    if s > 0:
                        low(s - 1, range(2, CHUNKS[s - 1]))
                add_halves(STEPS - 1)


def merge(nc, io, mg):
    with ExitStack() as ctx:
        def sb(name, shape, dt=F32):
            return ctx.enter_context(nc.sbuf_tensor(f"{name}_m", shape, dt))

        def sem(name):
            return nc.alloc_semaphore(name=f"{name}_m")

        og = sb("og", [P, 2, KD, TOK], F32R)
        wraw = sb("wraw", [P, 2, D])
        w = sb("w", [P, 2, 2, D], F32R)
        gt = sb("gt", [P, 2, 2, 512])
        tp = sb("tp", [P, 2, 2, 512])
        one = sb("one", [P, 1])
        ones_set = sem("ones_set")
        ya = ctx.enter_context(nc.psum_tensor("ya", [P, 4, 512], F32))
        yb = ctx.enter_context(nc.psum_tensor("yb", [P, 4, 512], F32))

        wraw_in = [sem("wraw_in0"), sem("wraw_in1")]
        gt_in = [sem("gt_in0"), sem("gt_in1")]
        w_hi, w_lo, w_begun = sem("w_hi"), sem("w_lo"), sem("w_begun")
        act_done, prod, summed, hi, lo, y_done = (sem(n) for n in ("act", "prod", "summed", "hi", "lo", "y_done"))
        block = ctx.enter_context(nc.Block())
        PIECES = [(e, t0, n) for e in range(2) for t0, n in GROUPS]
        TURNS = KD // 2
        NP = 6 * TURNS

        @block.sync
        def _(sp):
            def load_w(jj, e):
                sp.wait_ge(w_lo, jj * 2)
                sp.dma_start(wraw[:, e, :], io["w_br"][jj * 2 + e]).then_inc(wraw_in[e], 16)

            with sp.Fori(0, TURNS) as b:
                for n, (e, t0, tn) in enumerate(PIECES):
                    if n < 2:
                        sp.wait_ge(prod, b * 6)
                    else:
                        sp.wait_ge(prod, b * 6 + n - 1)
                    sp.dma_start(gt[:, n % 2, 0, 0:tn], io["o_d"][b * 2 + e, :, t0:t0 + tn]).then_inc(gt_in[n % 2], 16)
                    sp.dma_start(gt[:, n % 2, 1, 0:tn], io["gates_d"][b * 2 + e, :, t0:t0 + tn]).then_inc(gt_in[n % 2], 16)
            with sp.Fori(0, TURNS) as jj:
                for n, (e, t0, tn) in enumerate(PIECES):
                    if n % 3 == 0:
                        load_w(jj, e)
                    if n < 2:
                        sp.wait_ge(prod, NP + jj * 12)
                    else:
                        sp.wait_ge(prod, NP + jj * 12 + 2 * (n - 1))
                    for which in range(2):
                        sp.dma_start(gt[:, n % 2, which, 0:tn],
                                     io["gates_d"][jj * 2 + (8 + 8 * which + e), :, t0:t0 + tn]).then_inc(gt_in[n % 2], 16)

        @block.scalar
        def _(act):
            with act.Fori(0, TURNS) as b:
                for n, (e, t0, tn) in enumerate(PIECES):
                    act.wait_ge(gt_in[n % 2], (b * 3 + n // 2 + 1) * 32)
                    act.activation(gt[:, n % 2, 1, 0:tn], gt[:, n % 2, 1, 0:tn], ACT.Silu).then_inc(act_done, 1)
            with act.Fori(0, TURNS) as jj:
                for n, (e, t0, tn) in enumerate(PIECES):
                    act.wait_ge(gt_in[n % 2], (jj * 3 + n // 2 + 1 + NP // 2) * 32)
                    act.activation(gt[:, n % 2, :, 0:tn], gt[:, n % 2, :, 0:tn], ACT.Sigmoid).then_inc(act_done, 1)
                    act.wait_ge(summed, jj * 6 + n + 1)
                    act.activation(mg[:, 0, jj * 2 + e, t0:t0 + tn], tp[:, n % 2, 0, 0:tn], ACT.Copy).then_inc(hi, 1)

        @block.gpsimd
        def _(pool):
            pool.memset(one[:, :], 1.0).then_inc(ones_set, 1)
            pool.wait_ge(ones_set, 1)
            with pool.Fori(0, TURNS) as b:
                for n, (e, t0, tn) in enumerate(PIECES):
                    pool.wait_ge(hi, b * 6 + n + 1)
                    pool.tensor_tensor(og[:, 1, b * 2 + e, t0:t0 + tn], tp[:, n % 2, 0, 0:tn],
                                       og[:, 0, b * 2 + e, t0:t0 + tn].bitcast(F32), ALU.subtract).then_inc(lo, 1)
            with pool.Fori(0, TURNS) as jj:
                for e in range(2):
                    pool.wait_ge(wraw_in[e], (jj + 1) * 16)
                    pool.wait_ge(w_begun, jj * 2 + e)
                    split(pool, w[:, e, 0, :], w[:, e, 1, :], wraw[:, e, :], one, w_hi, jj * 2 + e + 1, w_lo)
                for n, (e, t0, tn) in enumerate(PIECES):
                    pool.wait_ge(hi, NP + jj * 6 + n + 1)
                    pool.tensor_tensor(mg[:, 1, jj * 2 + e, t0:t0 + tn], tp[:, n % 2, 0, 0:tn],
                                       mg[:, 0, jj * 2 + e, t0:t0 + tn].bitcast(F32), ALU.subtract).then_inc(lo, 1)

        @block.tensor
        def _(pe):
            pe.wait_ge(lo, NP)
            with pe.Fori(0, TURNS) as jj:
                for n, (e, t0, tn) in enumerate(PIECES):
                    if n % 3 == 0:
                        pe.wait_ge(w_lo, jj * 2 + e + 1)
                    pe.wait_ge(prod, NP + jj * 12 + (2 * (n - 3) if n > 3 else 0))
                    for br, y in ((0, ya), (1, yb)):
                        split_mm(pe, y[:, n % 4, 0:tn], lambda a, k: w[:, e, a, (4 * br + k) * P:(4 * br + k + 1) * P],
                                 lambda b, k: og[:, b, 4 * br + k, t0:t0 + tn], 4,
                                 w_begun if n % 3 == 0 and br == 0 else None).then_inc(y_done, 1)

        @block.vector
        def _(dve):
            with dve.Fori(0, TURNS) as b:
                for n, (e, t0, tn) in enumerate(PIECES):
                    dve.wait_ge(act_done, b * 6 + n + 1)
                    if n < 2:
                        dve.wait_ge(lo, b * 6)
                    else:
                        dve.wait_ge(lo, b * 6 + n - 1)
                    dve.tensor_tensor(tp[:, n % 2, 0, 0:tn], gt[:, n % 2, 0, 0:tn], gt[:, n % 2, 1, 0:tn], ALU.mult
                                      ).then_inc(prod, 1)
                    dve.wait_ge(prod, b * 6 + n + 1)
                    dve.tensor_copy(og[:, 0, b * 2 + e, t0:t0 + tn], tp[:, n % 2, 0, 0:tn]).then_inc(hi, 1)
            with dve.Fori(0, TURNS) as jj:
                for n, (e, t0, tn) in enumerate(PIECES):
                    dve.wait_ge(act_done, NP + jj * 6 + n + 1)
                    dve.wait_ge(y_done, (jj * 6 + n) * 2 + 2)
                    if n < 2:
                        dve.wait_ge(lo, NP + jj * 6)
                    else:
                        dve.wait_ge(lo, NP + jj * 6 + n - 1)
                    for br, y in ((0, ya), (1, yb)):
                        dve.tensor_tensor(tp[:, n % 2, br, 0:tn], y[:, n % 4, 0:tn], gt[:, n % 2, br, 0:tn], ALU.mult
                                          ).then_inc(prod, 1)
                    dve.wait_ge(prod, NP + (jj * 6 + n) * 2 + 2)
                    dve.tensor_tensor(tp[:, n % 2, 0, 0:tn], tp[:, n % 2, 0, 0:tn], tp[:, n % 2, 1, 0:tn], ALU.add
                                      ).then_inc(summed, 1)


def output(nc, io, mg):
    with ExitStack() as ctx:
        def sb(name, shape, dt=F32):
            return ctx.enter_context(nc.sbuf_tensor(f"{name}_o", shape, dt))

        def sem(name):
            return nc.alloc_semaphore(name=f"{name}_o")

        wraw = sb("wraw", [P, 2, D])
        w = sb("w", [P, 2, KD, D], F32R)
        x = sb("x", [P, 2, D])
        y = sb("y", [P, 2, D])
        gate = sb("gate", [P, 2 * D])
        gain = sb("gain", [P, D])
        sq = sb("sq", [P, D])
        ss, rms, rstd = sb("ss", [P, 2]), sb("rms", [P, 2]), sb("rstd", [P, 2])
        epsc = sb("eps", [P, 1])
        y_ps = ctx.enter_context(nc.psum_tensor("y_ps", [P, 4, D], F32))

        wraw_in = [sem("wraw_in0"), sem("wraw_in1")]
        x_in = [sem("x_in0"), sem("x_in1")]
        y_out = [sem("y_out0"), sem("y_out1")]
        rows_in, eps_set, w_hi, w_lo, mm_done, gated, res, sq_done, rms_done, r_done, y_done = (
            sem(n) for n in ("rows_in", "eps_set", "w_hi", "w_lo", "mm", "gated", "res", "sq", "rms", "r", "y"))
        block = ctx.enter_context(nc.Block())
        TT = TOK // P
        TURNS = TT // 2

        @block.sync
        def _(sp):
            for k in range(KD):
                if k >= 2:
                    sp.wait_ge(w_lo, k - 1)
                sp.dma_start(wraw[:, k % 2, :], io["w_out"][:, k, :]).then_inc(wraw_in[k % 2], 16)
            sp.dma_start(gate[:, :], io["gate_d"].rearrange("a b -> (a b)").rearrange("(o n) -> o n", o=1).to_broadcast([P, 2 * D])
                         ).then_inc(rows_in, 16)
            sp.dma_start(gain[:, :], io["gain"].to_broadcast([P, D])).then_inc(rows_in, 16)
            with sp.Fori(0, TURNS) as i:
                for e in range(2):
                    sp.wait_ge(res, i * 2)
                    sp.dma_start(x[:, e, :], io["x"][bass.ds(i * 256 + e * P, P), :]).then_inc(x_in[e], 16)
                for e in range(2):
                    sp.wait_ge(y_done, i * 2 + e + 1)
                    sp.dma_start(io["y"][bass.ds(i * 256 + e * P, P), :], y[:, e, :]).then_inc(y_out[e], 16)
            sp.wait_ge(y_out[0], TURNS * 16)
            sp.wait_ge(y_out[1], TURNS * 16)

        @block.gpsimd
        def _(pool):
            pool.memset(epsc[:, :], EPS).then_inc(eps_set, 1)
            with pool.Fori(0, TURNS) as i:
                for e in range(2):
                    pool.wait_ge(x_in[e], (i + 1) * 16)
                    pool.wait_ge(gated, i * 2 + e + 1)
                    pool.tensor_tensor(y[:, e, :], y[:, e, :], x[:, e, :], ALU.add).then_inc(res, 1)

        @block.tensor
        def _(pe):
            for t in range(TT):
                if t == 0:
                    pe.wait_ge(w_lo, KD)
                if t >= 4:
                    pe.wait_ge(gated, t - 3)
                for n in range(2):
                    mm = split_mm(pe, y_ps[:, t % 4, n * 512:(n + 1) * 512], lambda a, k: mg[:, a, k, t * P:(t + 1) * P],
                                  lambda b, k: w[:, b, k, n * 512:(n + 1) * 512], KD)
                mm.then_inc(mm_done, 1)

        @block.scalar
        def _(act):
            for k in range(KD):
                act.wait_ge(wraw_in[k % 2], 16 * (k // 2 + 1))
                act.activation(w[:, 0, k, :], wraw[:, k % 2, :], ACT.Copy).then_inc(w_hi, 1)
            act.wait_ge(eps_set, 1)
            with act.Fori(0, TURNS) as i:
                for e in range(2):
                    act.wait_ge(res, i * 2 + e + 1)
                    act.wait_ge(r_done, i * 2)
                    act.activation(sq[:, :], y[:, e, :], ACT.Square, accum_out=ss[:, e:e + 1]).then_inc(sq_done, 1)
                    act.wait_ge(sq_done, i * 2 + e + 1)
                    act.activation(rms[:, e:e + 1], ss[:, e:e + 1], ACT.Sqrt, bias=epsc[:, 0:1], scale=1.0 / D
                                   ).then_inc(rms_done, 1)

        @block.vector
        def _(dve):
            for k in range(KD):
                dve.wait_ge(w_hi, k + 1)
                dve.tensor_tensor(w[:, 1, k, :], wraw[:, k % 2, :], w[:, 0, k, :].bitcast(F32), ALU.subtract
                                  ).then_inc(w_lo, 1)
            dve.wait_ge(rows_in, 32)
            with dve.Fori(0, TURNS) as i:
                for e in range(2):
                    dve.wait_ge(mm_done, i * 2 + e + 1)
                    dve.wait_ge(y_out[e], i * 16)
                    dve.tensor_tensor(y[:, e, :], y_ps[:, bass.ds((i % 2) * 2 + e, 1), :].rearrange("p a b -> p (a b)"),
                                      gate[:, bass.ds((i // 4) * D, D)], ALU.mult).then_inc(gated, 1)
                for e in range(2):
                    dve.wait_ge(rms_done, i * 2 + e + 1)
                    dve.reciprocal(rstd[:, e:e + 1], rms[:, e:e + 1]).then_inc(r_done, 1)
                    dve.wait_ge(r_done, i * 2 + e + 1)
                    dve.scalar_tensor_tensor(out=y[:, e, :], in0=y[:, e, :], scalar=rstd[:, e:e + 1], in1=gain[:, :],
                                             op0=ALU.mult, op1=ALU.mult).then_inc(y_done, 1)


def build(nc, io):
    before = nc.snapshot_sems()
    with ExitStack() as ctx:
        hm = ctx.enter_context(nc.sbuf_tensor("h", [P, 2, KD, TOK], F32R))
        ident = ctx.enter_context(nc.sbuf_tensor("ident_sb", [P, P], F32))
        with ExitStack() as first:
            wv = first.enter_context(nc.sbuf_tensor("wv", [P, 2, KD, VH * HD], F32R))
            wkb = first.enter_context(nc.sbuf_tensor("wkb", [P, 2, D], F32R))
            startup(nc, io, hm, ident, wv, wkb)
            values(nc, io, hm, wv, wkb)
        pairs(nc, io, hm, ident, "a")
        nc.clear_and_free_semaphores(nc.allocated_since(before))
        nc.all_engine_barrier()
        pairs(nc, io, hm, ident, "b")
    with ExitStack() as ctx:
        mg = ctx.enter_context(nc.sbuf_tensor("mg", [P, 2, KD, TOK], F32R))
        merge(nc, io, mg)
        output(nc, io, mg)


def constants():
    c = {"ident": np.eye(P, dtype=np.float32)}
    qr, qc = np.arange(P) // QC, np.arange(P) % QC
    row = np.zeros((P, 2, KR), np.float32)
    for t in range(2):
        r, kr = QR * t + qr[:, None], 4 * t + np.arange(KR)[None]
        start = np.clip(r - NA_KH // 2, 0, ROWS - NA_KH)
        row[:, t] = np.where((kr >= start) & (kr < start + NA_KH), 0.0, BIG)
    col = np.zeros((P, 3, KC), np.float32)
    for ty, j in enumerate(TYPE_BLOCK):
        q, kc = j * QC + qc[:, None], KC0[j] + np.arange(KC)[None]
        start = np.clip(q - NA_KW // 2, 0, GRID_W - NA_KW)
        col[:, ty] = np.where((kc >= start) & (kc < start + NA_KW), 0.0, BIG)
    band = np.zeros((P, 3, NB), np.float32)
    for ty in range(3):
        off = np.arange(NB)[None] - P * ty - np.arange(P)[:, None]
        band[:, ty] = np.where(np.abs(off) <= WINDOW, 0.0, BIG)
    half = HD // 2
    inv = (np.float32(10000.0) ** (-np.arange(0, half, 2, dtype=np.float32) / np.float32(half))).astype(np.float32)
    t = np.arange(LAT)
    pos = np.stack([t // GRID_W, t % GRID_W]).astype(np.float32)
    ang = pos[:, None, :] * inv[None, :, None]
    cos, sin = np.cos(ang).astype(np.float32), np.sin(ang).astype(np.float32)
    c["cos"] = np.tile(np.concatenate([cos, cos], 1).reshape(HD, LAT), (2, 1))
    c["sin"] = np.tile(np.concatenate([-sin, sin], 1).reshape(HD, LAT), (2, 1))
    c["rowmask"], c["colmask"], c["band"] = row, col, band
    return c


def layout(x_prompt, x_sample, cache_a_k, cache_a_v, cache_b_k, cache_b_v, c, c_ctx, w_ada, b_ada, w_in, rpb_a,
           sink_b, w_br_a, w_br_b, w_out, final_norm_g):
    f = lambda a: np.asarray(a)
    a = constants()
    a["x"] = np.concatenate([f(x_sample)[0], f(x_prompt)[0]])
    a["c_col"] = np.stack([f(c)[0], f(c_ctx)], -1).reshape(KD, P, 2).transpose(1, 0, 2)
    a["b_col"] = f(b_ada)[0, :2 * D].reshape(2 * KD, P).T
    a["b_gate"] = f(b_ada)[:, 2 * D:]
    a["w_ada"] = f(w_ada)[0]
    blocks = f(w_in)[0].reshape(KD, P, -1, P).transpose(2, 1, 0, 3).reshape(-1, P, D)
    a["w_qa"], a["w_ka"], a["w_qb"], a["w_kb"] = blocks[0:4], blocks[4:8], blocks[16:20], blocks[20]
    a["w_gate"] = np.concatenate([blocks[12:16], blocks[22:26], blocks[26:42]])
    cols = f(w_in)[0].reshape(KD, P, -1).transpose(1, 0, 2)
    a["w_v"] = np.concatenate([cols[:, :, 1024:1536], cols[:, :, 2688:2816]], -1)
    a["w_br"] = np.concatenate([f(w)[0].reshape(4, P, KD, P).transpose(2, 1, 0, 3) for w in (w_br_a, w_br_b)], 2
                               ).reshape(KD, P, D)
    a["w_out"] = f(w_out)[0].reshape(KD, P, D).transpose(1, 0, 2)
    a["cka"] = f(cache_a_k)[0, 0].transpose(1, 2, 0).reshape(PAIRS, P, PAST)
    a["cva"] = f(cache_a_v)[0, 0].reshape(4, P, PAIRS, P).transpose(2, 1, 0, 3).reshape(PAIRS, P, 4 * P)
    kb = f(cache_b_k)[0, 0].transpose(1, 2, 0)
    a["ckb"] = np.stack([np.concatenate([kb[p // 2]] * 2) for p in range(PAIRS)])
    vb = f(cache_b_v)[0, 0].reshape(4, P, 2, HD).transpose(2, 1, 0, 3).reshape(2, P, 4 * HD)
    a["cvb"] = np.stack([vb[p // 2] for p in range(PAIRS)])
    pad = np.pad(f(rpb_a)[0], ((0, 0), (4, 4), (16, 16)))
    a["bias"] = np.stack([pad[:, QR - 1 - r:QR - 1 - r + BR, QC - 1 - q:QC - 1 - q + BC]
                          for r in range(QR) for q in range(QC)], 1)
    a["sink"] = f(sink_b)
    a["gain"] = f(final_norm_g)[None]
    return {k: np.ascontiguousarray(v) for k, v in a.items()}


SCRATCH = {"v_d": [TOK, VH * 2 * HD], "kb_d": [2, 2, HD, TOK], "gates_d": [GATE_BLOCKS, P, TOK],
           "o_d": [KD, P, TOK], "gate_d": [2, D]}
OUTS = {"y": [TOK, D], "new_ak": [PAIRS, P, PROMPT], "new_av": [PROMPT, 8 * HD], "new_bk": [P, PROMPT],
        "new_bv": [PROMPT, 2 * HD]}


def kernel(**inputs):
    import concourse.bacc as bacc
    from concourse.bass_utils import run_bass_kernel_spmd

    nc = bacc.Bacc("TRN2", target_bir_lowering=False, num_devices=1)
    arrays = {f"in_{k}": v for k, v in layout(**inputs).items()}
    io = {}
    for name, a in arrays.items():
        io[name[3:]] = nc.dram_tensor(name, list(a.shape), mybir.dt.from_np(a.dtype), kind="ExternalInput").ap()
    for name, shape in SCRATCH.items():
        io[name] = nc.dram_tensor(name, shape, F32, kind="Internal").ap()
    for name, shape in OUTS.items():
        io[name] = nc.dram_tensor(name, shape, F32, kind="ExternalOutput").ap()
    build(nc, io)
    got = run_bass_kernel_spmd(nc, [arrays], core_ids=[0]).results[0]
    y = got["y"]
    to_tok = lambda k, h: k.reshape(h, HD, PROMPT).transpose(2, 0, 1)[None, None]
    return (y[LAT:][None], y[:LAT][None], to_tok(got["new_ak"], NA_HEADS),
            got["new_av"].reshape(1, 1, PROMPT, NA_HEADS, HD), to_tok(got["new_bk"], 2),
            got["new_bv"].reshape(1, 1, PROMPT, 2, HD))
```

```python
from contextlib import ExitStack

import numpy as np

import concourse.bass as bass
from concourse import mybir

F32 = mybir.dt.float32
F32R = mybir.dt.float32r
ALU = mybir.AluOpType
ACT = mybir.ActivationFunctionType
AX = mybir.AxisListType

P = 128
D = 1024
KD = D // P
LAT, PROMPT = 1024, 256
TOK = LAT + PROMPT
PAST = 512
HD = 64
GRID_W = 64
ROWS = LAT // GRID_W
NA_HEADS, NA_KH, NA_KW = 8, 8, 16
QR, QC = 8, 16
KR, KC = 12, 32
NCB = GRID_W // QC
KC0 = [min(max(j * QC - (KC - QC) // 2, 0), GRID_W - KC) for j in range(NCB)]
BIAS_TYPE = [0, 1, 1, 2]
TYPE_BLOCK = [0, 1, 3]
TYPE_OFF = [KC0[j] - j * QC for j in TYPE_BLOCK]
BR, BC = 16, 48
WINDOW = 128
NB = KR * KC
SW = PAST + NB
PAIRS = 4
EPS = 1e-6
QSCALE = -(HD ** -0.5)
BIG = 1e30
VH = 10
UNIT = 320
UNITS = TOK // UNIT
GROUPS = [(0, 512), (512, 512), (1024, 256)]
GATE_BLOCKS = 24
GPP = 3
STEPS = 10
CHUNKS = [1, 1] + [4] * 8
CHUNK0 = [sum(CHUNKS[:s]) for s in range(STEPS)]
NCHUNK = sum(CHUNKS)


def split_mm(eng, out, lhs, rhs, n_k, begun=None):
    for k in range(n_k):
        for i, (a, b) in enumerate(((0, 0), (0, 1), (1, 0))):
            mm = eng.matmul(out, lhs(a, k), rhs(b, k), start=(k == 0 and i == 0), stop=(k == n_k - 1 and i == 2))
            if begun is not None and k == 0 and i == 0:
                mm.then_inc(begun, 1)
    return mm


def split(eng, hi, lo, src, one, hi_sem, hi_value, lo_sem):
    eng.tensor_tensor(hi, src, one[:, :].to_broadcast(list(src.shape)), ALU.mult).then_inc(hi_sem, 1)
    eng.wait_ge(hi_sem, hi_value)
    eng.tensor_tensor(lo, src, hi.bitcast(F32), ALU.subtract).then_inc(lo_sem, 1)


def startup(nc, io, hm, ident, wv, wkb):
    with ExitStack() as ctx:
        def sb(name, shape, dt=F32):
            return ctx.enter_context(nc.sbuf_tensor(name, shape, dt))

        def ps(name, shape):
            return ctx.enter_context(nc.psum_tensor(name, shape, F32))

        def sem(name):
            return nc.alloc_semaphore(name=name)

        XG = [(0, 4), (4, 4), (8, 2)]
        x = sb("x", [P, 2, 4, D])
        wada = sb("wada", [P, 4, D])
        vraw = sb("vraw", [P, 2, VH * HD])
        kraw = sb("kraw", [P, D])
        h32 = sb("h32", [P, 2, 512])
        modrow = sb("modrow", [2, 2 * D])
        ccol = sb("ccol", [P, KD, 2])
        scol = sb("scol", [P, KD, 2])
        bcol = sb("bcol", [P, 2 * KD])
        modc = sb("modc", [P, 2 * KD, 2])
        modf = sb("modf", [P, 2 * KD, 2])
        ss = sb("ss", [P, 12])
        rms = sb("rms", [P, 12])
        rstd = sb("rstd", [P, 12])
        epsc = sb("epsc", [P, 1])
        one = sb("one", [P, 1])
        mod_ps = ps("mod_ps", [P, 4, 512])
        t_ps = ps("t_ps", [P, 2, 512])
        junk = ps("junk", [P, D])

        small_in, ident_in, kraw_in, eps_set = sem("small_in"), sem("ident_in"), sem("kraw_in"), sem("eps_set")
        x_in = [sem(f"x_in{g}") for g in range(3)]
        wada_in = [sem(f"wada_in{i}") for i in range(4)]
        vraw_in = [sem(f"vraw_in{i}") for i in range(2)]
        silu_done, wada_used, mod_row, mod_t, mod_c, mod_ready = (
            sem(n) for n in ("silu_done", "wada_used", "mod_row", "mod_t", "mod_c", "mod_ready"))
        sq_done, rms_done, rstd_done, xn_done, xt_done = (
            sem(n) for n in ("sq_done", "rms_done", "rstd_done", "xn_done", "xt_done"))
        h_done, hi_done, lo_done, v_hi, v_lo, k_hi, k_lo = (
            sem(n) for n in ("h_done", "hi_done", "lo_done", "v_hi", "v_lo", "k_hi", "k_lo"))

        block = ctx.enter_context(nc.Block())
        chunks = [(g, k) for g in range(3) for k in range(KD)]

        @block.sync
        def _(sp):
            def load_x(g):
                t0, n = XG[g]
                if g == 2:
                    sp.wait_ge(xt_done, KD)
                sp.dma_start(x[:, g % 2, 0:n, :], io["x"][t0 * P:(t0 + n) * P, :].rearrange("(t p) d -> p t d", p=P)
                             ).then_inc(x_in[g], 16)

            def load_wada(i):
                if i >= 4:
                    sp.wait_ge(wada_used, i - 3)
                k, half = i // 2, i % 2
                sp.dma_start(wada[:, i % 4, :], io["w_ada"][k * P:(k + 1) * P, half * D:(half + 1) * D]
                             ).then_inc(wada_in[i % 4], 16)

            sp.dma_start(ccol[:, :, :], io["c_col"]).then_inc(small_in, 16)
            sp.dma_start(bcol[:, :], io["b_col"]).then_inc(small_in, 16)
            sp.dma_start(ident[:, :], io["ident"]).then_inc(ident_in, 16)
            load_x(0)
            for i in range(2 * KD):
                load_wada(i)
                if i == 7:
                    load_x(1)
            for k in range(KD):
                if k >= 2:
                    sp.wait_ge(v_lo, k - 1)
                sp.dma_start(vraw[:, k % 2, :], io["w_v"][:, k, :]).then_inc(vraw_in[k % 2], 16)
            sp.dma_start(kraw[:, :], io["w_kb"]).then_inc(kraw_in, 16)
            load_x(2)

        @block.gpsimd
        def _(pool):
            pool.memset(epsc[:, :], EPS).then_inc(eps_set, 1)
            pool.memset(one[:, :], 1.0).then_inc(eps_set, 1)
            pool.wait_ge(eps_set, 2)
            for k in range(KD):
                pool.wait_ge(vraw_in[k % 2], 16 * (k // 2 + 1))
                split(pool, wv[:, 0, k, :], wv[:, 1, k, :], vraw[:, k % 2, :], one, v_hi, k + 1, v_lo)
            pool.wait_ge(kraw_in, 16)
            split(pool, wkb[:, 0, :], wkb[:, 1, :], kraw[:, :], one, k_hi, 1, k_lo)

        @block.scalar
        def _(act):
            act.wait_ge(small_in, 32)
            act.activation(scol[:, :, :], ccol[:, :, :], ACT.Silu).then_inc(silu_done, 1)
            act.wait_ge(eps_set, 1)

            def norms(g):
                t0, n = XG[g]
                act.wait_ge(x_in[g], 16)
                for t in range(n):
                    if t0 + t > 0:
                        act.wait_ge(sq_done, t0 + t)
                    act.activation(junk[:, :], x[:, g % 2, t, :], ACT.Square, accum_out=ss[:, t0 + t:t0 + t + 1]
                                   ).then_inc(sq_done, 1)
                act.wait_ge(sq_done, t0 + n)
                act.activation(rms[:, t0:t0 + n], ss[:, t0:t0 + n], ACT.Sqrt, bias=epsc[:, 0:1], scale=1.0 / D
                               ).then_inc(rms_done, 1)

            norms(0)
            norms(1)
            act.wait_ge(mod_ready, 1)
            for i, (g, k) in enumerate(chunks):
                if i == KD + 2:
                    norms(2)
                n, stream = XG[g][1] * P, int(g == 2)
                act.wait_ge(xt_done, i + 1)
                if i >= 2:
                    act.wait_ge(lo_done, i - 1)
                act.activation(h32[:, i % 2, 0:n], t_ps[:, i % 2, 0:n], ACT.Identity,
                               bias=modf[:, k, stream:stream + 1], scale=modf[:, KD + k, stream:stream + 1]
                               ).then_inc(h_done, 1)

        @block.tensor
        def _(pe):
            pe.wait_ge(silu_done, 1)
            for i in range(2 * KD):
                k, half = i // 2, i % 2
                pe.wait_ge(wada_in[i % 4], 16 * (i // 4 + 1))
                for c in range(2):
                    mm = pe.matmul(mod_ps[0:2, 2 * half + c, :], scol[:, k, :], wada[:, i % 4, c * 512:(c + 1) * 512],
                                   start=(k == 0), stop=(k == KD - 1))
                mm.then_inc(wada_used, 1)
            pe.wait_ge(ident_in, 16)
            pe.wait_ge(mod_row, 1)
            for b in range(2 * KD):
                mm = pe.transpose(mod_ps[:, 0, 2 * b:2 * b + 2], modrow[0:2, b * P:(b + 1) * P], ident[0:2, 0:2])
            mm.then_inc(mod_t, 1)
            for i, (g, k) in enumerate(chunks):
                pe.wait_ge(xn_done, XG[g][0] + XG[g][1])
                if i >= 2:
                    pe.wait_ge(h_done, i - 1)
                for t in range(XG[g][1]):
                    mm = pe.transpose(t_ps[:, i % 2, t * P:(t + 1) * P], x[:, g % 2, t, k * P:(k + 1) * P], ident[:, :])
                mm.then_inc(xt_done, 1)

        @block.vector
        def _(dve):
            def normalise(g):
                t0, n = XG[g]
                dve.wait_ge(rms_done, g + 1)
                dve.reciprocal(rstd[:, t0:t0 + n], rms[:, t0:t0 + n]).then_inc(rstd_done, 1)
                dve.wait_ge(rstd_done, g + 1)
                for t in range(n):
                    dve.tensor_scalar(x[:, g % 2, t, :], x[:, g % 2, t, :], rstd[:, t0 + t:t0 + t + 1], None, ALU.mult
                                      ).then_inc(xn_done, 1)

            normalise(0)
            normalise(1)
            dve.wait_ge(wada_used, 2 * KD)
            dve.tensor_copy(modrow[:, :], mod_ps[0:2, :, :].rearrange("p a b -> p (a b)")).then_inc(mod_row, 1)
            dve.wait_ge(mod_t, 1)
            dve.wait_ge(small_in, 32)
            for s in range(2):
                dve.tensor_tensor(modc[:, :, s], mod_ps[:, 0, 0:4 * KD].rearrange("p (b s) -> p b s", s=2)[:, :, s],
                                  bcol[:, :], ALU.add).then_inc(mod_c, 1)
            dve.wait_ge(mod_c, 2)
            dve.tensor_copy(modf[:, 0:KD, :], modc[:, 0:KD, :]).then_inc(mod_c, 1)
            dve.tensor_scalar(modf[:, KD:, :], modc[:, KD:, :], 1.0, None, ALU.add).then_inc(mod_ready, 1)
            for i, (g, k) in enumerate(chunks):
                if i == KD + 2:
                    normalise(2)
                t0, n = XG[g][0] * P, XG[g][1] * P
                dve.wait_ge(h_done, i + 1)
                dve.tensor_copy(hm[:, 0, k, t0:t0 + n], h32[:, i % 2, 0:n]).then_inc(hi_done, 1)
                dve.wait_ge(hi_done, i + 1)
                dve.tensor_tensor(hm[:, 1, k, t0:t0 + n], h32[:, i % 2, 0:n], hm[:, 0, k, t0:t0 + n].bitcast(F32),
                                  ALU.subtract).then_inc(lo_done, 1)


SWAP16 = [(i + 16) % 32 for i in range(32)]


def values(nc, io, hm, wv, wkb):
    with ExitStack() as ctx:
        def sb(name, shape, dt=F32):
            return ctx.enter_context(nc.sbuf_tensor(name, shape, dt))

        def ps(name, shape):
            return ctx.enter_context(nc.psum_tensor(name, shape, F32))

        def sem(name):
            return nc.alloc_semaphore(name=name)

        vst = sb("vst", [P, 2, VH, 2 * HD], F32R)
        vout = sb("vout", [P, 2, VH * HD])
        kst = sb("kst", [P, 2, TOK], F32R)
        kout = sb("kout", [P, PROMPT])
        cos, sin = sb("cos_v", [P, LAT]), sb("sin_v", [P, LAT])
        raw, swp, rot = sb("raw_v", [P, 512]), sb("swp_v", [P, 512]), sb("rot_v", [P, 512])
        wgate = sb("wgate", [P, 2, D])
        gcc, gsc = sb("gcc", [P, KD, 2]), sb("gsc", [P, KD, 2])
        gb, grow = sb("gb", [2, D]), sb("grow", [2, D])
        v_ps = ps("v_ps", [P, 4, 512])
        g_ps = ps("g_ps", [P, 2, 512])

        small_in, table_in, silu_done = sem("v_small_in"), sem("v_table_in"), sem("v_silu")
        wg_in = [sem(f"wg_in{i}") for i in range(2)]
        wg_used, g_row, g_out = sem("wg_used"), sem("g_row"), sem("g_out")
        mm_done, v_hi, v_lo, v_copy = sem("v_mm"), sem("v_hi2"), sem("v_lo2"), sem("v_copy")
        v_out = [sem(f"v_out{i}") for i in range(2)]
        vo_out = sem("vo_out")
        k_raw, k_swp, k_cos, k_sin, k_rot, k_hi, k_lo, k_copy, k_out = (
            sem(n) for n in ("k_raw", "k_swp", "k_cos", "k_sin", "k_rot", "kv_hi", "kv_lo", "k_copy", "k_out"))
        block = ctx.enter_context(nc.Block())
        TT = TOK // P
        NU = 2 * TT
        HW = VH * HD // 2

        @block.sync
        def _(sp):
            sp.dma_start(gcc[:, :, :], io["c_col"]).then_inc(small_in, 16)
            sp.dma_start(gb[:, :], io["b_gate"].to_broadcast([2, D])).then_inc(small_in, 16)
            sp.dma_start(cos[:, :], io["cos"]).then_inc(table_in, 16)
            sp.dma_start(sin[:, :], io["sin"]).then_inc(table_in, 16)

            def load_gate_weights(k):
                sp.dma_start(wgate[:, k % 2, :], io["w_ada"][k * P:(k + 1) * P, 2 * D:3 * D]).then_inc(wg_in[k % 2], 16)

            load_gate_weights(0)
            load_gate_weights(1)
            for t in range(TT):
                sp.wait_ge(v_lo, 2 * t + 2)
                sp.dma_start(io["v_d"][t * P:(t + 1) * P, :], vst[:, t % 2, :, :].rearrange("p h c -> p (h c)").bitcast(F32)
                             ).then_inc(v_out[t % 2], 16)
                if 2 <= t < KD:
                    sp.wait_ge(wg_used, t - 1)
                    load_gate_weights(t)
                if t * P >= LAT:
                    s = t - LAT // P
                    sp.wait_ge(v_copy, 2 * s + 2)
                    sp.dma_start(io["new_av"][s * P:(s + 1) * P, :], vout[:, s, 0:8 * HD]).then_inc(vo_out, 16)
                    sp.dma_start(io["new_bv"][s * P:(s + 1) * P, :], vout[:, s, 8 * HD:]).then_inc(vo_out, 16)
            sp.wait_ge(g_row, 1)
            sp.dma_start(io["gate_d"], grow[:, :]).then_inc(g_out, 16)
            sp.wait_ge(k_copy, 1)
            sp.dma_start(io["new_bk"], kout[:, :]).then_inc(k_out, 16)
            sp.wait_ge(k_lo, 3)
            for part in range(2):
                for kv in range(2):
                    sp.dma_start(io["kb_d"][kv, part], kst[kv * HD:(kv + 1) * HD, part, :].bitcast(F32)).then_inc(k_out, 16)
            sp.wait_ge(v_out[0], 16 * (TT // 2))
            sp.wait_ge(v_out[1], 16 * (TT // 2))
            sp.wait_ge(vo_out, 64)
            sp.wait_ge(g_out, 16)
            sp.wait_ge(k_out, 80)

        @block.tensor
        def _(pe):
            for u in range(NU):
                t, n = u // 2, u % 2
                if u >= 4:
                    pe.wait_ge(v_lo, u - 3)
                split_mm(pe, v_ps[:, u % 4, 0:HW], lambda a, k: hm[:, a, k, t * P:(t + 1) * P],
                         lambda b, k: wv[:, b, k, n * HW:(n + 1) * HW], KD).then_inc(mm_done, 1)
                if n == 0 and 2 <= t < KD + 2:
                    k = t - 2
                    if k == 0:
                        pe.wait_ge(silu_done, 1)
                    pe.wait_ge(wg_in[k % 2], 16 * (k // 2 + 1))
                    for c in range(2):
                        mm = pe.matmul(g_ps[0:2, c, :], gsc[:, k, :], wgate[:, k % 2, c * 512:(c + 1) * 512],
                                       start=(k == 0), stop=(k == KD - 1))
                    mm.then_inc(wg_used, 1)
            for g, (t0, n) in enumerate(GROUPS):
                u = NU + g
                pe.wait_ge(v_lo, u - 3)
                split_mm(pe, v_ps[:, u % 4, 0:n], lambda a, k: wkb[:, a, k * P:(k + 1) * P],
                         lambda b, k: hm[:, b, k, t0:t0 + n], KD).then_inc(mm_done, 1)

        @block.scalar
        def _(act):
            act.wait_ge(small_in, 32)
            act.activation(gsc[:, :, :], gcc[:, :, :], ACT.Silu).then_inc(silu_done, 1)
            for u in range(NU):
                t, n = u // 2, u % 2
                act.wait_ge(mm_done, u + 1)
                if t >= 2 and n == 0:
                    act.wait_ge(v_out[t % 2], 16 * (t // 2))
                if t * P >= LAT:
                    act.activation(vout[:, t - LAT // P, n * HW:(n + 1) * HW], v_ps[:, u % 4, 0:HW], ACT.Copy
                                   ).then_inc(v_copy, 1)
                act.activation(vst[:, t % 2, 5 * n:5 * n + 5, 0:HD],
                               v_ps[:, u % 4, 0:HW].rearrange("p (h c) -> p h c", c=HD), ACT.Copy).then_inc(v_hi, 1)
            for g, (t0, n) in enumerate(GROUPS):
                act.wait_ge(mm_done, NU + g + 1)
                if g == 1:
                    act.wait_ge(k_lo, 1)
                if g == 2:
                    act.wait_ge(k_lo, 2)
                act.activation((rot if g == 2 else raw)[:, 0:n], v_ps[:, (NU + g) % 4, 0:n], ACT.Copy).then_inc(k_raw, 1)

        @block.gpsimd
        def _(pool):
            pool.wait_ge(table_in, 32)
            for g, (t0, n) in enumerate(GROUPS[:2]):
                pool.wait_ge(k_swp, g + 1)
                pool.tensor_tensor(swp[:, :], swp[:, :], sin[:, t0:t0 + n], ALU.mult).then_inc(k_sin, 1)

        @block.vector
        def _(dve):
            for u in range(NU):
                t, n = u // 2, u % 2
                hi = vst[:, t % 2, 5 * n:5 * n + 5, 0:HD]
                dve.wait_ge(v_hi, u + 1)
                dve.tensor_tensor(vst[:, t % 2, 5 * n:5 * n + 5, HD:],
                                  v_ps[:, u % 4, 0:HW].rearrange("p (h c) -> p h c", c=HD), hi.bitcast(F32),
                                  ALU.subtract).then_inc(v_lo, 1)
            dve.wait_ge(table_in, 32)
            for g, (t0, n) in enumerate(GROUPS):
                dve.wait_ge(k_raw, g + 1)
                if g < 2:
                    dve.tensor_tensor(rot[:, :], raw[:, :], cos[:, t0:t0 + n], ALU.mult).then_inc(k_cos, 1)
                    dve.stream_shuffle(swp[:, :], raw[:, :], SWAP16).then_inc(k_swp, 1)
                    dve.wait_ge(k_sin, g + 1)
                    dve.wait_ge(k_cos, g + 1)
                    dve.tensor_tensor(rot[:, :], rot[:, :], swp[:, :], ALU.add).then_inc(k_rot, 1)
                    dve.wait_ge(k_rot, g + 1)
                else:
                    dve.tensor_copy(kout[:, :], rot[:, 0:n]).then_inc(k_copy, 1)
                dve.tensor_copy(kst[:, 0, t0:t0 + n], rot[:, 0:n]).then_inc(k_hi, 1)
                dve.wait_ge(k_hi, g + 1)
                dve.tensor_tensor(kst[:, 1, t0:t0 + n], rot[:, 0:n], kst[:, 0, t0:t0 + n].bitcast(F32), ALU.subtract
                                  ).then_inc(k_lo, 1)
            dve.wait_ge(small_in, 32)
            dve.wait_ge(wg_used, KD)
            dve.tensor_tensor(grow[:, :], g_ps[0:2, :, :].rearrange("p a b -> p (a b)"), gb[:, :], ALU.add
                              ).then_inc(g_row, 1)


def pairs(nc, io, hm, ident, branch):
    A = branch == "a"
    with ExitStack() as ctx:
        def sb(name, shape, dt=F32):
            return ctx.enter_context(nc.sbuf_tensor(f"{name}_{branch}", shape, dt))

        def ps(name, shape):
            return ctx.enter_context(nc.psum_tensor(f"{name}_{branch}", shape, F32))

        def sem(name):
            return nc.alloc_semaphore(name=f"{name}_{branch}")

        w = sb("w", [P, 3, 2, D], F32R)
        wraw = sb("wraw", [P, D])
        craw = sb("craw", [P, D])
        q1 = sb("q1", [P, 2, TOK], F32R)
        q2 = sb("q2", [P, TOK], F32R)
        kk = sb("kk", [P, 2, TOK], F32R)
        kc = sb("kc", [P, 2, PAST], F32R)
        CH = 2 if A else 1
        vc = sb("vc", [P, PAST // P, CH, 2 * HD], F32R)
        vw = sb("vw", [P, 16 if A else 8, CH * 2 * HD], F32R)
        vp = sb("vp", [P, 2, CH * 2 * HD], F32R)
        pr = sb("pr", [P, 2, NB + PAST + NB])
        pt = sb("pt", [P, 2, 14 * P], F32R)
        ost = sb("ost", [P, TOK])
        gst = sb("gst", [P, 2, UNIT])
        otmp = sb("otmp", [HD, 2 * P])
        one, qscale = sb("one", [P, 1]), sb("qscale", [P, 1])
        mn = sb("mn", [P, 2])
        nm = sb("nm", [P, 2])
        mx = sb("mx", [P, 2])
        den = sb("den", [P, 2])
        rden = sb("rden", [P, 2])
        if A:
            rb = sb("rb", [P, BR, BC])
            comb = sb("comb", [P, 2, 2, NB])
            rowm = sb("rowm", [P, 2, KR])
            colm = sb("colm", [P, 3, KC])
            kout = sb("kout", [P, PROMPT])
        else:
            band = sb("band", [P, 3, NB])
            cos, sin = sb("cos", [P, LAT]), sb("sin", [P, LAT])
            raw, swp, rot = sb("raw", [P, 512]), sb("swp", [P, 512]), sb("rot", [P, 512])
            sink = sb("sink", [P, 8])
            nsink = sb("nsink", [P, 8])
            nsk = sb("nsk", [P, 2])
            esk = sb("esk", [P, 2])
            den2 = sb("den2", [P, 2])
        s_ps = ps("s_ps", [P, 4, 512])
        t_ps = ps("t_ps", [P, 2, 512])
        o_ps = ps("o_ps", [P, 512])
        d_ps = ps("d_ps", [P, 512])

        PROJ = 2 if A else 1
        TILES = PROJ + GPP
        SLOT = [0, 1, 2, 0, 1] if A else [0, 1, 2, 1]
        NG = PROJ * 3

        def slot_free(i):
            last = max([k for k in range(i) if SLOT[k] == SLOT[i]] or
                       [k - TILES for k in range(TILES) if SLOT[k] == SLOT[i]])
            return max(last + 2, 0)

        w_in, q_in = sem("w_in"), sem("q_in")
        craw_in, w_hi, w_lo = sem("craw_in"), sem("w_hi"), sem("w_lo")
        w_begun, w_scaled = sem("w_begun"), sem("w_scaled")
        c_split = sem("c_split")
        const_in, vw_in, kk_in = sem("const_in"), sem("vw_in"), sem("kk_in")
        rb_in, comb_t, comb_done = sem("rb_in"), sem("comb_t"), sem("comb_done")
        ckh, cvh = sem("ckh"), sem("cvh")
        proj_done, xa, xd, x_used = sem("proj_done"), sem("xa"), sem("xd"), sem("x_used")
        ko_done, ko_out = sem("ko_done"), sem("ko_out")
        s_done, m1_done, m2_done, m3_done, m_done, exp_done = (
            sem(n) for n in ("s_done", "m1_done", "m2_done", "m3_done", "m_done", "exp_done"))
        esk_done, den_done, r_done, p_done = sem("esk_done"), sem("den_done"), sem("r_done"), sem("p_done")
        t_done, hi_done, lo_done, pva_done, pvb_done, ot_done, o_done = (
            sem(n) for n in ("t_done", "hi_done", "lo_done", "pva_done", "pvb_done", "ot_done", "o_done"))
        d_done, g_done = sem("d_done"), sem("g_done")
        g_out = [sem("g_out0"), sem("g_out1")]
        o_out = sem("o_out")
        r_raw, r_swp, r_cos, r_sin, r_rot = (sem(n) for n in ("r_raw", "r_swp", "r_cos", "r_sin", "r_rot"))
        nsk_done, ones_set = sem("nsk_done"), sem("ones_set")

        block = ctx.enter_context(nc.Block())
        base = 0 if A else PAIRS

        def grid(ap, r0, nr, c0, ncol):
            return ap[..., 0:LAT].rearrange("p (r c) -> p r c", c=GRID_W)[:, r0:r0 + nr, c0:c0 + ncol]

        def rows(ap):
            return ap.rearrange("p (r j c) -> p r j c", r=QR, c=QC) if ap.shape[-1] == 512 else ap

        def tiled(ap):
            return ap.rearrange("p (j r c) -> p r j c", r=QR, c=QC) if ap.shape[-1] == 512 else ap

        def near_bank(s, t):
            return s_ps[:, 2 * t, PAST - NB:PAST] if s % 2 else s_ps[:, 2 * t + 1, 0:NB]

        def scores_run(s, t):
            both = s_ps[:, 2 * t:2 * t + 2, :].rearrange("p a b -> p (a b)")
            return both[:, 0:PROMPT] if s < 2 else both[:, PAST - NB:] if s % 2 else both[:, 0:SW]

        def probs_run(s, t):
            return pr[:, t, NB:NB + PROMPT] if s < 2 else pr[:, t, 0:SW] if s % 2 else pr[:, t, NB:]

        def probs_block(s, t, kb):
            c0 = NB + kb * P if kb < 4 or s % 2 == 0 else (kb - 4) * P
            return pr[:, t, c0:c0 + P]

        def chunk_blocks(s):
            if s < 2:
                return [[(0, 0), (0, 1), (1, 0), (1, 1)]]
            if A:
                near = [(4, 0), (5, 0), (4, 1), (6, 0), (5, 1), (6, 1)]
            else:
                near = [(kb, t) for kb in (4, 5, 6) for t in (0, 1)]
            ctx_ = [(kb, t) for kb in range(4) for t in (0, 1)]
            return [ctx_[0:4], ctx_[4:8], near[0:4], near[4:6]]

        @block.sync
        def _(sp):
            if A:
                sp.dma_start(rowm[:, :, :], io["rowmask"]).then_inc(const_in, 16)
                sp.dma_start(colm[:, :, :], io["colmask"]).then_inc(const_in, 16)
            else:
                sp.dma_start(band[:, :, :], io["band"]).then_inc(const_in, 16)
                sp.dma_start(cos[:, :], io["cos"]).then_inc(const_in, 16)
                sp.dma_start(sin[:, :], io["sin"]).then_inc(const_in, 16)
                sp.dma_start(sink[:, :], io["sink"].to_broadcast([P, 8])).then_inc(const_in, 16)
            with sp.Fori(0, PAIRS) as p:
                def load_tile(i):
                    if i < PROJ:
                        src = io["w_k" + branch][p]
                    else:
                        src = io["w_gate"][(p + base) * GPP + (i - PROJ)]
                    sp.wait_ge(w_lo, p * TILES + i)
                    sp.dma_start(wraw[:, :], src).then_inc(w_in, 16)

                sp.wait_ge(c_split, p * 3)
                sp.dma_start(craw[:, :], io["w_q" + branch][p]).then_inc(q_in, 16)
                sp.wait_ge(w_lo, p * TILES + 1)
                sp.dma_start(craw[:, 0:PAST], io["ck" + branch][p]).then_inc(craw_in, 16)
                sp.dma_start(craw[:, PAST:PAST + 4 * CH * HD], io["cv" + branch][p]).then_inc(craw_in, 16)
                if A:
                    load_tile(1)
                sp.wait_ge(pvb_done, p * (STEPS - 2))
                if A:
                    for rg in range(4):
                        for j in range(NCB):
                            v = io["v_d"][0:LAT, :].rearrange("(r c) n -> r c n", c=GRID_W)
                            sp.dma_start(vw[:, rg * NCB + j, :].bitcast(F32),
                                         v[4 * rg:4 * rg + 4, KC0[j]:KC0[j] + KC, bass.ds(p * 256, 256)]
                                         ).then_inc(vw_in, 16)
                    sp.dma_start(vp[:, :, :].bitcast(F32),
                                 io["v_d"][LAT:TOK, bass.ds(p * 256, 256)].rearrange("(t p) n -> p t n", p=P)
                                 ).then_inc(vw_in, 16)
                else:
                    kv = p // 2
                    v = io["v_d"][:, bass.ds(kv * 128 + 1024, 128)]
                    sp.dma_start(vw[:, :, :].bitcast(F32), v[0:LAT, :].rearrange("(t p) n -> p t n", p=P)).then_inc(vw_in, 16)
                    sp.dma_start(vp[:, :, :].bitcast(F32), v[LAT:TOK, :].rearrange("(t p) n -> p t n", p=P)).then_inc(vw_in, 16)
                    sp.wait_ge(exp_done, p * 2 * STEPS)
                    for h in range(2):
                        for part in range(2):
                            r0 = HD * ((h + part) % 2)
                            sp.dma_start(kk[r0:r0 + HD, h, :].bitcast(F32), io["kb_d"][kv, part]).then_inc(kk_in, 16)
                if A:
                    sp.wait_ge(comb_done, p * 12)
                    sp.dma_start(rb[:, :, :], io["bias"][p * 2]).then_inc(rb_in, 16)
                for i in range(PROJ, TILES):
                    load_tile(i)
                if A:
                    sp.wait_ge(comb_done, p * 12 + 6)
                    sp.dma_start(rb[:, :, :], io["bias"][p * 2 + 1]).then_inc(rb_in, 16)

        @block.gpsimd
        def _(pool):
            pool.memset(one[:, :], 1.0).then_inc(ones_set, 1)
            pool.memset(qscale[:, :], QSCALE).then_inc(ones_set, 1)
            pool.wait_ge(ones_set, 2)
            pool.wait_ge(const_in, 32 if A else 64)
            with pool.Fori(0, PAIRS) as p:
                def split_tile(i):
                    slot = SLOT[i]
                    if i > 0:
                        raw_w = wraw[:, :]
                        pool.wait_ge(w_in, (p * (TILES - 1) + i) * 16)
                    else:
                        raw_w = craw[:, :]
                        pool.wait_ge(q_in, (p + 1) * 16)
                        pool.tensor_tensor(raw_w, raw_w, qscale[:, :].to_broadcast([P, D]), ALU.mult
                                           ).then_inc(w_scaled, 1)
                        pool.wait_ge(w_scaled, p + 1)
                    pool.wait_ge(w_begun, p * TILES + slot_free(i))
                    split(pool, w[:, slot, 0, :], w[:, slot, 1, :], raw_w, one, w_hi, p * TILES + i + 1, w_lo)

                def bias(h, ty):
                    n = 3 * h + ty
                    if ty == 0:
                        pool.wait_ge(rb_in, (p * 2 + h + 1) * 16)
                    if n >= 2:
                        pool.wait_ge(m_done, p * 2 * STEPS + 4 + [2, 6, 8, 10][n - 2])
                    for t in range(2):
                        b = rb[:, (4 if t == 0 else 0):(4 if t == 0 else 0) + KR, TYPE_OFF[ty] + 16:TYPE_OFF[ty] + 16 + KC]
                        c = comb[:, n % 2, t, :].rearrange("p (r c) -> p r c", c=KC)
                        rm = rowm[:, t, :].rearrange("p (r o) -> p r o", o=1).to_broadcast([P, KR, KC])
                        cm = colm[:, ty:ty + 1, :].to_broadcast([P, KR, KC])
                        pool.tensor_tensor(c, rm, b, ALU.subtract).then_inc(comb_t, 1)
                        pool.wait_ge(comb_t, p * 12 + 2 * n + t + 1)
                        pool.tensor_tensor(c, c, cm, ALU.add).then_inc(comb_done, 1)

                for i in range(PROJ):
                    split_tile(i)
                if A:
                    pool.wait_ge(m_done, p * 2 * STEPS)
                    bias(0, 0)
                    bias(0, 1)
                    split_tile(2)
                    split_tile(3)
                    bias(0, 2)
                    bias(1, 0)
                    bias(1, 1)
                    split_tile(4)
                    bias(1, 2)
                else:
                    for g in range(2):
                        pool.wait_ge(r_swp, p * 2 + g + 1)
                        pool.tensor_tensor(swp[:, :], swp[:, :], sin[:, g * 512:(g + 1) * 512], ALU.mult).then_inc(r_sin, 1)
                    for i in range(PROJ, TILES):
                        split_tile(i)

        @block.tensor
        def _(pe):
            with pe.Fori(0, PAIRS) as p:
                pe.wait_ge(exp_done, p * 2 * STEPS)
                for n in range(NG):
                    i, (t0, tn) = n // 3, GROUPS[n % 3]
                    if n % 3 == 0:
                        pe.wait_ge(w_lo, p * TILES + i + 1)
                    if n >= 4:
                        pe.wait_ge(x_used, p * NG + n - 3)
                    mm = split_mm(pe, s_ps[:, n % 4, 0:tn], lambda a, k: w[:, SLOT[i], a, k * P:(k + 1) * P],
                                  lambda b, k: hm[:, b, k, t0:t0 + tn], KD, w_begun if n % 3 == 0 else None)
                    mm.then_inc(proj_done, 1)

                def unit(u):
                    i, t0 = PROJ + u // UNITS, (u % UNITS) * UNIT
                    if u % UNITS == 0:
                        pe.wait_ge(w_lo, p * TILES + i + 1)
                    pe.wait_ge(g_done, p * GPP * UNITS + u)
                    mm = split_mm(pe, d_ps[:, 0:UNIT], lambda a, k: w[:, SLOT[i], a, k * P:(k + 1) * P],
                                  lambda b, k: hm[:, b, k, t0:t0 + UNIT], KD, w_begun if u % UNITS == 0 else None)
                    mm.then_inc(d_done, 1)

                def score(s, t, out, rhs):
                    if s < 2:
                        h, cols = s, lambda ap: ap[..., LAT + t * P:LAT + (t + 1) * P]
                    elif A:
                        h, cols = (s - 2) // 4, lambda ap: ap[..., (4 * t + (s - 2) % 4) * P:(4 * t + (s - 2) % 4 + 1) * P]
                    else:
                        h, cols = t, lambda ap: ap[..., (s - 2) * P:(s - 1) * P]
                    r0 = HD * h
                    pe.matmul(out, cols(q1[:, h, :]), rhs(h, slice(0, P)), start=True, stop=False)
                    return pe.matmul(out, cols(q2[r0:r0 + HD, :]), rhs(h, slice(r0, r0 + HD)), start=False, stop=True)

                def scores(s):
                    if s == 0:
                        pe.wait_ge(x_used, p * NG + NG)
                        pe.wait_ge(c_split, p * 3 + 3)
                        if not A:
                            pe.wait_ge(kk_in, (p + 1) * 64)
                    else:
                        pe.wait_ge(exp_done, p * 2 * STEPS + 2 * s)
                    for t in range(2):
                        if s < 2:
                            mm = score(s, t, s_ps[:, 2 * t, 0:PROMPT], lambda h, r: kk[r, h, LAT:TOK])
                            continue
                        score(s, t, s_ps[:, 2 * t + s % 2, :], lambda h, r: kc[r, h, :])
                        if A:
                            j = (s - 2) % 4
                            mm = score(s, t, near_bank(s, t),
                                       lambda h, r: grid(kk[r, h, :], 4 * t, KR, KC0[j], KC))
                        else:
                            w0 = min(max(s - 3, 0), 5) * P
                            mm = score(s, t, near_bank(s, t), lambda h, r: kk[r, h, w0:w0 + NB])
                    mm.then_inc(s_done, 1)

                def transposes(s, c):
                    n = CHUNK0[s] + c
                    if c == 0:
                        pe.wait_ge(p_done, p * 2 * STEPS + 2 * s + 2)
                    if n >= 2:
                        pe.wait_ge(lo_done, p * NCHUNK + n - 1)
                    for b, (kb, t) in enumerate(chunk_blocks(s)[c]):
                        mm = pe.transpose(t_ps[:, n % 2, b * P:(b + 1) * P], probs_block(s, t, kb), ident[:, :])
                    mm.then_inc(t_done, 1)

                def weighted(s, half):
                    if s == 0:
                        pe.wait_ge(vw_in, (p + 1) * 16 * (17 if A else 2))
                    last_chunk = CHUNKS[s] if half or s < 2 else 2
                    pe.wait_ge(lo_done, p * NCHUNK + CHUNK0[s] + last_chunk)
                    if half == 0:
                        pe.wait_ge(o_done, p * STEPS + s)
                    if s < 2:
                        h = s if A else 0
                        work = [(vp[:, kb, h * P:(h + 1) * P], 2 * kb, 0, 2) for kb in range(2)]
                    elif half == 0:
                        h = (s - 2) // 4 if A else 0
                        work = [(vc[:, kb, h, :], 2 * kb, 0, 2) for kb in range(4)]
                    elif A:
                        h, j = (s - 2) // 4, (s - 2) % 4
                        work = [(vw[:, rg * NCB + j, h * P:(h + 1) * P], b0, c0, nb)
                                for rg, b0, c0, nb in ((0, 8, 0, 1), (1, 9, 0, 2), (2, 11, 0, 2), (3, 13, 1, 1))]
                    else:
                        w0 = min(max(s - 3, 0), 5)
                        work = [(vw[:, w0 + kb, :], 8 + 2 * kb, 0, 2) for kb in range(3)]
                    for n, (v, b0, c0, nb) in enumerate(work):
                        for part in range(2):
                            mm = pe.matmul(o_ps[:, c0 * P:(c0 + nb) * P], v, pt[:, part, b0 * P:(b0 + nb) * P],
                                           start=(half == 0 and n == 0 and part == 0),
                                           stop=((half == 1 or s < 2) and n == len(work) - 1 and part == 1),
                                           skip_group_check=True)
                    mm.then_inc(pvb_done if half else pva_done, 1)

                for s in range(STEPS + 1):
                    if s < STEPS:
                        scores(s)
                    if s >= 4:
                        weighted(s - 2, 1)
                    if s > 0:
                        for c in range(min(2, CHUNKS[s - 1])):
                            transposes(s - 1, c)
                    unit(s)
                    if s > 0:
                        for c in range(2, CHUNKS[s - 1]):
                            transposes(s - 1, c)
                        weighted(s - 1, 0)
                unit(STEPS + 1)
                weighted(STEPS - 1, 1)

        @block.scalar
        def _(act):
            with act.Fori(0, PAIRS) as p:
                act.wait_ge(craw_in, (p + 1) * 32)
                for h in range(2):
                    r0 = HD * h
                    act.activation(kc[r0:r0 + HD, h, :], craw[r0:r0 + HD, 0:PAST], ACT.Copy).then_inc(ckh, 1)
                act.activation(vc[:, :, :, 0:HD],
                               craw[:, PAST:PAST + 4 * CH * HD].rearrange("p (b h c) -> p b h c", h=CH, c=HD),
                               ACT.Copy).then_inc(cvh, 1)
                for n in range(NG):
                    t0, tn = GROUPS[n % 3]
                    tok, bank = slice(t0, t0 + tn), s_ps[:, n % 4, 0:tn]
                    act.wait_ge(proj_done, p * NG + n + 1)
                    if A and n < 3:
                        act.activation(tiled(q1[0:HD, 0, tok]), rows(bank[0:HD, :]), ACT.Copy).then_inc(xa, 1)
                        act.wait_ge(xd, p * 9 + 2 * n + 1)
                        act.activation(tiled(q1[0:HD, 1, tok]), rows(bank[HD:P, :]), ACT.Copy).then_inc(xa, 1)
                    elif A:
                        act.activation(kk[0:HD, 0, tok], bank[0:HD, :], ACT.Copy).then_inc(xa, 1)
                    else:
                        act.wait_ge(x_used, p * NG + n)
                        act.activation((rot if n == 2 else raw)[:, 0:tn], bank, ACT.Copy).then_inc(r_raw, 1)
                        if n < 2:
                            act.wait_ge(r_rot, p * 2 + n + 1)
                        else:
                            act.wait_ge(r_raw, p * 3 + 3)
                        for h in range(2):
                            act.activation(q1[0:HD, h, tok], rot[h * HD:(h + 1) * HD, 0:tn], ACT.Copy
                                           ).then_inc(xa, 1)

                if A:
                    act.wait_ge(ko_done, p + 1)
                    act.dma_start(io["new_ak"][p], kout[:, :]).then_inc(ko_out, 16)

                def high(s, chunks):
                    for c in chunks:
                        n = CHUNK0[s] + c
                        cols = len(chunk_blocks(s)[c]) * P
                        act.wait_ge(t_done, p * NCHUNK + n + 1)
                        if c == 0:
                            act.wait_ge(pva_done, p * STEPS + s)
                        if c == 2:
                            act.wait_ge(pvb_done, p * (STEPS - 2) + s - 2)
                        act.activation(pt[:, 0, c * 512:c * 512 + cols], t_ps[:, n % 2, 0:cols], ACT.Copy
                                       ).then_inc(hi_done, 1)

                def exps(s):
                    for t in range(2):
                        n = p * 2 * STEPS + 2 * s + t + 1
                        act.wait_ge(m_done, n)
                        if t == 0:
                            act.wait_ge(t_done, p * NCHUNK + (CHUNK0[s - 1] + min(2, CHUNKS[s - 1]) if s > 0 else 0))
                            act.wait_ge(r_done, p * STEPS + s)
                        act.activation(probs_run(s, t), scores_run(s, t), ACT.Exp, bias=mx[:, t:t + 1], scale=-1.0,
                                       accum_out=den[:, t:t + 1]).then_inc(exp_done, 1)
                        if not A:
                            h = s if s < 2 else t
                            act.activation(esk[:, t:t + 1], nsk[:, h:h + 1], ACT.Exp, bias=mx[:, t:t + 1], scale=-1.0
                                           ).then_inc(esk_done, 1)

                def gate_out(u):
                    act.wait_ge(g_done, p * GPP * UNITS + u + 1)
                    blk = (p + base) * GPP + u // UNITS
                    act.dma_start(io["gates_d"][blk, :, (u % UNITS) * UNIT:(u % UNITS + 1) * UNIT], gst[:, u % 2, :]
                                  ).then_inc(g_out[u % 2], 16)

                def gate(u):
                    act.wait_ge(d_done, p * GPP * UNITS + u + 1)
                    act.wait_ge(g_out[u % 2], (p * (GPP * UNITS // 2) + u // 2) * 16)
                    act.activation(gst[:, u % 2, :], d_ps[:, 0:UNIT], ACT.Copy).then_inc(g_done, 1)
                    if u > 0:
                        gate_out(u - 1)

                def low_half(s):
                    if s < 2:
                        act.wait_ge(pva_done, p * STEPS + s + 1)
                    else:
                        act.wait_ge(pvb_done, p * (STEPS - 2) + s - 1)
                    act.wait_ge(o_done, p * STEPS + s)
                    act.activation(otmp[:, :], o_ps[HD:P, 0:2 * P], ACT.Copy).then_inc(ot_done, 1)

                for s in range(STEPS + 1):
                    if s >= 2:
                        low_half(s - 2)
                    if s > 0:
                        high(s - 1, range(min(2, CHUNKS[s - 1])))
                    if s < STEPS:
                        exps(s)
                    gate(s)
                    if s > 0:
                        high(s - 1, range(2, CHUNKS[s - 1]))
                gate(STEPS + 1)
                gate_out(STEPS + 1)
                low_half(STEPS - 1)
                act.wait_ge(o_done, (p + 1) * STEPS)
                act.dma_start(io["o_d"][p + base], ost[:, :]).then_inc(o_out, 16)
            act.wait_ge(g_out[0], PAIRS * GPP * UNITS // 2 * 16)
            act.wait_ge(g_out[1], PAIRS * GPP * UNITS // 2 * 16)
            act.wait_ge(o_out, PAIRS * 16)
            if A:
                act.wait_ge(ko_out, PAIRS * 16)

        @block.vector
        def _(dve):
            if not A:
                dve.wait_ge(const_in, 64)
                dve.tensor_scalar(nsink[:, :], sink[:, :], -1.0, None, ALU.mult).then_inc(nsk_done, 1)
                dve.wait_ge(nsk_done, 1)
            with dve.Fori(0, PAIRS) as p:
                if not A:
                    dve.tensor_copy(nsk[:, :], nsink[:, bass.ds(p * 2, 2)]).then_inc(nsk_done, 1)
                for h in range(2):
                    r0, r1 = HD * h, HD * (1 - h)
                    dve.wait_ge(ckh, p * 2 + h + 1)
                    dve.tensor_tensor(kc[r1:r1 + HD, h, :], craw[r0:r0 + HD, 0:PAST],
                                      kc[r0:r0 + HD, h, :].bitcast(F32), ALU.subtract).then_inc(c_split, 1)
                dve.wait_ge(cvh, p + 1)
                dve.tensor_tensor(vc[:, :, :, HD:],
                                  craw[:, PAST:PAST + 4 * CH * HD].rearrange("p (b h c) -> p b h c", h=CH, c=HD),
                                  vc[:, :, :, 0:HD].bitcast(F32), ALU.subtract).then_inc(c_split, 1)
                for n in range(NG):
                    t0, tn = GROUPS[n % 3]
                    tok, bank = slice(t0, t0 + tn), s_ps[:, n % 4, 0:tn]
                    if A:
                        dve.wait_ge(proj_done, p * NG + n + 1)
                    if A and n < 3:
                        dve.tensor_copy(tiled(q1[HD:P, 1, tok]), rows(bank[HD:P, :])).then_inc(xd, 1)
                        dve.wait_ge(xa, p * 9 + 2 * n + 1)
                        dve.tensor_copy(tiled(q1[HD:P, 0, tok]), rows(bank[0:HD, :])).then_inc(xd, 1)
                        dve.tensor_tensor(tiled(q2[0:HD, tok]), rows(bank[0:HD, :]), tiled(q1[0:HD, 0, tok]).bitcast(F32),
                                          ALU.subtract)
                        dve.wait_ge(xa, p * 9 + 2 * n + 2)
                        dve.wait_ge(xd, p * 9 + 2 * n + 1)
                        dve.tensor_tensor(tiled(q2[HD:P, tok]), rows(bank[HD:P, :]), tiled(q1[HD:P, 1, tok]).bitcast(F32),
                                          ALU.subtract).then_inc(x_used, 1)
                    elif A:
                        dve.tensor_copy(kk[HD:P, 1, tok], bank[HD:P, :]).then_inc(xd, 1)
                        dve.wait_ge(xa, p * 9 + n + 4)
                        dve.wait_ge(xd, p * 9 + n + 4)
                        if n == 5:
                            dve.wait_ge(ko_out, p * 16)
                            dve.tensor_copy(kout[:, :], bank).then_inc(ko_done, 1)
                        dve.tensor_tensor(kk[HD:P, 0, tok], bank[0:HD, :], kk[0:HD, 0, tok].bitcast(F32), ALU.subtract)
                        dve.tensor_tensor(kk[0:HD, 1, tok], bank[HD:P, :], kk[HD:P, 1, tok].bitcast(F32), ALU.subtract
                                          ).then_inc(x_used, 1)
                    else:
                        dve.wait_ge(r_raw, p * 3 + n + 1)
                        if n < 2:
                            dve.tensor_tensor(rot[:, :], raw[:, :], cos[:, tok], ALU.mult).then_inc(r_cos, 1)
                            dve.stream_shuffle(swp[:, :], raw[:, :], SWAP16).then_inc(r_swp, 1)
                            dve.wait_ge(r_sin, p * 2 + n + 1)
                            dve.wait_ge(r_cos, p * 2 + n + 1)
                            dve.tensor_tensor(rot[:, :], rot[:, :], swp[:, :], ALU.add).then_inc(r_rot, 1)
                            dve.wait_ge(r_rot, p * 2 + n + 1)
                        for h in range(2):
                            dve.tensor_copy(q1[HD:P, h, tok], rot[h * HD:(h + 1) * HD, 0:tn]).then_inc(xd, 1)
                        dve.wait_ge(xa, p * 6 + 2 * n + 2)
                        dve.wait_ge(xd, p * 6 + 2 * n + 2)
                        for h in range(2):
                            r = slice(h * HD, (h + 1) * HD)
                            last = dve.tensor_tensor(q2[r, tok], rot[r, 0:tn], q1[r, h, tok].bitcast(F32), ALU.subtract)
                        last.then_inc(x_used, 1)

                def low(s, chunks):
                    for c in chunks:
                        n = CHUNK0[s] + c
                        cols = len(chunk_blocks(s)[c]) * P
                        dve.wait_ge(hi_done, p * NCHUNK + n + 1)
                        dve.tensor_tensor(pt[:, 1, c * 512:c * 512 + cols], t_ps[:, n % 2, 0:cols],
                                          pt[:, 0, c * 512:c * 512 + cols].bitcast(F32), ALU.subtract).then_inc(lo_done, 1)

                def minima(s):
                    width = PROMPT if s < 2 else PAST
                    dve.wait_ge(s_done, p * STEPS + s + 1)
                    ctx_min = mx if A and s < 2 else mn
                    if A and s >= 2:
                        h, j = (s - 2) // 4, (s - 2) % 4
                        n = 3 * h + BIAS_TYPE[j]
                        dve.wait_ge(comb_done, p * 12 + 2 * n + 2)
                    red = dve.tensor_reduce(ctx_min[:, :],
                                            s_ps[:, :, :].rearrange("p (t b) c -> p t b c", b=2)[:, :, s % 2 if s >= 2 else 0, 0:width],
                                            AX.X, ALU.min)
                    if A and s < 2:
                        red.then_inc(m_done, 2)
                        return
                    red.then_inc(m1_done, 1)
                    if s >= 2:
                        for t in range(2):
                            near = comb[:, n % 2, t, :] if A else \
                                band[:, 0 if s == 2 else 2 if s == STEPS - 1 else 1, :]
                            bank = near_bank(s, t)
                            red = dve.tensor_tensor_reduce(bank, bank, near, 1.0, BIG, ALU.add, ALU.min, nm[:, t:t + 1])
                        red.then_inc(m2_done, 1)
                    if A:
                        dve.wait_ge(m1_done, p * (STEPS - 2) + s - 1)
                        dve.wait_ge(m2_done, p * (STEPS - 2) + s - 1)
                        dve.tensor_tensor(mx[:, :], mn[:, :], nm[:, :], ALU.min).then_inc(m_done, 2)
                        return
                    dve.wait_ge(m1_done, p * STEPS + s + 1)
                    if s < 2:
                        sk = nsk[:, s:s + 1].to_broadcast([P, 2])
                    else:
                        sk = nsk[:, :]
                        dve.wait_ge(m2_done, p * (STEPS - 2) + s - 1)
                        dve.tensor_tensor(nm[:, :], mn[:, :], nm[:, :], ALU.min).then_inc(m3_done, 1)
                        dve.wait_ge(m3_done, p * (STEPS - 2) + s - 1)
                    if s == 0:
                        dve.wait_ge(nsk_done, p + 2)
                    dve.tensor_tensor(mx[:, :], (mn if s < 2 else nm)[:, :], sk, ALU.min).then_inc(m_done, 2)

                def normalise(s):
                    dve.wait_ge(exp_done, p * 2 * STEPS + 2 * s + 2)
                    if s > 0:
                        dve.wait_ge(p_done, p * 2 * STEPS + 2 * s)
                    if A:
                        dve.reciprocal(rden[:, :], den[:, :]).then_inc(r_done, 1)
                    else:
                        dve.wait_ge(esk_done, p * 2 * STEPS + 2 * s + 2)
                        dve.tensor_tensor(den2[:, :], den[:, :], esk[:, :], ALU.add).then_inc(den_done, 1)
                        dve.wait_ge(den_done, p * STEPS + s + 1)
                        dve.reciprocal(rden[:, :], den2[:, :]).then_inc(r_done, 1)
                    dve.wait_ge(r_done, p * STEPS + s + 1)
                    for t in range(2):
                        dve.tensor_scalar(probs_run(s, t), probs_run(s, t), rden[:, t:t + 1], None, ALU.mult
                                          ).then_inc(p_done, 1)

                def add_halves(s):
                    dve.wait_ge(ot_done, p * STEPS + s + 1)
                    if s == 0:
                        dve.wait_ge(o_out, p * 16)
                    if s < 2:
                        dve.tensor_tensor(ost[HD * s:HD * s + HD, LAT:TOK], o_ps[0:HD, 0:2 * P], otmp[:, :], ALU.add
                                          ).then_inc(o_done, 1)
                    elif A:
                        h, j = (s - 2) // 4, (s - 2) % 4
                        dst = grid(ost[HD * h:HD * h + HD, :], 0, ROWS, QC * j, QC)
                        dve.tensor_tensor(dst, o_ps[0:HD, 0:2 * P].rearrange("p (r c) -> p r c", c=QC),
                                          otmp[:, :].rearrange("p (r c) -> p r c", c=QC), ALU.add).then_inc(o_done, 1)
                    else:
                        for t in range(2):
                            last = dve.tensor_tensor(ost[HD * t:HD * t + HD, (s - 2) * P:(s - 1) * P],
                                                     o_ps[0:HD, t * P:(t + 1) * P], otmp[:, t * P:(t + 1) * P], ALU.add)
                        last.then_inc(o_done, 1)

                for s in range(STEPS + 1):
                    if s < STEPS:
                        minima(s)
                    if s >= 2:
                        add_halves(s - 2)
                    if s > 0:
                        low(s - 1, range(min(2, CHUNKS[s - 1])))
                    if s < STEPS:
                        normalise(s)
                    if s > 0:
                        low(s - 1, range(2, CHUNKS[s - 1]))
                add_halves(STEPS - 1)


def finish(nc, io):
    with ExitStack() as ctx:
        def sb(name, shape, dt=F32):
            return ctx.enter_context(nc.sbuf_tensor(f"{name}_f", shape, dt))

        def sem(name):
            return nc.alloc_semaphore(name=f"{name}_f")

        CT = 256
        CHUNKS_ = TOK // CT
        PIECES = 4
        GSLOTS = 4
        wb = sb("wb", [P, 2, KD, D], F32R)
        wo = sb("wo", [P, 2, KD, D], F32R)
        og = sb("og", [P, 2, KD, CT], F32R)
        oz = sb("oz", [P, 2, 2, 2, CT])
        gt = sb("gt", [P, GSLOTS, 2, CT])
        tp = sb("tp", [P, 2, 2, CT])
        mg = sb("mg", [P, 2, KD, CT], F32R)
        x, y = sb("x", [P, 2, D]), sb("y", [P, 2, D])
        gate, gain = sb("gate", [P, D]), sb("gain", [P, D])
        ss, rms, rstd = sb("ss", [P, 2]), sb("rms", [P, 2]), sb("rstd", [P, 2])
        epsc = sb("eps", [P, 1])
        b_ps = ctx.enter_context(nc.psum_tensor("b_ps", [P, 2, 2, 512], F32))
        y_ps = ctx.enter_context(nc.psum_tensor("y_ps", [P, 2, D], F32))

        w_in = [sem(f"w_in{s}") for s in range(4)]
        w_hi, w_lo_dve, w_lo_pool = sem("w_hi"), sem("w_lo_dve"), sem("w_lo_pool")
        oz_in = [sem("oz_in0"), sem("oz_in1")]
        silu_done, og_prod, og_hi, og_lo = (sem(n) for n in ("silu", "og_prod", "og_hi", "og_lo"))
        gt_in = [sem(f"gt_in{s}") for s in range(GSLOTS)]
        sig_done, b_done, b_prod, summed, mg_hi, mg_lo = (
            sem(n) for n in ("sig", "b_done", "b_prod", "summed", "mg_hi", "mg_lo"))
        x_in, y_out = [sem("x_in0"), sem("x_in1")], [sem("y_out0"), sem("y_out1")]
        gate_in, gain_in, eps_set = sem("gate_in"), sem("gain_in"), sem("eps_set")
        y_mm, gated, res, sq_done, rms_done, r_done, y_done = (
            sem(n) for n in ("y_mm", "gated", "res", "sq", "rms", "r", "y"))
        block = ctx.enter_context(nc.Block())

        WT = 2 * KD
        DVE_TILES = [m for m in range(WT) if m < KD or m % 2 == 0]
        POOL_TILES = [m for m in range(WT) if m not in DVE_TILES]
        AHEAD = 3
        EXTRA = [[3], [4], [5], [6], [7, 8], [9, 10], [11, 12], [13, 14, 15]]

        def raw_w(m):
            return (x, y)[m % 4 // 2][:, m % 2, :]

        def parts(m):
            w = wb if m < KD else wo
            return w[:, 0, m % KD, :], w[:, 1, m % KD, :]

        def wait_split(eng, m):
            if m in DVE_TILES:
                eng.wait_ge(w_lo_dve, DVE_TILES.index(m) + 1)
            else:
                eng.wait_ge(w_lo_pool, POOL_TILES.index(m) + 1)

        def turns(eng, body):
            body(0, True, False)
            with eng.Fori(1, CHUNKS_ - 1) as i:
                body(i, False, False)
            body(CHUNKS_ - 1, False, True)

        @block.sync
        def _(sp):
            def load_w(m):
                if m >= 4:
                    wait_split(sp, m - 4)
                src = io["w_br"][m] if m < KD else io["w_out"][:, m - KD, :]
                sp.dma_start(raw_w(m), src).then_inc(w_in[m % 4], 16)

            def load_oz(i, n):
                tok = bass.ds(i * CT, CT)
                srcs = [io[d][2 * n:2 * n + 2, :, tok].rearrange("b p t -> p b t") for d in ("o_d", "gates_d")]
                if not (isinstance(i, int) and i == 0 and n < 2):
                    sp.wait_ge(og_lo, i * PIECES + n - 1)
                for which in range(2):
                    sp.dma_start(oz[:, n % 2, which, :, :], srcs[which]).then_inc(oz_in[n % 2], 16)

            def load_gt(i, j):
                src = io["gates_d"][8:24, :, bass.ds(i * CT, CT)].rearrange("(w j) p t -> j p w t", w=2)[j]
                if not (isinstance(i, int) and i == 0 and j < GSLOTS):
                    sp.wait_ge(b_prod, i * 2 * KD + 2 * (j - GSLOTS + 1))
                sp.dma_start(gt[:, j % GSLOTS, :, :], src).then_inc(gt_in[j % GSLOTS], 16)

            load_oz(0, 0)
            load_oz(0, 1)
            load_w(0)
            load_w(1)
            load_oz(0, 2)
            load_oz(0, 3)
            for j in range(GSLOTS):
                load_gt(0, j)
                load_w(j + 2)

            def body(i, first, last):
                for j in range(GSLOTS, KD):
                    if first:
                        load_w(2 * j - 2)
                        load_w(2 * j - 1)
                    load_gt(i, j)
                if first:
                    load_w(WT - 2)
                    load_w(WT - 1)
                    sp.dma_start(gain[:, :], io["gain"].to_broadcast([P, D])).then_inc(gain_in, 16)
                if not last:
                    load_oz(i + 1, 0)
                    load_oz(i + 1, 1)
                for e in range(2):
                    src = io["x"][bass.ds(i * CT + e * P, P), :]
                    if first:
                        wait_split(sp, WT - 1 - e)
                        wait_split(sp, WT - 3 - e)
                    else:
                        sp.wait_ge(sq_done, i * 2 + e - 1)
                    sp.dma_start(x[:, e, :], src).then_inc(x_in[e], 16)
                stream = io["gate_d"][bass.ds(i // (LAT // CT), 1), :].to_broadcast([P, D])
                if not first:
                    sp.wait_ge(gated, i * 4)
                sp.dma_start(gate[:, :], stream).then_inc(gate_in, 16)
                if not last:
                    load_oz(i + 1, 2)
                    load_oz(i + 1, 3)
                    for j in range(GSLOTS):
                        load_gt(i + 1, j)
                for e in range(2):
                    dst = io["y"][bass.ds(i * CT + e * P, P), :]
                    sp.wait_ge(y_done, i * 2 + e + 1)
                    sp.dma_start(dst, y[:, e, :]).then_inc(y_out[e], 16)

            turns(sp, body)
            sp.wait_ge(y_out[0], CHUNKS_ * 16)
            sp.wait_ge(y_out[1], CHUNKS_ * 16)

        @block.scalar
        def _(act):
            def silu(i, n):
                act.wait_ge(oz_in[n % 2], (i * (PIECES // 2) + n // 2 + 1) * 32)
                act.activation(oz[:, n % 2, 1, :, :], oz[:, n % 2, 1, :, :], ACT.Silu).then_inc(silu_done, 1)

            def high(m):
                act.wait_ge(w_in[m % 4], (m // 4 + 1) * 16)
                act.activation(parts(m)[0], raw_w(m), ACT.Copy).then_inc(w_hi, 1)

            def sigmoid(i, j):
                act.wait_ge(gt_in[j % GSLOTS], (i * (KD // GSLOTS) + j // GSLOTS + 1) * 16)
                act.activation(gt[:, j % GSLOTS, :, :], gt[:, j % GSLOTS, :, :], ACT.Sigmoid).then_inc(sig_done, 1)

            silu(0, 0)
            silu(0, 1)
            high(0)
            silu(0, 2)
            silu(0, 3)
            high(1)
            high(2)
            act.wait_ge(eps_set, 1)

            def body(i, first, last):
                sigmoid(i, 0)
                for j in range(KD):
                    if j + 1 < KD:
                        sigmoid(i, j + 1)
                    act.wait_ge(summed, i * KD + j + 1)
                    act.activation(mg[:, 0, j, :], tp[:, j % 2, 0, :], ACT.Copy).then_inc(mg_hi, 1)
                    if first:
                        for m in EXTRA[j]:
                            high(m)
                if not last:
                    for n in range(PIECES):
                        silu(i + 1, n)
                for e in range(2):
                    act.wait_ge(res, i * 4 + 2 * e + 2)
                    act.activation(x[:, e, :], y[:, e, :], ACT.Square, accum_out=ss[:, e:e + 1]).then_inc(sq_done, 1)
                    act.wait_ge(sq_done, i * 2 + e + 1)
                    if not first:
                        act.wait_ge(r_done, i * 2 + e - 1)
                    act.activation(rms[:, e:e + 1], ss[:, e:e + 1], ACT.Sqrt, bias=epsc[:, 0:1], scale=1.0 / D
                                   ).then_inc(rms_done, 1)

            turns(act, body)

        @block.gpsimd
        def _(pool):
            def og_low(i, n):
                pool.wait_ge(og_hi, i * PIECES + n + 1)
                pool.tensor_tensor(og[:, 1, 2 * n:2 * n + 2, :], oz[:, n % 2, 0, :, :],
                                   og[:, 0, 2 * n:2 * n + 2, :].bitcast(F32), ALU.subtract).then_inc(og_lo, 1)

            pool.memset(epsc[:, :], EPS).then_inc(eps_set, 1)
            for n in range(PIECES):
                og_low(0, n)

            def body(i, first, last):
                for j in range(KD):
                    pool.wait_ge(b_prod, (i * KD + j) * 2 + 2)
                    pool.tensor_tensor(tp[:, j % 2, 0, :], tp[:, j % 2, 0, :], tp[:, j % 2, 1, :], ALU.add
                                       ).then_inc(summed, 1)
                    pool.wait_ge(mg_hi, i * KD + j + 1)
                    pool.tensor_tensor(mg[:, 1, j, :], tp[:, j % 2, 0, :], mg[:, 0, j, :].bitcast(F32), ALU.subtract
                                       ).then_inc(mg_lo, 1)
                    if first:
                        for m in EXTRA[j]:
                            if m in POOL_TILES:
                                pool.wait_ge(w_hi, m + 1)
                                hi, lo = parts(m)
                                pool.tensor_tensor(lo, raw_w(m), hi.bitcast(F32), ALU.subtract).then_inc(w_lo_pool, 1)
                if not last:
                    for n in range(PIECES):
                        og_low(i + 1, n)

            turns(pool, body)

        @block.tensor
        def _(pe):
            def body(i, first, last):
                for j in range(KD):
                    if first:
                        wait_split(pe, j)
                    for br in range(2):
                        if j == 0:
                            pe.wait_ge(og_lo, i * PIECES + 2 * br + 2)
                        if not (first and j < 2):
                            pe.wait_ge(b_prod, 2 * (i * KD + j - 2) + br + 1)
                        split_mm(pe, b_ps[:, j % 2, br, 0:CT],
                                 lambda a, k: wb[:, a, j, (4 * br + k) * P:(4 * br + k + 1) * P],
                                 lambda b, k: og[:, b, 4 * br + k, :], 4).then_inc(b_done, 1)
                for e in range(2):
                    for n in range(2):
                        if not first:
                            pe.wait_ge(gated, i * 4 + 2 * e + n - 3)
                        for k in range(KD):
                            if e == 0 and n == 0:
                                pe.wait_ge(mg_lo, i * KD + k + 1)
                                if first:
                                    wait_split(pe, KD + k)
                            for q, (a, b) in enumerate(((0, 0), (0, 1), (1, 0))):
                                mm = pe.matmul(y_ps[:, e, n * 512:(n + 1) * 512], mg[:, a, k, e * P:(e + 1) * P],
                                               wo[:, b, k, n * 512:(n + 1) * 512],
                                               start=(k == 0 and q == 0), stop=(k == KD - 1 and q == 2))
                        mm.then_inc(y_mm, 1)

            turns(pe, body)

        @block.vector
        def _(dve):
            def gate_o(i, n):
                dve.wait_ge(silu_done, i * PIECES + n + 1)
                dve.tensor_tensor(oz[:, n % 2, 0, :, :], oz[:, n % 2, 0, :, :], oz[:, n % 2, 1, :, :], ALU.mult
                                  ).then_inc(og_prod, 1)
                dve.wait_ge(og_prod, i * PIECES + n + 1)
                if n == 0 and not (isinstance(i, int) and i == 0):
                    dve.wait_ge(b_done, i * 2 * KD)
                dve.tensor_copy(og[:, 0, 2 * n:2 * n + 2, :], oz[:, n % 2, 0, :, :]).then_inc(og_hi, 1)

            def low(m):
                dve.wait_ge(w_hi, m + 1)
                hi, lo = parts(m)
                dve.tensor_tensor(lo, raw_w(m), hi.bitcast(F32), ALU.subtract).then_inc(w_lo_dve, 1)

            gate_o(0, 0)
            gate_o(0, 1)
            low(0)
            gate_o(0, 2)
            gate_o(0, 3)
            low(1)
            low(2)

            def body(i, first, last):
                for j in range(KD):
                    dve.wait_ge(sig_done, i * KD + j + 1)
                    if not (first and j < 2):
                        dve.wait_ge(mg_lo, i * KD + j - 1)
                    for br in range(2):
                        dve.wait_ge(b_done, (i * KD + j) * 2 + br + 1)
                        dve.tensor_tensor(tp[:, j % 2, br, :], b_ps[:, j % 2, br, 0:CT], gt[:, j % GSLOTS, br, :], ALU.mult
                                          ).then_inc(b_prod, 1)
                    if first:
                        for m in EXTRA[j]:
                            if m in DVE_TILES:
                                low(m)
                if not last:
                    for n in range(PIECES):
                        gate_o(i + 1, n)
                if first:
                    dve.wait_ge(gain_in, 16)
                dve.wait_ge(gate_in, (i + 1) * 16)
                for e in range(2):
                    dve.wait_ge(x_in[e], (i + 1) * 16)
                    if not first:
                        dve.wait_ge(y_out[e], i * 16)
                    for n in range(2):
                        half = slice(n * 512, (n + 1) * 512)
                        dve.wait_ge(y_mm, i * 4 + 2 * e + n + 1)
                        dve.tensor_tensor(y[:, e, half], y_ps[:, e, half], gate[:, half], ALU.mult).then_inc(gated, 1)
                        dve.wait_ge(gated, i * 4 + 2 * e + n + 1)
                        dve.tensor_tensor(y[:, e, half], y[:, e, half], x[:, e, half], ALU.add).then_inc(res, 1)
                    dve.wait_ge(rms_done, i * 2 + e + 1)
                    dve.reciprocal(rstd[:, e:e + 1], rms[:, e:e + 1]).then_inc(r_done, 1)
                    dve.wait_ge(r_done, i * 2 + e + 1)
                    dve.scalar_tensor_tensor(out=y[:, e, :], in0=y[:, e, :], scalar=rstd[:, e:e + 1], in1=gain[:, :],
                                             op0=ALU.mult, op1=ALU.mult).then_inc(y_done, 1)

            turns(dve, body)


def build(nc, io):
    before = nc.snapshot_sems()
    with ExitStack() as ctx:
        hm = ctx.enter_context(nc.sbuf_tensor("h", [P, 2, KD, TOK], F32R))
        ident = ctx.enter_context(nc.sbuf_tensor("ident_sb", [P, P], F32))
        with ExitStack() as first:
            wv = first.enter_context(nc.sbuf_tensor("wv", [P, 2, KD, VH * HD], F32R))
            wkb = first.enter_context(nc.sbuf_tensor("wkb", [P, 2, D], F32R))
            startup(nc, io, hm, ident, wv, wkb)
            values(nc, io, hm, wv, wkb)
        pairs(nc, io, hm, ident, "a")
        nc.clear_and_free_semaphores(nc.allocated_since(before))
        nc.all_engine_barrier()
        pairs(nc, io, hm, ident, "b")
    finish(nc, io)


def constants():
    c = {"ident": np.eye(P, dtype=np.float32)}
    qr, qc = np.arange(P) // QC, np.arange(P) % QC
    row = np.zeros((P, 2, KR), np.float32)
    for t in range(2):
        r, kr = QR * t + qr[:, None], 4 * t + np.arange(KR)[None]
        start = np.clip(r - NA_KH // 2, 0, ROWS - NA_KH)
        row[:, t] = np.where((kr >= start) & (kr < start + NA_KH), 0.0, BIG)
    col = np.zeros((P, 3, KC), np.float32)
    for ty, j in enumerate(TYPE_BLOCK):
        q, kc = j * QC + qc[:, None], KC0[j] + np.arange(KC)[None]
        start = np.clip(q - NA_KW // 2, 0, GRID_W - NA_KW)
        col[:, ty] = np.where((kc >= start) & (kc < start + NA_KW), 0.0, BIG)
    band = np.zeros((P, 3, NB), np.float32)
    for ty in range(3):
        off = np.arange(NB)[None] - P * ty - np.arange(P)[:, None]
        band[:, ty] = np.where(np.abs(off) <= WINDOW, 0.0, BIG)
    half = HD // 2
    inv = (np.float32(10000.0) ** (-np.arange(0, half, 2, dtype=np.float32) / np.float32(half))).astype(np.float32)
    t = np.arange(LAT)
    pos = np.stack([t // GRID_W, t % GRID_W]).astype(np.float32)
    ang = pos[:, None, :] * inv[None, :, None]
    cos, sin = np.cos(ang).astype(np.float32), np.sin(ang).astype(np.float32)
    c["cos"] = np.tile(np.concatenate([cos, cos], 1).reshape(HD, LAT), (2, 1))
    c["sin"] = np.tile(np.concatenate([-sin, sin], 1).reshape(HD, LAT), (2, 1))
    c["rowmask"], c["colmask"], c["band"] = row, col, band
    return c


def layout(x_prompt, x_sample, cache_a_k, cache_a_v, cache_b_k, cache_b_v, c, c_ctx, w_ada, b_ada, w_in, rpb_a,
           sink_b, w_br_a, w_br_b, w_out, final_norm_g):
    f = lambda a: np.asarray(a)
    a = constants()
    a["x"] = np.concatenate([f(x_sample)[0], f(x_prompt)[0]])
    a["c_col"] = np.stack([f(c)[0], f(c_ctx)], -1).reshape(KD, P, 2).transpose(1, 0, 2)
    a["b_col"] = f(b_ada)[0, :2 * D].reshape(2 * KD, P).T
    a["b_gate"] = f(b_ada)[:, 2 * D:]
    a["w_ada"] = f(w_ada)[0]
    blocks = f(w_in)[0].reshape(KD, P, -1, P).transpose(2, 1, 0, 3).reshape(-1, P, D)
    a["w_qa"], a["w_ka"], a["w_qb"], a["w_kb"] = blocks[0:4], blocks[4:8], blocks[16:20], blocks[20]
    a["w_gate"] = np.concatenate([blocks[12:16], blocks[22:26], blocks[26:42]])
    cols = f(w_in)[0].reshape(KD, P, -1).transpose(1, 0, 2)
    a["w_v"] = np.concatenate([cols[:, :, 1024:1536], cols[:, :, 2688:2816]], -1)
    a["w_br"] = np.concatenate([f(w)[0].reshape(4, P, KD, P).transpose(2, 1, 0, 3) for w in (w_br_a, w_br_b)], 2
                               ).reshape(KD, P, D)
    a["w_out"] = f(w_out)[0].reshape(KD, P, D).transpose(1, 0, 2)
    a["cka"] = f(cache_a_k)[0, 0].transpose(1, 2, 0).reshape(PAIRS, P, PAST)
    a["cva"] = f(cache_a_v)[0, 0].reshape(4, P, PAIRS, P).transpose(2, 1, 0, 3).reshape(PAIRS, P, 4 * P)
    kb = f(cache_b_k)[0, 0].transpose(1, 2, 0)
    a["ckb"] = np.stack([np.concatenate([kb[p // 2]] * 2) for p in range(PAIRS)])
    vb = f(cache_b_v)[0, 0].reshape(4, P, 2, HD).transpose(2, 1, 0, 3).reshape(2, P, 4 * HD)
    a["cvb"] = np.stack([vb[p // 2] for p in range(PAIRS)])
    pad = np.pad(f(rpb_a)[0], ((0, 0), (4, 4), (16, 16)))
    a["bias"] = np.stack([pad[:, QR - 1 - r:QR - 1 - r + BR, QC - 1 - q:QC - 1 - q + BC]
                          for r in range(QR) for q in range(QC)], 1)
    a["sink"] = f(sink_b)
    a["gain"] = f(final_norm_g)[None]
    return {k: np.ascontiguousarray(v) for k, v in a.items()}


SCRATCH = {"v_d": [TOK, VH * 2 * HD], "kb_d": [2, 2, HD, TOK], "gates_d": [GATE_BLOCKS, P, TOK],
           "o_d": [KD, P, TOK], "gate_d": [2, D]}
OUTS = {"y": [TOK, D], "new_ak": [PAIRS, P, PROMPT], "new_av": [PROMPT, 8 * HD], "new_bk": [P, PROMPT],
        "new_bv": [PROMPT, 2 * HD]}


def kernel(**inputs):
    import concourse.bacc as bacc
    from concourse.bass_utils import run_bass_kernel_spmd

    nc = bacc.Bacc("TRN2", target_bir_lowering=False, num_devices=1)
    arrays = {f"in_{k}": v for k, v in layout(**inputs).items()}
    io = {}
    for name, a in arrays.items():
        io[name[3:]] = nc.dram_tensor(name, list(a.shape), mybir.dt.from_np(a.dtype), kind="ExternalInput").ap()
    for name, shape in SCRATCH.items():
        io[name] = nc.dram_tensor(name, shape, F32, kind="Internal").ap()
    for name, shape in OUTS.items():
        io[name] = nc.dram_tensor(name, shape, F32, kind="ExternalOutput").ap()
    build(nc, io)
    got = run_bass_kernel_spmd(nc, [arrays], core_ids=[0]).results[0]
    y = got["y"]
    to_tok = lambda k, h: k.reshape(h, HD, PROMPT).transpose(2, 0, 1)[None, None]
    return (y[LAT:][None], y[:LAT][None], to_tok(got["new_ak"], NA_HEADS),
            got["new_av"].reshape(1, 1, PROMPT, NA_HEADS, HD), to_tok(got["new_bk"], 2),
            got["new_bv"].reshape(1, 1, PROMPT, 2, HD))
```

```python
from contextlib import ExitStack

import numpy as np

import concourse.bass as bass
from concourse import mybir

F32 = mybir.dt.float32
F32R = mybir.dt.float32r
ALU = mybir.AluOpType
ACT = mybir.ActivationFunctionType
AX = mybir.AxisListType

P = 128
D = 1024
KD = D // P
LAT, PROMPT = 1024, 256
TOK = LAT + PROMPT
PAST = 512
HD = 64
GRID_W = 64
ROWS = LAT // GRID_W
NA_HEADS, NA_KH, NA_KW = 8, 8, 16
QR, QC = 8, 16
KR, KC = 12, 32
NCB = GRID_W // QC
KC0 = [min(max(j * QC - (KC - QC) // 2, 0), GRID_W - KC) for j in range(NCB)]
BIAS_TYPE = [0, 1, 1, 2]
TYPE_BLOCK = [0, 1, 3]
TYPE_OFF = [KC0[j] - j * QC for j in TYPE_BLOCK]
BR, BC = 16, 48
WINDOW = 128
NB = KR * KC
SW = PAST + NB
PAIRS = 4
EPS = 1e-6
QSCALE = -(HD ** -0.5)
BIG = 1e30
VH = 10
UNIT = 320
UNITS = TOK // UNIT
GROUPS = [(0, 512), (512, 512), (1024, 256)]
GATE_BLOCKS = 24
GPP = 3
STEPS = 10
CHUNKS = [1, 1] + [4] * 8
CHUNK0 = [sum(CHUNKS[:s]) for s in range(STEPS)]
NCHUNK = sum(CHUNKS)


def split_mm(eng, out, lhs, rhs, n_k, begun=None):
    for k in range(n_k):
        for i, (a, b) in enumerate(((0, 0), (0, 1), (1, 0))):
            mm = eng.matmul(out, lhs(a, k), rhs(b, k), start=(k == 0 and i == 0), stop=(k == n_k - 1 and i == 2))
            if begun is not None and k == 0 and i == 0:
                mm.then_inc(begun, 1)
    return mm


def split(eng, hi, lo, src, one, hi_sem, hi_value, lo_sem):
    eng.tensor_tensor(hi, src, one[:, :].to_broadcast(list(src.shape)), ALU.mult).then_inc(hi_sem, 1)
    eng.wait_ge(hi_sem, hi_value)
    eng.tensor_tensor(lo, src, hi.bitcast(F32), ALU.subtract).then_inc(lo_sem, 1)


def startup(nc, io, hm, ident, wv, wkb):
    with ExitStack() as ctx:
        def sb(name, shape, dt=F32):
            return ctx.enter_context(nc.sbuf_tensor(name, shape, dt))

        def ps(name, shape):
            return ctx.enter_context(nc.psum_tensor(name, shape, F32))

        def sem(name):
            return nc.alloc_semaphore(name=name)

        XG = [(0, 4), (4, 4), (8, 2)]
        x4, x2 = sb("x4", [P, 2, 4, D]), sb("x2", [P, 2, D])
        wada = sb("wada", [P, 4, D])
        vraw = sb("vraw", [P, 2, VH * HD])
        h32 = sb("h32", [P, 2, 512])
        modrow = wada[0:2, 0:2, :].rearrange("p a b -> p (a b)")
        kraw = wada[:, 3, :]
        ccol = sb("ccol", [P, KD, 2])
        scol = sb("scol", [P, KD, 2])
        bcol = sb("bcol", [P, 2 * KD])
        modc = sb("modc", [P, 2 * KD, 2])
        modf = sb("modf", [P, 2 * KD, 2])
        ss = sb("ss", [P, 12])
        rms = sb("rms", [P, 12])
        rstd = sb("rstd", [P, 12])
        epsc = sb("epsc", [P, 1])
        one = sb("one", [P, 1])
        mod_ps = ps("mod_ps", [P, 4, 512])
        t_ps = ps("t_ps", [P, 2, 512])
        junk = ps("junk", [P, D])

        small_in, ident_in, kraw_in, eps_set = sem("small_in"), sem("ident_in"), sem("kraw_in"), sem("eps_set")
        x_in = [sem(f"x_in{g}") for g in range(3)]
        wada_in = [sem(f"wada_in{i}") for i in range(8)]
        vraw_in = [sem(f"vraw_in{i}") for i in range(2)]
        silu_done, wada_used, mod_row, mod_t, mod_c, mod_ready = (
            sem(n) for n in ("silu_done", "wada_used", "mod_row", "mod_t", "mod_c", "mod_ready"))
        sq_done, rms_done, rstd_done, xn_done, xt_done = (
            sem(n) for n in ("sq_done", "rms_done", "rstd_done", "xn_done", "xt_done"))
        h_done, hi_done, lo_done, v_hi, v_lo, k_hi, k_lo = (
            sem(n) for n in ("h_done", "hi_done", "lo_done", "v_hi", "v_lo", "k_hi", "k_lo"))

        block = ctx.enter_context(nc.Block())
        chunks = [(g, k) for g in range(3) for k in range(KD)]

        def wslot(i):
            return wada[:, i % 8, :] if i % 8 < 4 else x4[:, 1, i % 8 - 4, :]

        def x(g):
            return x4[:, g, :, :] if g < 2 else x2

        @block.sync
        def _(sp):
            def load_x(g):
                t0, n = XG[g]
                sp.dma_start(x(g)[:, :, :], io["x"][t0 * P:(t0 + n) * P, :].rearrange("(t p) d -> p t d", p=P)
                             ).then_inc(x_in[g], 16)

            def load_wada(i):
                if i >= 8:
                    sp.wait_ge(wada_used, i - 7)
                k, half = i // 2, i % 2
                sp.dma_start(wslot(i), io["w_ada"][k * P:(k + 1) * P, half * D:(half + 1) * D]
                             ).then_inc(wada_in[i % 8], 16)

            sp.dma_start(ccol[:, :, :], io["c_col"]).then_inc(small_in, 16)
            sp.dma_start(bcol[:, :], io["b_col"]).then_inc(small_in, 16)
            for i in range(2 * KD):
                load_wada(i)
                if i == 10:
                    load_x(0)
            sp.dma_start(ident[:, :], io["ident"]).then_inc(ident_in, 16)
            sp.wait_ge(wada_used, 2 * KD)
            load_x(1)
            sp.dma_start(kraw, io["w_kb"]).then_inc(kraw_in, 16)
            for k in range(KD):
                if k >= 2:
                    sp.wait_ge(v_lo, k - 1)
                sp.dma_start(vraw[:, k % 2, :], io["w_v"][:, k, :]).then_inc(vraw_in[k % 2], 16)
                if k == 2:
                    load_x(2)

        @block.gpsimd
        def _(pool):
            pool.memset(epsc[:, :], EPS).then_inc(eps_set, 1)
            pool.memset(one[:, :], 1.0).then_inc(eps_set, 1)
            pool.wait_ge(eps_set, 2)
            pool.wait_ge(kraw_in, 16)
            split(pool, wkb[:, 0, :], wkb[:, 1, :], kraw, one, k_hi, 1, k_lo)
            for k in range(KD):
                pool.wait_ge(vraw_in[k % 2], 16 * (k // 2 + 1))
                split(pool, wv[:, 0, k, :], wv[:, 1, k, :], vraw[:, k % 2, :], one, v_hi, k + 1, v_lo)

        @block.scalar
        def _(act):
            act.wait_ge(small_in, 32)
            act.activation(scol[:, :, :], ccol[:, :, :], ACT.Silu).then_inc(silu_done, 1)
            act.wait_ge(eps_set, 1)

            def norms(g):
                t0, n = XG[g]
                act.wait_ge(x_in[g], 16)
                for t in range(n):
                    if t0 + t > 0:
                        act.wait_ge(sq_done, t0 + t)
                    act.activation(junk[:, :], x(g)[:, t, :], ACT.Square, accum_out=ss[:, t0 + t:t0 + t + 1]
                                   ).then_inc(sq_done, 1)
                act.wait_ge(sq_done, t0 + n)
                act.activation(rms[:, t0:t0 + n], ss[:, t0:t0 + n], ACT.Sqrt, bias=epsc[:, 0:1], scale=1.0 / D
                               ).then_inc(rms_done, 1)

            norms(0)
            act.wait_ge(mod_ready, 1)
            for i, (g, k) in enumerate(chunks):
                if i == 4:
                    norms(1)
                if i == KD + 4:
                    norms(2)
                n, stream = XG[g][1] * P, int(g == 2)
                act.wait_ge(xt_done, i + 1)
                if i >= 2:
                    act.wait_ge(lo_done, i - 1)
                act.activation(h32[:, i % 2, 0:n], t_ps[:, i % 2, 0:n], ACT.Identity,
                               bias=modf[:, k, stream:stream + 1], scale=modf[:, KD + k, stream:stream + 1]
                               ).then_inc(h_done, 1)

        @block.tensor
        def _(pe):
            pe.wait_ge(silu_done, 1)
            for i in range(2 * KD):
                k, half = i // 2, i % 2
                pe.wait_ge(wada_in[i % 8], 16 * (i // 8 + 1))
                for c in range(2):
                    mm = pe.matmul(mod_ps[0:2, 2 * half + c, :], scol[:, k, :], wslot(i)[:, c * 512:(c + 1) * 512],
                                   start=(k == 0), stop=(k == KD - 1))
                mm.then_inc(wada_used, 1)
            pe.wait_ge(ident_in, 16)
            pe.wait_ge(mod_row, 1)
            for b in range(2 * KD):
                mm = pe.transpose(mod_ps[:, 0, 2 * b:2 * b + 2], modrow[:, b * P:(b + 1) * P], ident[0:2, 0:2])
            mm.then_inc(mod_t, 1)
            for i, (g, k) in enumerate(chunks):
                pe.wait_ge(xn_done, XG[g][0] + XG[g][1])
                if i >= 2:
                    pe.wait_ge(h_done, i - 1)
                for t in range(XG[g][1]):
                    mm = pe.transpose(t_ps[:, i % 2, t * P:(t + 1) * P], x(g)[:, t, k * P:(k + 1) * P], ident[:, :])
                mm.then_inc(xt_done, 1)

        @block.vector
        def _(dve):
            def normalise(g):
                t0, n = XG[g]
                dve.wait_ge(rms_done, g + 1)
                dve.reciprocal(rstd[:, t0:t0 + n], rms[:, t0:t0 + n]).then_inc(rstd_done, 1)
                dve.wait_ge(rstd_done, g + 1)
                for t in range(n):
                    dve.tensor_scalar(x(g)[:, t, :], x(g)[:, t, :], rstd[:, t0 + t:t0 + t + 1], None, ALU.mult
                                      ).then_inc(xn_done, 1)

            normalise(0)
            dve.wait_ge(wada_used, 2 * KD)
            dve.tensor_copy(modrow, mod_ps[0:2, :, :].rearrange("p a b -> p (a b)")).then_inc(mod_row, 1)
            dve.wait_ge(mod_t, 1)
            dve.wait_ge(small_in, 32)
            for s in range(2):
                dve.tensor_tensor(modc[:, :, s], mod_ps[:, 0, 0:4 * KD].rearrange("p (b s) -> p b s", s=2)[:, :, s],
                                  bcol[:, :], ALU.add).then_inc(mod_c, 1)
            dve.wait_ge(mod_c, 2)
            dve.tensor_copy(modf[:, 0:KD, :], modc[:, 0:KD, :]).then_inc(mod_c, 1)
            dve.tensor_scalar(modf[:, KD:, :], modc[:, KD:, :], 1.0, None, ALU.add).then_inc(mod_ready, 1)
            for i, (g, k) in enumerate(chunks):
                if i == 4:
                    normalise(1)
                if i == KD + 4:
                    normalise(2)
                t0, n = XG[g][0] * P, XG[g][1] * P
                dve.wait_ge(h_done, i + 1)
                dve.tensor_copy(hm[:, 0, k, t0:t0 + n], h32[:, i % 2, 0:n]).then_inc(hi_done, 1)
                dve.wait_ge(hi_done, i + 1)
                dve.tensor_tensor(hm[:, 1, k, t0:t0 + n], h32[:, i % 2, 0:n], hm[:, 0, k, t0:t0 + n].bitcast(F32),
                                  ALU.subtract).then_inc(lo_done, 1)


SWAP16 = [(i + 16) % 32 for i in range(32)]


def values(nc, io, hm, wv, wkb, wq, craw):
    with ExitStack() as ctx:
        def sb(name, shape, dt=F32):
            return ctx.enter_context(nc.sbuf_tensor(name, shape, dt))

        def ps(name, shape):
            return ctx.enter_context(nc.psum_tensor(name, shape, F32))

        def sem(name):
            return nc.alloc_semaphore(name=name)

        vst = sb("vst", [P, 2, VH, 2 * HD], F32R)
        vout = sb("vout", [P, 2, VH * HD])
        kst = sb("kst", [P, 2, TOK], F32R)
        kout = sb("kout", [P, PROMPT])
        cos, sin = sb("cos_v", [P, LAT]), sb("sin_v", [P, LAT])
        raw, swp, rot = sb("raw_v", [P, 512]), sb("swp_v", [P, 512]), sb("rot_v", [P, 512])
        wgate = sb("wgate", [P, 2, D])
        gcc, gsc = sb("gcc", [P, KD, 2]), sb("gsc", [P, KD, 2])
        gb, grow = sb("gb", [2, D]), sb("grow", [2, D])
        v_ps = ps("v_ps", [P, 3, 512])
        k_ps = ps("k_ps", [P, 3, 512])
        g_ps = ps("g_ps", [P, 2, 512])

        one = sb("one_v", [P, 1])
        ones_set, q_in, q_hi, q_lo = sem("v_ones"), sem("v_q_in"), sem("v_q_hi"), sem("v_q_lo")
        small_in, table_in, silu_done = sem("v_small_in"), sem("v_table_in"), sem("v_silu")
        wg_in = [sem(f"wg_in{i}") for i in range(2)]
        wg_used, g_row, g_out = sem("wg_used"), sem("g_row"), sem("g_out")
        mm_done, k_mm, v_hi, v_lo, v_copy = sem("v_mm"), sem("v_k_mm"), sem("v_hi2"), sem("v_lo2"), sem("v_copy")
        v_out = [sem(f"v_out{i}") for i in range(2)]
        vo_out = sem("vo_out")
        k_raw, k_swp, k_cos, k_sin, k_rot, k_hi, k_lo, k_copy, k_out = (
            sem(n) for n in ("k_raw", "k_swp", "k_cos", "k_sin", "k_rot", "kv_hi", "kv_lo", "k_copy", "k_out"))
        block = ctx.enter_context(nc.Block())
        TT = TOK // P
        NU = 2 * TT
        HW = VH * HD // 2

        @block.sync
        def _(sp):
            sp.dma_start(gcc[:, :, :], io["c_col"]).then_inc(small_in, 16)
            sp.dma_start(gb[:, :], io["b_gate"].to_broadcast([2, D])).then_inc(small_in, 16)
            sp.dma_start(cos[:, :], io["cos"]).then_inc(table_in, 16)
            sp.dma_start(sin[:, :], io["sin"]).then_inc(table_in, 16)

            def store_k():
                sp.wait_ge(k_copy, 1)
                sp.dma_start(io["new_bk"], kout[:, :]).then_inc(k_out, 16)
                sp.wait_ge(k_lo, 3)
                for part in range(2):
                    for kv in range(2):
                        sp.dma_start(io["kb_d"][kv, part], kst[kv * HD:(kv + 1) * HD, part, :].bitcast(F32)
                                     ).then_inc(k_out, 16)

            def load_gate_weights(k):
                sp.dma_start(wgate[:, k % 2, :], io["w_ada"][k * P:(k + 1) * P, 2 * D:3 * D]).then_inc(wg_in[k % 2], 16)

            load_gate_weights(0)
            load_gate_weights(1)
            sp.dma_start(craw[:, :], io["w_q"][0]).then_inc(q_in, 16)
            for t in range(TT):
                sp.wait_ge(v_lo, 2 * t + 2)
                sp.dma_start(io["v_d"][t * P:(t + 1) * P, :], vst[:, t % 2, :, :].rearrange("p h c -> p (h c)").bitcast(F32)
                             ).then_inc(v_out[t % 2], 16)
                if t == 2:
                    store_k()
                if 2 <= t < KD:
                    sp.wait_ge(wg_used, t - 1)
                    load_gate_weights(t)
                if t * P >= LAT:
                    s = t - LAT // P
                    sp.wait_ge(v_copy, 2 * s + 2)
                    sp.dma_start(io["new_av"][s * P:(s + 1) * P, :], vout[:, s, 0:8 * HD]).then_inc(vo_out, 16)
                    sp.dma_start(io["new_bv"][s * P:(s + 1) * P, :], vout[:, s, 8 * HD:]).then_inc(vo_out, 16)
            sp.wait_ge(g_row, 1)
            sp.dma_start(io["gate_d"], grow[:, :]).then_inc(g_out, 16)
            sp.wait_ge(v_out[0], 16 * (TT // 2))
            sp.wait_ge(v_out[1], 16 * (TT // 2))
            sp.wait_ge(vo_out, 64)
            sp.wait_ge(g_out, 16)
            sp.wait_ge(k_out, 80)

        @block.tensor
        def _(pe):
            for g, (t0, n) in enumerate(GROUPS):
                split_mm(pe, k_ps[:, g, 0:n], lambda a, k: wkb[:, a, k * P:(k + 1) * P],
                         lambda b, k: hm[:, b, k, t0:t0 + n], KD).then_inc(k_mm, 1)
            for u in range(NU):
                t, n = u // 2, u % 2
                if u >= 3:
                    pe.wait_ge(v_lo, u - 2)
                split_mm(pe, v_ps[:, u % 3, 0:HW], lambda a, k: hm[:, a, k, t * P:(t + 1) * P],
                         lambda b, k: wv[:, b, k, n * HW:(n + 1) * HW], KD).then_inc(mm_done, 1)
                if n == 0 and 2 <= t < KD + 2:
                    k = t - 2
                    if k == 0:
                        pe.wait_ge(silu_done, 1)
                    pe.wait_ge(wg_in[k % 2], 16 * (k // 2 + 1))
                    for c in range(2):
                        mm = pe.matmul(g_ps[0:2, c, :], gsc[:, k, :], wgate[:, k % 2, c * 512:(c + 1) * 512],
                                       start=(k == 0), stop=(k == KD - 1))
                    mm.then_inc(wg_used, 1)

        @block.scalar
        def _(act):
            act.wait_ge(small_in, 32)
            act.activation(gsc[:, :, :], gcc[:, :, :], ACT.Silu).then_inc(silu_done, 1)
            for g, (t0, n) in enumerate(GROUPS):
                act.wait_ge(k_mm, g + 1)
                if g > 0:
                    act.wait_ge(k_lo, g)
                act.activation((rot if g == 2 else raw)[:, 0:n], k_ps[:, g, 0:n], ACT.Copy).then_inc(k_raw, 1)
            for u in range(NU):
                t, n = u // 2, u % 2
                act.wait_ge(mm_done, u + 1)
                if t >= 2 and n == 0:
                    act.wait_ge(v_out[t % 2], 16 * (t // 2))
                if t * P >= LAT:
                    act.activation(vout[:, t - LAT // P, n * HW:(n + 1) * HW], v_ps[:, u % 3, 0:HW], ACT.Copy
                                   ).then_inc(v_copy, 1)
                act.activation(vst[:, t % 2, 5 * n:5 * n + 5, 0:HD],
                               v_ps[:, u % 3, 0:HW].rearrange("p (h c) -> p h c", c=HD), ACT.Copy).then_inc(v_hi, 1)

        @block.gpsimd
        def _(pool):
            pool.memset(one[:, :], 1.0).then_inc(ones_set, 1)
            pool.wait_ge(ones_set, 1)
            pool.wait_ge(table_in, 32)
            for g, (t0, n) in enumerate(GROUPS[:2]):
                pool.wait_ge(k_swp, g + 1)
                pool.tensor_tensor(swp[:, :], swp[:, :], sin[:, t0:t0 + n], ALU.mult).then_inc(k_sin, 1)
            pool.wait_ge(q_in, 16)
            split(pool, wq[:, 0, :], wq[:, 1, :], craw[:, :], one, q_hi, 1, q_lo)

        @block.vector
        def _(dve):
            dve.wait_ge(table_in, 32)
            for g, (t0, n) in enumerate(GROUPS):
                dve.wait_ge(k_raw, g + 1)
                if g < 2:
                    dve.tensor_tensor(rot[:, :], raw[:, :], cos[:, t0:t0 + n], ALU.mult).then_inc(k_cos, 1)
                    dve.stream_shuffle(swp[:, :], raw[:, :], SWAP16).then_inc(k_swp, 1)
                    dve.wait_ge(k_sin, g + 1)
                    dve.wait_ge(k_cos, g + 1)
                    dve.tensor_tensor(rot[:, :], rot[:, :], swp[:, :], ALU.add).then_inc(k_rot, 1)
                    dve.wait_ge(k_rot, g + 1)
                else:
                    dve.tensor_copy(kout[:, :], rot[:, 0:n]).then_inc(k_copy, 1)
                dve.tensor_copy(kst[:, 0, t0:t0 + n], rot[:, 0:n]).then_inc(k_hi, 1)
                dve.wait_ge(k_hi, g + 1)
                dve.tensor_tensor(kst[:, 1, t0:t0 + n], rot[:, 0:n], kst[:, 0, t0:t0 + n].bitcast(F32), ALU.subtract
                                  ).then_inc(k_lo, 1)
            for u in range(NU):
                t, n = u // 2, u % 2
                hi = vst[:, t % 2, 5 * n:5 * n + 5, 0:HD]
                dve.wait_ge(v_hi, u + 1)
                dve.tensor_tensor(vst[:, t % 2, 5 * n:5 * n + 5, HD:],
                                  v_ps[:, u % 3, 0:HW].rearrange("p (h c) -> p h c", c=HD), hi.bitcast(F32),
                                  ALU.subtract).then_inc(v_lo, 1)
            dve.wait_ge(small_in, 32)
            dve.wait_ge(wg_used, KD)
            dve.tensor_tensor(grow[:, :], g_ps[0:2, :, :].rearrange("p a b -> p (a b)"), gb[:, :], ALU.add
                              ).then_inc(g_row, 1)


def pairs(nc, io, hm, ident, wq, craw, branch):
    A = branch == "a"
    with ExitStack() as ctx:
        def sb(name, shape, dt=F32):
            return ctx.enter_context(nc.sbuf_tensor(f"{name}_{branch}", shape, dt))

        def ps(name, shape):
            return ctx.enter_context(nc.psum_tensor(f"{name}_{branch}", shape, F32))

        def sem(name):
            return nc.alloc_semaphore(name=f"{name}_{branch}")

        wkg = sb("wkg", [P, 2, 2, D], F32R)
        wraw = sb("wraw", [P, D])
        q1 = sb("q1", [P, 2, TOK], F32R)
        q2 = sb("q2", [P, TOK], F32R)
        kk = sb("kk", [P, 2, TOK], F32R)
        kc = sb("kc", [P, 2, PAST], F32R)
        CH = 2 if A else 1
        vc = sb("vc", [P, PAST // P, CH, 2 * HD], F32R)
        vw = sb("vw", [P, 16 if A else 8, CH * 2 * HD], F32R)
        vp = sb("vp", [P, 2, CH * 2 * HD], F32R)
        pr = sb("pr", [P, 2, NB + PAST + NB])
        pt = sb("pt", [P, 2, 14 * P], F32R)
        ost = sb("ost", [P, TOK])
        gst = sb("gst", [P, 2, UNIT])
        otmp = sb("otmp", [HD, 2 * P])
        one = sb("one", [P, 1])
        mn = sb("mn", [P, 2])
        nm = sb("nm", [P, 2])
        mx = sb("mx", [P, 2])
        den = sb("den", [P, 2])
        rden = sb("rden", [P, 2])
        if A:
            rb = sb("rb", [P, BR, BC])
            comb = sb("comb", [P, 2, 2, NB])
            rowm = sb("rowm", [P, 2, KR])
            colm = sb("colm", [P, 3, KC])
            kout = sb("kout", [P, PROMPT])
        else:
            band = sb("band", [P, 3, NB])
            cos, sin = sb("cos", [P, LAT]), sb("sin", [P, LAT])
            raw, swp, rot = sb("raw", [P, 512]), sb("swp", [P, 512]), sb("rot", [P, 512])
            sink = sb("sink", [P, 8])
            nsink = sb("nsink", [P, 8])
            nsk = sb("nsk", [P, 2])
            esk = sb("esk", [P, 2])
            den2 = sb("den2", [P, 2])
        s_ps = ps("s_ps", [P, 4, 512])
        t_ps = ps("t_ps", [P, 2, 512])
        o_ps = ps("o_ps", [P, 512])
        d_ps = ps("d_ps", [P, 512])

        PROJ = 2 if A else 1
        TILES = PROJ + GPP
        SLOT = [0, 1, 2, 1, 2] if A else [0, 1, 2, 1]
        NG = PROJ * 3
        if A:
            PROJECTED = [(0, 0, 0), (0, 1, 1), (0, 2, 2), (1, 2, 3), (1, 0, 1), (1, 1, 3)]
        else:
            PROJECTED = [(0, 2, 0), (0, 0, 1), (0, 1, 3)]
        EARLY = None if A else 2
        PROMPT_READY = 4 if A else 1

        def wt(i, part, k):
            w = wq if i == 0 else wkg[:, SLOT[i] - 1]
            return w[:, part, k * P:(k + 1) * P]

        def slot_free(i):
            last = max([k for k in range(i) if SLOT[k] == SLOT[i]] or
                       [k - TILES for k in range(TILES) if SLOT[k] == SLOT[i]])
            return max(last + 2, 0)

        w_in, q_in = sem("w_in"), sem("q_in")
        craw_in, w_hi, w_lo = sem("craw_in"), sem("w_hi"), sem("w_lo")
        w_begun = sem("w_begun")
        c_split = sem("c_split")
        const_in, sink_in, band_in, vw_in, kk_in = (sem(n) for n in ("const_in", "sink_in", "band_in", "vw_in", "kk_in"))
        rb_in, comb_t, comb_done = sem("rb_in"), sem("comb_t"), sem("comb_done")
        ckh, cvh = sem("ckh"), sem("cvh")
        proj_done, xa, xd, x_used = sem("proj_done"), sem("xa"), sem("xd"), sem("x_used")
        ko_done, ko_out = sem("ko_done"), sem("ko_out")
        s_done, m1_done, m2_done, m3_done, m_done, exp_done = (
            sem(n) for n in ("s_done", "m1_done", "m2_done", "m3_done", "m_done", "exp_done"))
        esk_done, den_done, r_done, p_done = sem("esk_done"), sem("den_done"), sem("r_done"), sem("p_done")
        t_done, hi_done, lo_done, pva_done, pvb_done, ot_done, o_done = (
            sem(n) for n in ("t_done", "hi_done", "lo_done", "pva_done", "pvb_done", "ot_done", "o_done"))
        d_done, g_done = sem("d_done"), sem("g_done")
        g_out = [sem("g_out0"), sem("g_out1")]
        o_out = sem("o_out")
        r_raw, r_swp, r_cos, r_sin, r_rot = (sem(n) for n in ("r_raw", "r_swp", "r_cos", "r_sin", "r_rot"))
        nsk_done, ones_set = sem("nsk_done"), sem("ones_set")

        block = ctx.enter_context(nc.Block())
        base = 0 if A else PAIRS

        def grid(ap, r0, nr, c0, ncol):
            return ap[..., 0:LAT].rearrange("p (r c) -> p r c", c=GRID_W)[:, r0:r0 + nr, c0:c0 + ncol]

        def rows(ap):
            return ap.rearrange("p (r j c) -> p r j c", r=QR, c=QC) if ap.shape[-1] == 512 else ap

        def tiled(ap):
            return ap.rearrange("p (j r c) -> p r j c", r=QR, c=QC) if ap.shape[-1] == 512 else ap

        def near_bank(s, t):
            return s_ps[:, 2 * t, PAST - NB:PAST] if s % 2 else s_ps[:, 2 * t + 1, 0:NB]

        def scores_run(s, t):
            both = s_ps[:, 2 * t:2 * t + 2, :].rearrange("p a b -> p (a b)")
            return both[:, 0:PROMPT] if s < 2 else both[:, PAST - NB:] if s % 2 else both[:, 0:SW]

        def probs_run(s, t):
            return pr[:, t, NB:NB + PROMPT] if s < 2 else pr[:, t, 0:SW] if s % 2 else pr[:, t, NB:]

        def probs_block(s, t, kb):
            c0 = NB + kb * P if kb < 4 or s % 2 == 0 else (kb - 4) * P
            return pr[:, t, c0:c0 + P]

        def chunk_blocks(s):
            if s < 2:
                return [[(0, 0), (0, 1), (1, 0), (1, 1)]]
            if A:
                near = [(4, 0), (5, 0), (4, 1), (6, 0), (5, 1), (6, 1)]
            else:
                near = [(kb, t) for kb in (4, 5, 6) for t in (0, 1)]
            ctx_ = [(kb, t) for kb in range(4) for t in (0, 1)]
            return [ctx_[0:4], ctx_[4:8], near[0:4], near[4:6]]

        @block.sync
        def _(sp):
            with sp.Fori(0, PAIRS) as p:
                def load_tile(i):
                    if i < PROJ:
                        src = io["w_k" + branch][p]
                    else:
                        src = io["w_gate"][(p + base) * GPP + (i - PROJ)]
                    sp.wait_ge(w_lo, p * TILES + i - 1 if i > 1 else p * TILES)
                    sp.dma_start(wraw[:, :], src).then_inc(w_in, 16)

                def load_caches():
                    sp.wait_ge(w_lo, p * TILES)
                    sp.dma_start(craw[:, 0:PAST], io["ck" + branch][p]).then_inc(craw_in, 16)
                    sp.dma_start(craw[:, PAST:PAST + 4 * CH * HD], io["cv" + branch][p]).then_inc(craw_in, 16)

                if A:
                    load_caches()
                    load_tile(1)
                else:
                    kv = p // 2
                    sp.wait_ge(exp_done, p * 2 * STEPS)
                    for h in range(2):
                        for part in range(2):
                            r0 = HD * ((h + part) % 2)
                            sp.dma_start(kk[r0:r0 + HD, h, :].bitcast(F32), io["kb_d"][kv, part]).then_inc(kk_in, 16)
                    load_tile(1)
                    load_caches()
                sp.wait_ge(pvb_done, p * (STEPS - 2))
                if A:
                    for rg in range(4):
                        for j in range(NCB):
                            v = io["v_d"][0:LAT, :].rearrange("(r c) n -> r c n", c=GRID_W)
                            sp.dma_start(vw[:, rg * NCB + j, :].bitcast(F32),
                                         v[4 * rg:4 * rg + 4, KC0[j]:KC0[j] + KC, bass.ds(p * 256, 256)]
                                         ).then_inc(vw_in, 16)
                    sp.dma_start(vp[:, :, :].bitcast(F32),
                                 io["v_d"][LAT:TOK, bass.ds(p * 256, 256)].rearrange("(t p) n -> p t n", p=P)
                                 ).then_inc(vw_in, 16)
                else:
                    v = io["v_d"][:, bass.ds(kv * 128 + 1024, 128)]
                    sp.dma_start(vw[:, :, :].bitcast(F32), v[0:LAT, :].rearrange("(t p) n -> p t n", p=P)).then_inc(vw_in, 16)
                    sp.dma_start(vp[:, :, :].bitcast(F32), v[LAT:TOK, :].rearrange("(t p) n -> p t n", p=P)).then_inc(vw_in, 16)
                if A:
                    sp.wait_ge(comb_done, p * 12)
                    sp.dma_start(rb[:, :, :], io["bias"][p * 2]).then_inc(rb_in, 16)
                for i in range(2, TILES):
                    load_tile(i)
                    if i == 2:
                        src = io["w_q"][p + base + 1]
                        sp.wait_ge(c_split, p * 3 + 3)
                        sp.dma_start(craw[:, :], src).then_inc(q_in, 16)
                if A:
                    sp.wait_ge(comb_done, p * 12 + 6)
                    sp.dma_start(rb[:, :, :], io["bias"][p * 2 + 1]).then_inc(rb_in, 16)

        @block.gpsimd
        def _(pool):
            pool.memset(one[:, :], 1.0).then_inc(ones_set, 1)
            pool.wait_ge(ones_set, 1)
            if A:
                pool.wait_ge(const_in, 32)
            with pool.Fori(0, PAIRS) as p:
                def split_tile(i):
                    pool.wait_ge(w_in, (p * (TILES - 1) + i) * 16)
                    pool.wait_ge(w_begun, p * TILES + slot_free(i))
                    w = wkg[:, SLOT[i] - 1]
                    split(pool, w[:, 0, :], w[:, 1, :], wraw[:, :], one, w_hi, p * TILES + i, w_lo)

                def split_next_q():
                    pool.wait_ge(q_in, (p + 1) * 16)
                    pool.wait_ge(w_begun, p * TILES + 2)
                    split(pool, wq[:, 0, :], wq[:, 1, :], craw[:, :], one, w_hi, (p + 1) * TILES, w_lo)

                def bias(h, ty):
                    n = 3 * h + ty
                    if ty == 0:
                        pool.wait_ge(rb_in, (p * 2 + h + 1) * 16)
                    if n >= 2:
                        pool.wait_ge(m_done, p * 2 * STEPS + 4 + [2, 6, 8, 10][n - 2])
                    for t in range(2):
                        b = rb[:, (4 if t == 0 else 0):(4 if t == 0 else 0) + KR, TYPE_OFF[ty] + 16:TYPE_OFF[ty] + 16 + KC]
                        c = comb[:, n % 2, t, :].rearrange("p (r c) -> p r c", c=KC)
                        rm = rowm[:, t, :].rearrange("p (r o) -> p r o", o=1).to_broadcast([P, KR, KC])
                        cm = colm[:, ty:ty + 1, :].to_broadcast([P, KR, KC])
                        pool.tensor_tensor(c, rm, b, ALU.subtract).then_inc(comb_t, 1)
                        pool.wait_ge(comb_t, p * 12 + 2 * n + t + 1)
                        pool.tensor_tensor(c, c, cm, ALU.add).then_inc(comb_done, 1)

                if A:
                    split_tile(1)
                    pool.wait_ge(m_done, p * 2 * STEPS)
                    bias(0, 0)
                    bias(0, 1)
                    split_tile(2)
                    split_tile(3)
                    bias(0, 2)
                    bias(1, 0)
                    bias(1, 1)
                    split_tile(4)
                    split_next_q()
                    bias(1, 2)
                else:
                    for i in range(PROJ, TILES):
                        split_tile(i)
                    split_next_q()

        @block.tensor
        def _(pe):
            with pe.Fori(0, PAIRS) as p:
                pe.wait_ge(exp_done, p * 2 * STEPS)

                def project(n):
                    i, g, bank = PROJECTED[n]
                    t0, tn = GROUPS[g]
                    if n % 3 == 0:
                        pe.wait_ge(w_lo, p * TILES + i)
                    earlier = [m for m in range(n) if PROJECTED[m][2] == bank]
                    if earlier:
                        pe.wait_ge(x_used, p * NG + earlier[-1] + 1)
                    mm = split_mm(pe, s_ps[:, bank, 0:tn], lambda a, k: wt(i, a, k),
                                  lambda b, k: hm[:, b, k, t0:t0 + tn], KD, w_begun if n % 3 == 0 else None)
                    mm.then_inc(proj_done, 1)

                def unit(u):
                    i, t0 = PROJ + u // UNITS, (u % UNITS) * UNIT
                    if u % UNITS == 0:
                        pe.wait_ge(w_lo, p * TILES + i)
                    pe.wait_ge(g_done, p * GPP * UNITS + u)
                    mm = split_mm(pe, d_ps[:, 0:UNIT], lambda a, k: wt(i, a, k),
                                  lambda b, k: hm[:, b, k, t0:t0 + UNIT], KD, w_begun if u % UNITS == 0 else None)
                    mm.then_inc(d_done, 1)

                def score(s, t, out, rhs):
                    if s < 2:
                        h, cols = s, lambda ap: ap[..., LAT + t * P:LAT + (t + 1) * P]
                    elif A:
                        h, cols = (s - 2) // 4, lambda ap: ap[..., (4 * t + (s - 2) % 4) * P:(4 * t + (s - 2) % 4 + 1) * P]
                    else:
                        h, cols = t, lambda ap: ap[..., (s - 2) * P:(s - 1) * P]
                    r0 = HD * h
                    pe.matmul(out, cols(q1[:, h, :]), rhs(h, slice(0, P)), start=True, stop=False)
                    return pe.matmul(out, cols(q2[r0:r0 + HD, :]), rhs(h, slice(r0, r0 + HD)), start=False, stop=True)

                def scores(s):
                    if s == 0:
                        pe.wait_ge(x_used, p * NG + PROMPT_READY)
                        if not A:
                            pe.wait_ge(kk_in, (p + 1) * 64)
                    else:
                        if s == 2:
                            pe.wait_ge(x_used, p * NG + NG)
                            pe.wait_ge(c_split, p * 3 + 3)
                        pe.wait_ge(exp_done, p * 2 * STEPS + 2 * s)
                    for t in range(2):
                        if s < 2:
                            mm = score(s, t, s_ps[:, 2 * t, 0:PROMPT], lambda h, r: kk[r, h, LAT:TOK])
                            continue
                        score(s, t, s_ps[:, 2 * t + s % 2, :], lambda h, r: kc[r, h, :])
                        if A:
                            j = (s - 2) % 4
                            mm = score(s, t, near_bank(s, t),
                                       lambda h, r: grid(kk[r, h, :], 4 * t, KR, KC0[j], KC))
                        else:
                            w0 = min(max(s - 3, 0), 5) * P
                            mm = score(s, t, near_bank(s, t), lambda h, r: kk[r, h, w0:w0 + NB])
                    mm.then_inc(s_done, 1)

                def transposes(s, c):
                    n = CHUNK0[s] + c
                    if c == 0:
                        pe.wait_ge(p_done, p * 2 * STEPS + 2 * s + 2)
                    if n >= 2:
                        pe.wait_ge(lo_done, p * NCHUNK + n - 1)
                    for b, (kb, t) in enumerate(chunk_blocks(s)[c]):
                        mm = pe.transpose(t_ps[:, n % 2, b * P:(b + 1) * P], probs_block(s, t, kb), ident[:, :])
                    mm.then_inc(t_done, 1)

                def weighted(s, half):
                    if s == 0:
                        pe.wait_ge(vw_in, (p + 1) * 16 * (17 if A else 2))
                    last_chunk = CHUNKS[s] if half or s < 2 else 2
                    pe.wait_ge(lo_done, p * NCHUNK + CHUNK0[s] + last_chunk)
                    if half == 0:
                        pe.wait_ge(o_done, p * STEPS + s)
                    if s < 2:
                        h = s if A else 0
                        work = [(vp[:, kb, h * P:(h + 1) * P], 2 * kb, 0, 2) for kb in range(2)]
                    elif half == 0:
                        h = (s - 2) // 4 if A else 0
                        work = [(vc[:, kb, h, :], 2 * kb, 0, 2) for kb in range(4)]
                    elif A:
                        h, j = (s - 2) // 4, (s - 2) % 4
                        work = [(vw[:, rg * NCB + j, h * P:(h + 1) * P], b0, c0, nb)
                                for rg, b0, c0, nb in ((0, 8, 0, 1), (1, 9, 0, 2), (2, 11, 0, 2), (3, 13, 1, 1))]
                    else:
                        w0 = min(max(s - 3, 0), 5)
                        work = [(vw[:, w0 + kb, :], 8 + 2 * kb, 0, 2) for kb in range(3)]
                    for n, (v, b0, c0, nb) in enumerate(work):
                        for part in range(2):
                            mm = pe.matmul(o_ps[:, c0 * P:(c0 + nb) * P], v, pt[:, part, b0 * P:(b0 + nb) * P],
                                           start=(half == 0 and n == 0 and part == 0),
                                           stop=((half == 1 or s < 2) and n == len(work) - 1 and part == 1),
                                           skip_group_check=True)
                    mm.then_inc(pvb_done if half else pva_done, 1)

                for n in range(NG):
                    if n == EARLY:
                        scores(0)
                    project(n)
                for s in range(STEPS + 1):
                    if s < STEPS and not (s == 0 and EARLY):
                        scores(s)
                    if 4 <= s < STEPS:
                        weighted(s - 2, 1)
                    if s == STEPS:
                        unit(s)
                    if s > 0:
                        for c in range(min(2, CHUNKS[s - 1])):
                            transposes(s - 1, c)
                    if s < STEPS:
                        unit(s)
                    else:
                        weighted(s - 2, 1)
                    if s > 0:
                        for c in range(2, CHUNKS[s - 1]):
                            transposes(s - 1, c)
                        weighted(s - 1, 0)
                unit(STEPS + 1)
                weighted(STEPS - 1, 1)

        @block.scalar
        def _(act):
            if A:
                act.dma_start(rowm[:, :, :], io["rowmask"]).then_inc(const_in, 16)
                act.dma_start(colm[:, :, :], io["colmask"]).then_inc(const_in, 16)
            else:
                act.dma_start(sink[:, :], io["sink"].to_broadcast([P, 8])).then_inc(sink_in, 16)
                act.dma_start(cos[:, :], io["cos"]).then_inc(const_in, 16)
                act.dma_start(sin[:, :], io["sin"]).then_inc(const_in, 16)
                act.dma_start(band[:, :, :], io["band"]).then_inc(band_in, 16)
            with act.Fori(0, PAIRS) as p:
                def split_caches():
                    act.wait_ge(craw_in, (p + 1) * 32)
                    for h in range(2):
                        r0 = HD * h
                        act.activation(kc[r0:r0 + HD, h, :], craw[r0:r0 + HD, 0:PAST], ACT.Copy,
                                       scale=QSCALE if A else 1.0).then_inc(ckh, 1)
                    act.activation(vc[:, :, :, 0:HD],
                                   craw[:, PAST:PAST + 4 * CH * HD].rearrange("p (b h c) -> p b h c", h=CH, c=HD),
                                   ACT.Copy).then_inc(cvh, 1)

                def projected(n):
                    _, g, bank = PROJECTED[n]
                    t0, tn = GROUPS[g]
                    tok, bank = slice(t0, t0 + tn), s_ps[:, bank, 0:tn]
                    act.wait_ge(proj_done, p * NG + n + 1)
                    if A and n < 3:
                        act.activation(tiled(q1[0:HD, 0, tok]), rows(bank[0:HD, :]), ACT.Copy).then_inc(xa, 1)
                        act.wait_ge(xd, p * 9 + 2 * n + 1)
                        act.activation(tiled(q1[0:HD, 1, tok]), rows(bank[HD:P, :]), ACT.Copy).then_inc(xa, 1)
                    elif A:
                        act.activation(kk[0:HD, 0, tok], bank[0:HD, :], ACT.Copy, scale=QSCALE).then_inc(xa, 1)
                    else:
                        if g == 2:
                            act.wait_ge(x_used, p * NG)
                        else:
                            act.wait_ge(r_swp, p * 2 + g)
                        act.activation((rot if g == 2 else raw)[:, 0:tn], bank, ACT.Copy, scale=QSCALE).then_inc(r_raw, 1)
                        if n == EARLY:
                            exps(0)
                            gate(0)
                        if g == 2:
                            act.wait_ge(r_raw, p * 3 + n + 1)
                        else:
                            act.wait_ge(r_rot, p * 2 + g + 1)
                        for h in range(2):
                            act.activation(q1[0:HD, h, tok], rot[h * HD:(h + 1) * HD, 0:tn], ACT.Copy
                                           ).then_inc(xa, 1)

                def high(s, chunks):
                    for c in chunks:
                        n = CHUNK0[s] + c
                        cols = len(chunk_blocks(s)[c]) * P
                        act.wait_ge(t_done, p * NCHUNK + n + 1)
                        if c == 0:
                            act.wait_ge(pva_done, p * STEPS + s)
                        if c == 2:
                            act.wait_ge(pvb_done, p * (STEPS - 2) + s - 2)
                        act.activation(pt[:, 0, c * 512:c * 512 + cols], t_ps[:, n % 2, 0:cols], ACT.Copy
                                       ).then_inc(hi_done, 1)

                def exps(s):
                    for t in range(2):
                        n = p * 2 * STEPS + 2 * s + t + 1
                        act.wait_ge(m_done, n)
                        if t == 0:
                            act.wait_ge(t_done, p * NCHUNK + (CHUNK0[s - 1] + min(2, CHUNKS[s - 1]) if s > 0 else 0))
                            act.wait_ge(r_done, p * STEPS + s)
                        act.activation(probs_run(s, t), scores_run(s, t), ACT.Exp, bias=mx[:, t:t + 1], scale=-1.0,
                                       accum_out=den[:, t:t + 1]).then_inc(exp_done, 1)
                        if not A:
                            h = s if s < 2 else t
                            act.activation(esk[:, t:t + 1], nsk[:, h:h + 1], ACT.Exp, bias=mx[:, t:t + 1], scale=-1.0
                                           ).then_inc(esk_done, 1)

                def gate_out(u):
                    act.wait_ge(g_done, p * GPP * UNITS + u + 1)
                    blk = (p + base) * GPP + u // UNITS
                    act.dma_start(io["gates_d"][blk, :, (u % UNITS) * UNIT:(u % UNITS + 1) * UNIT], gst[:, u % 2, :]
                                  ).then_inc(g_out[u % 2], 16)

                def gate(u):
                    act.wait_ge(d_done, p * GPP * UNITS + u + 1)
                    act.wait_ge(g_out[u % 2], (p * (GPP * UNITS // 2) + u // 2) * 16)
                    act.activation(gst[:, u % 2, :], d_ps[:, 0:UNIT], ACT.Copy).then_inc(g_done, 1)
                    if u > 0:
                        gate_out(u - 1)

                def low_half(s):
                    if s < 2:
                        act.wait_ge(pva_done, p * STEPS + s + 1)
                    else:
                        act.wait_ge(pvb_done, p * (STEPS - 2) + s - 1)
                    act.wait_ge(o_done, p * STEPS + s)
                    act.activation(otmp[:, :], o_ps[HD:P, 0:2 * P], ACT.Copy).then_inc(ot_done, 1)

                for n in range(NG):
                    if n == (0 if A else 1):
                        split_caches()
                    projected(n)
                if A:
                    act.wait_ge(ko_done, p + 1)
                    act.dma_start(io["new_ak"][p], kout[:, :]).then_inc(ko_out, 16)
                for s in range(STEPS + 1):
                    if s == STEPS:
                        gate(s)
                    elif s >= 2:
                        low_half(s - 2)
                    if s > 0:
                        high(s - 1, range(min(2, CHUNKS[s - 1])))
                    if s < STEPS and not (s == 0 and EARLY):
                        exps(s)
                        gate(s)
                    if s == STEPS:
                        low_half(s - 2)
                    if s > 0:
                        high(s - 1, range(2, CHUNKS[s - 1]))
                gate(STEPS + 1)
                gate_out(STEPS + 1)
                low_half(STEPS - 1)
                act.wait_ge(o_done, (p + 1) * STEPS)
                act.dma_start(io["o_d"][p + base], ost[:, :]).then_inc(o_out, 16)
            act.wait_ge(g_out[0], PAIRS * GPP * UNITS // 2 * 16)
            act.wait_ge(g_out[1], PAIRS * GPP * UNITS // 2 * 16)
            act.wait_ge(o_out, PAIRS * 16)
            if A:
                act.wait_ge(ko_out, PAIRS * 16)

        @block.vector
        def _(dve):
            if not A:
                dve.wait_ge(sink_in, 16)
                dve.tensor_scalar(nsink[:, :], sink[:, :], -1.0, None, ALU.mult).then_inc(nsk_done, 1)
                dve.wait_ge(nsk_done, 1)
            with dve.Fori(0, PAIRS) as p:
                if not A:
                    dve.tensor_copy(nsk[:, :], nsink[:, bass.ds(p * 2, 2)]).then_inc(nsk_done, 1)
                def split_caches():
                    for h in range(2):
                        r0, r1 = HD * h, HD * (1 - h)
                        dve.wait_ge(ckh, p * 2 + h + 1)
                        dve.scalar_tensor_tensor(out=kc[r1:r1 + HD, h, :], in0=craw[r0:r0 + HD, 0:PAST],
                                                 scalar=QSCALE if A else 1.0, in1=kc[r0:r0 + HD, h, :].bitcast(F32),
                                                 op0=ALU.mult, op1=ALU.subtract).then_inc(c_split, 1)
                    dve.wait_ge(cvh, p + 1)
                    dve.tensor_tensor(vc[:, :, :, HD:],
                                      craw[:, PAST:PAST + 4 * CH * HD].rearrange("p (b h c) -> p b h c", h=CH, c=HD),
                                      vc[:, :, :, 0:HD].bitcast(F32), ALU.subtract).then_inc(c_split, 1)

                def projected(n):
                    _, g, bank = PROJECTED[n]
                    t0, tn = GROUPS[g]
                    tok, bank = slice(t0, t0 + tn), s_ps[:, bank, 0:tn]
                    if A:
                        dve.wait_ge(proj_done, p * NG + n + 1)
                    if A and n < 3:
                        dve.tensor_copy(tiled(q1[HD:P, 1, tok]), rows(bank[HD:P, :])).then_inc(xd, 1)
                        dve.wait_ge(xa, p * 9 + 2 * n + 1)
                        dve.tensor_copy(tiled(q1[HD:P, 0, tok]), rows(bank[0:HD, :])).then_inc(xd, 1)
                        dve.tensor_tensor(tiled(q2[0:HD, tok]), rows(bank[0:HD, :]), tiled(q1[0:HD, 0, tok]).bitcast(F32),
                                          ALU.subtract)
                        dve.wait_ge(xa, p * 9 + 2 * n + 2)
                        dve.wait_ge(xd, p * 9 + 2 * n + 1)
                        dve.tensor_tensor(tiled(q2[HD:P, tok]), rows(bank[HD:P, :]), tiled(q1[HD:P, 1, tok]).bitcast(F32),
                                          ALU.subtract).then_inc(x_used, 1)
                    elif A:
                        dve.tensor_scalar(kk[HD:P, 1, tok], bank[HD:P, :], QSCALE, None, ALU.mult).then_inc(xd, 1)
                        dve.wait_ge(xa, p * 9 + n + 4)
                        dve.wait_ge(xd, p * 9 + n + 4)
                        if g == 2:
                            dve.wait_ge(ko_out, p * 16)
                            dve.tensor_copy(kout[:, :], bank).then_inc(ko_done, 1)
                        for h in range(2):
                            r = slice(h * HD, (h + 1) * HD)
                            last = dve.scalar_tensor_tensor(
                                out=kk[(1 - h) * HD:(2 - h) * HD, h, tok], in0=bank[r, :], scalar=QSCALE,
                                in1=kk[r, h, tok].bitcast(F32), op0=ALU.mult, op1=ALU.subtract)
                        last.then_inc(x_used, 1)
                    else:
                        dve.wait_ge(r_raw, p * 3 + n + 1)
                        if g < 2:
                            dve.wait_ge(const_in, 32)
                            dve.wait_ge(x_used, p * NG + n)
                            dve.tensor_tensor(rot[:, :], raw[:, :], cos[:, tok], ALU.mult).then_inc(r_cos, 1)
                            dve.stream_shuffle(swp[:, :], raw[:, :], SWAP16).then_inc(r_swp, 1)
                            dve.wait_ge(r_swp, p * 2 + g + 1)
                            dve.tensor_tensor(swp[:, :], swp[:, :], sin[:, tok], ALU.mult).then_inc(r_sin, 1)
                            dve.wait_ge(r_sin, p * 2 + g + 1)
                            dve.wait_ge(r_cos, p * 2 + g + 1)
                            dve.tensor_tensor(rot[:, :], rot[:, :], swp[:, :], ALU.add).then_inc(r_rot, 1)
                            dve.wait_ge(r_rot, p * 2 + g + 1)
                        if n == EARLY:
                            normalise(0)
                        for h in range(2):
                            dve.tensor_copy(q1[HD:P, h, tok], rot[h * HD:(h + 1) * HD, 0:tn]).then_inc(xd, 1)
                        dve.wait_ge(xa, p * 6 + 2 * n + 2)
                        dve.wait_ge(xd, p * 6 + 2 * n + 2)
                        for h in range(2):
                            r = slice(h * HD, (h + 1) * HD)
                            last = dve.tensor_tensor(q2[r, tok], rot[r, 0:tn], q1[r, h, tok].bitcast(F32), ALU.subtract)
                        last.then_inc(x_used, 1)

                def low(s, chunks):
                    for c in chunks:
                        n = CHUNK0[s] + c
                        cols = len(chunk_blocks(s)[c]) * P
                        dve.wait_ge(hi_done, p * NCHUNK + n + 1)
                        dve.tensor_tensor(pt[:, 1, c * 512:c * 512 + cols], t_ps[:, n % 2, 0:cols],
                                          pt[:, 0, c * 512:c * 512 + cols].bitcast(F32), ALU.subtract).then_inc(lo_done, 1)

                def minima(s):
                    width = PROMPT if s < 2 else PAST
                    dve.wait_ge(s_done, p * STEPS + s + 1)
                    ctx_min = mx if A and s < 2 else mn
                    if A and s >= 2:
                        h, j = (s - 2) // 4, (s - 2) % 4
                        n = 3 * h + BIAS_TYPE[j]
                        dve.wait_ge(comb_done, p * 12 + 2 * n + 2)
                    red = dve.tensor_reduce(ctx_min[:, :],
                                            s_ps[:, :, :].rearrange("p (t b) c -> p t b c", b=2)[:, :, s % 2 if s >= 2 else 0, 0:width],
                                            AX.X, ALU.min)
                    if A and s < 2:
                        red.then_inc(m_done, 2)
                        return
                    red.then_inc(m1_done, 1)
                    if s >= 2:
                        if not A:
                            dve.wait_ge(band_in, 16)
                        for t in range(2):
                            near = comb[:, n % 2, t, :] if A else \
                                band[:, 0 if s == 2 else 2 if s == STEPS - 1 else 1, :]
                            bank = near_bank(s, t)
                            red = dve.tensor_tensor_reduce(bank, bank, near, 1.0, BIG, ALU.add, ALU.min, nm[:, t:t + 1])
                        red.then_inc(m2_done, 1)
                    if A:
                        dve.wait_ge(m1_done, p * (STEPS - 2) + s - 1)
                        dve.wait_ge(m2_done, p * (STEPS - 2) + s - 1)
                        dve.tensor_tensor(mx[:, :], mn[:, :], nm[:, :], ALU.min).then_inc(m_done, 2)
                        return
                    dve.wait_ge(m1_done, p * STEPS + s + 1)
                    if s < 2:
                        sk = nsk[:, s:s + 1].to_broadcast([P, 2])
                    else:
                        sk = nsk[:, :]
                        dve.wait_ge(m2_done, p * (STEPS - 2) + s - 1)
                        dve.tensor_tensor(nm[:, :], mn[:, :], nm[:, :], ALU.min).then_inc(m3_done, 1)
                        dve.wait_ge(m3_done, p * (STEPS - 2) + s - 1)
                    if s == 0:
                        dve.wait_ge(nsk_done, p + 2)
                    dve.tensor_tensor(mx[:, :], (mn if s < 2 else nm)[:, :], sk, ALU.min).then_inc(m_done, 2)

                def normalise(s):
                    dve.wait_ge(exp_done, p * 2 * STEPS + 2 * s + 2)
                    if s > 0:
                        dve.wait_ge(p_done, p * 2 * STEPS + 2 * s)
                    if A:
                        dve.reciprocal(rden[:, :], den[:, :]).then_inc(r_done, 1)
                    else:
                        dve.wait_ge(esk_done, p * 2 * STEPS + 2 * s + 2)
                        dve.tensor_tensor(den2[:, :], den[:, :], esk[:, :], ALU.add).then_inc(den_done, 1)
                        dve.wait_ge(den_done, p * STEPS + s + 1)
                        dve.reciprocal(rden[:, :], den2[:, :]).then_inc(r_done, 1)
                    dve.wait_ge(r_done, p * STEPS + s + 1)
                    for t in range(2):
                        dve.tensor_scalar(probs_run(s, t), probs_run(s, t), rden[:, t:t + 1], None, ALU.mult
                                          ).then_inc(p_done, 1)

                def add_halves(s):
                    dve.wait_ge(ot_done, p * STEPS + s + 1)
                    if s == 0:
                        dve.wait_ge(o_out, p * 16)
                    if s < 2:
                        dve.tensor_tensor(ost[HD * s:HD * s + HD, LAT:TOK], o_ps[0:HD, 0:2 * P], otmp[:, :], ALU.add
                                          ).then_inc(o_done, 1)
                    elif A:
                        h, j = (s - 2) // 4, (s - 2) % 4
                        dst = grid(ost[HD * h:HD * h + HD, :], 0, ROWS, QC * j, QC)
                        dve.tensor_tensor(dst, o_ps[0:HD, 0:2 * P].rearrange("p (r c) -> p r c", c=QC),
                                          otmp[:, :].rearrange("p (r c) -> p r c", c=QC), ALU.add).then_inc(o_done, 1)
                    else:
                        for t in range(2):
                            last = dve.tensor_tensor(ost[HD * t:HD * t + HD, (s - 2) * P:(s - 1) * P],
                                                     o_ps[0:HD, t * P:(t + 1) * P], otmp[:, t * P:(t + 1) * P], ALU.add)
                        last.then_inc(o_done, 1)

                for n in range(NG):
                    if n == (0 if A else 1):
                        split_caches()
                    if n == EARLY:
                        minima(0)
                    projected(n)
                for s in range(STEPS + 1):
                    if s < STEPS and not (s == 0 and EARLY):
                        minima(s)
                    if 2 <= s < STEPS:
                        add_halves(s - 2)
                    if s > 0:
                        low(s - 1, range(min(2, CHUNKS[s - 1])))
                    if s == STEPS:
                        add_halves(s - 2)
                    if s < STEPS and not (s == 0 and EARLY):
                        normalise(s)
                    if s > 0:
                        low(s - 1, range(2, CHUNKS[s - 1]))
                add_halves(STEPS - 1)


def finish(nc, io):
    with ExitStack() as ctx:
        def sb(name, shape, dt=F32):
            return ctx.enter_context(nc.sbuf_tensor(f"{name}_f", shape, dt))

        def sem(name):
            return nc.alloc_semaphore(name=f"{name}_f")

        CT = 256
        CHUNKS_ = TOK // CT
        PIECES = 4
        GSLOTS = 4
        wb = sb("wb", [P, 2, KD, D], F32R)
        wo = sb("wo", [P, 2, KD, D], F32R)
        og = sb("og", [P, 2, KD, CT], F32R)
        oz = sb("oz", [P, 2, 2, 2, CT])
        gt = sb("gt", [P, GSLOTS, 2, CT])
        tp = sb("tp", [P, 2, 2, CT])
        mg = sb("mg", [P, 2, KD, CT], F32R)
        x, y = sb("x", [P, 2, D]), sb("y", [P, 2, D])
        gate, gain = sb("gate", [P, D]), sb("gain", [P, D])
        ss, rms, rstd = sb("ss", [P, 2]), sb("rms", [P, 2]), sb("rstd", [P, 2])
        epsc = sb("eps", [P, 1])
        b_ps = ctx.enter_context(nc.psum_tensor("b_ps", [P, 2, 2, 512], F32))
        y_ps = ctx.enter_context(nc.psum_tensor("y_ps", [P, 2, D], F32))

        w_in = [sem(f"w_in{s}") for s in range(4)]
        w_hi, w_lo_dve, w_lo_pool = sem("w_hi"), sem("w_lo_dve"), sem("w_lo_pool")
        oz_in = [sem("oz_in0"), sem("oz_in1")]
        silu_done, og_prod, og_hi, og_lo = (sem(n) for n in ("silu", "og_prod", "og_hi", "og_lo"))
        gt_in = [sem(f"gt_in{s}") for s in range(GSLOTS)]
        sig_done, b_done, b_prod, summed, mg_hi, mg_lo = (
            sem(n) for n in ("sig", "b_done", "b_prod", "summed", "mg_hi", "mg_lo"))
        x_in, y_out = [sem("x_in0"), sem("x_in1")], [sem("y_out0"), sem("y_out1")]
        gate_in, gain_in, eps_set = sem("gate_in"), sem("gain_in"), sem("eps_set")
        y_mm, gated, res, sq_done, rms_done, r_done, y_done = (
            sem(n) for n in ("y_mm", "gated", "res", "sq", "rms", "r", "y"))
        block = ctx.enter_context(nc.Block())

        WT = 2 * KD
        DVE_TILES = [m for m in range(WT) if m < KD or m % 2 == 0]
        POOL_TILES = [m for m in range(WT) if m not in DVE_TILES]
        AHEAD = 3
        EXTRA = [[3], [4, 5], [6], [7, 8], [9], [10, 11], [12], [13, 14], [15]]

        def raw_w(m):
            return (x, y)[m % 4 // 2][:, m % 2, :]

        def parts(m):
            w = wb if m < KD else wo
            return w[:, 0, m % KD, :], w[:, 1, m % KD, :]

        def wait_split(eng, m):
            if m in DVE_TILES:
                eng.wait_ge(w_lo_dve, DVE_TILES.index(m) + 1)
            else:
                eng.wait_ge(w_lo_pool, POOL_TILES.index(m) + 1)

        def turns(eng, body):
            body(0, True, False)
            with eng.Fori(1, CHUNKS_ - 1) as i:
                body(i, False, False)
            body(CHUNKS_ - 1, False, True)

        @block.sync
        def _(sp):
            def load_w(m):
                if m >= 4:
                    wait_split(sp, m - 4)
                src = io["w_br"][m] if m < KD else io["w_out"][:, m - KD, :]
                sp.dma_start(raw_w(m), src).then_inc(w_in[m % 4], 16)

            def load_oz(i, n):
                tok = bass.ds(i * CT, CT)
                srcs = [io[d][2 * n:2 * n + 2, :, tok].rearrange("b p t -> p b t") for d in ("o_d", "gates_d")]
                if not (isinstance(i, int) and i == 0 and n < 2):
                    sp.wait_ge(og_lo, i * PIECES + n - 1)
                for which in range(2):
                    sp.dma_start(oz[:, n % 2, which, :, :], srcs[which]).then_inc(oz_in[n % 2], 16)

            def load_gt(i, j):
                src = io["gates_d"][8:24, :, bass.ds(i * CT, CT)].rearrange("(w j) p t -> j p w t", w=2)[j]
                if not (isinstance(i, int) and i == 0 and j < GSLOTS):
                    sp.wait_ge(b_prod, i * 2 * KD + 2 * (j - GSLOTS + 1))
                sp.dma_start(gt[:, j % GSLOTS, :, :], src).then_inc(gt_in[j % GSLOTS], 16)

            load_oz(0, 0)
            load_oz(0, 1)
            load_w(0)
            load_w(1)
            load_oz(0, 2)
            load_oz(0, 3)
            for j in range(GSLOTS):
                load_gt(0, j)
                load_w(j + 2)

            def body(i, first, last):
                for j in range(GSLOTS, KD):
                    if first:
                        load_w(2 * j - 2)
                        load_w(2 * j - 1)
                    load_gt(i, j)
                if first:
                    load_w(WT - 2)
                    load_w(WT - 1)
                    sp.dma_start(gain[:, :], io["gain"].to_broadcast([P, D])).then_inc(gain_in, 16)
                if not last:
                    load_oz(i + 1, 0)
                    load_oz(i + 1, 1)
                for e in range(2):
                    src = io["x"][bass.ds(i * CT + e * P, P), :]
                    if first:
                        wait_split(sp, WT - 4 + e)
                    else:
                        sp.wait_ge(sq_done, i * 2 + e - 1)
                    sp.dma_start(x[:, e, :], src).then_inc(x_in[e], 16)
                stream = io["gate_d"][bass.ds(i // (LAT // CT), 1), :].to_broadcast([P, D])
                if not first:
                    sp.wait_ge(gated, i * 4)
                sp.dma_start(gate[:, :], stream).then_inc(gate_in, 16)
                if not last:
                    load_oz(i + 1, 2)
                    load_oz(i + 1, 3)
                    for j in range(GSLOTS):
                        load_gt(i + 1, j)
                for e in range(2):
                    dst = io["y"][bass.ds(i * CT + e * P, P), :]
                    sp.wait_ge(y_done, i * 2 + e + 1)
                    sp.dma_start(dst, y[:, e, :]).then_inc(y_out[e], 16)

            turns(sp, body)
            sp.wait_ge(y_out[0], CHUNKS_ * 16)
            sp.wait_ge(y_out[1], CHUNKS_ * 16)

        @block.scalar
        def _(act):
            def silu(i, n):
                act.wait_ge(oz_in[n % 2], (i * (PIECES // 2) + n // 2 + 1) * 32)
                act.activation(oz[:, n % 2, 1, :, :], oz[:, n % 2, 1, :, :], ACT.Silu).then_inc(silu_done, 1)

            def high(m):
                act.wait_ge(w_in[m % 4], (m // 4 + 1) * 16)
                act.activation(parts(m)[0], raw_w(m), ACT.Copy).then_inc(w_hi, 1)

            def sigmoid(i, j):
                act.wait_ge(gt_in[j % GSLOTS], (i * (KD // GSLOTS) + j // GSLOTS + 1) * 16)
                act.activation(gt[:, j % GSLOTS, :, :], gt[:, j % GSLOTS, :, :], ACT.Sigmoid).then_inc(sig_done, 1)

            silu(0, 0)
            silu(0, 1)
            high(0)
            silu(0, 2)
            silu(0, 3)
            high(1)
            high(2)
            act.wait_ge(eps_set, 1)

            def body(i, first, last):
                sigmoid(i, 0)
                for j in range(KD):
                    if j + 1 < KD:
                        sigmoid(i, j + 1)
                    if first:
                        for m in EXTRA[j]:
                            high(m)
                    act.wait_ge(summed, i * KD + j + 1)
                    act.activation(mg[:, 0, j, :], tp[:, j % 2, 0, :], ACT.Copy).then_inc(mg_hi, 1)
                if first:
                    for m in EXTRA[KD]:
                        high(m)
                if not last:
                    for n in range(PIECES):
                        silu(i + 1, n)
                for e in range(2):
                    act.wait_ge(res, i * 4 + 2 * e + 2)
                    act.activation(x[:, e, :], y[:, e, :], ACT.Square, accum_out=ss[:, e:e + 1]).then_inc(sq_done, 1)
                    act.wait_ge(sq_done, i * 2 + e + 1)
                    if not first:
                        act.wait_ge(r_done, i * 2 + e - 1)
                    act.activation(rms[:, e:e + 1], ss[:, e:e + 1], ACT.Sqrt, bias=epsc[:, 0:1], scale=1.0 / D
                                   ).then_inc(rms_done, 1)

            turns(act, body)

        @block.gpsimd
        def _(pool):
            def og_low(i, n):
                pool.wait_ge(og_hi, i * PIECES + n + 1)
                pool.tensor_tensor(og[:, 1, 2 * n:2 * n + 2, :], oz[:, n % 2, 0, :, :],
                                   og[:, 0, 2 * n:2 * n + 2, :].bitcast(F32), ALU.subtract).then_inc(og_lo, 1)

            def lows(j):
                for m in EXTRA[j]:
                    if m in POOL_TILES:
                        pool.wait_ge(w_hi, m + 1)
                        hi, lo = parts(m)
                        pool.tensor_tensor(lo, raw_w(m), hi.bitcast(F32), ALU.subtract).then_inc(w_lo_pool, 1)

            pool.memset(epsc[:, :], EPS).then_inc(eps_set, 1)
            for n in range(PIECES):
                og_low(0, n)

            def body(i, first, last):
                for j in range(KD):
                    pool.wait_ge(b_prod, (i * KD + j) * 2 + 2)
                    pool.tensor_tensor(tp[:, j % 2, 0, :], tp[:, j % 2, 0, :], tp[:, j % 2, 1, :], ALU.add
                                       ).then_inc(summed, 1)
                    pool.wait_ge(mg_hi, i * KD + j + 1)
                    pool.tensor_tensor(mg[:, 1, j, :], tp[:, j % 2, 0, :], mg[:, 0, j, :].bitcast(F32), ALU.subtract
                                       ).then_inc(mg_lo, 1)
                    if first:
                        lows(j)
                if first:
                    lows(KD)
                if not last:
                    for n in range(PIECES):
                        og_low(i + 1, n)

            turns(pool, body)

        @block.tensor
        def _(pe):
            def body(i, first, last):
                for j in range(KD):
                    if first:
                        wait_split(pe, j)
                    for br in range(2):
                        if j == 0:
                            pe.wait_ge(og_lo, i * PIECES + 2 * br + 2)
                        if not (first and j < 2):
                            pe.wait_ge(b_prod, 2 * (i * KD + j - 2) + br + 1)
                        split_mm(pe, b_ps[:, j % 2, br, 0:CT],
                                 lambda a, k: wb[:, a, j, (4 * br + k) * P:(4 * br + k + 1) * P],
                                 lambda b, k: og[:, b, 4 * br + k, :], 4).then_inc(b_done, 1)
                for e in range(2):
                    for n in range(2):
                        if not first:
                            pe.wait_ge(gated, i * 4 + 2 * e + n - 3)
                        for k in range(KD):
                            if e == 0 and n == 0:
                                pe.wait_ge(mg_lo, i * KD + k + 1)
                                if first:
                                    wait_split(pe, KD + k)
                            for q, (a, b) in enumerate(((0, 0), (0, 1), (1, 0))):
                                mm = pe.matmul(y_ps[:, e, n * 512:(n + 1) * 512], mg[:, a, k, e * P:(e + 1) * P],
                                               wo[:, b, k, n * 512:(n + 1) * 512],
                                               start=(k == 0 and q == 0), stop=(k == KD - 1 and q == 2))
                        mm.then_inc(y_mm, 1)

            turns(pe, body)

        @block.vector
        def _(dve):
            def gate_o(i, n):
                dve.wait_ge(silu_done, i * PIECES + n + 1)
                dve.tensor_tensor(oz[:, n % 2, 0, :, :], oz[:, n % 2, 0, :, :], oz[:, n % 2, 1, :, :], ALU.mult
                                  ).then_inc(og_prod, 1)
                dve.wait_ge(og_prod, i * PIECES + n + 1)
                if n == 0 and not (isinstance(i, int) and i == 0):
                    dve.wait_ge(b_done, i * 2 * KD)
                dve.tensor_copy(og[:, 0, 2 * n:2 * n + 2, :], oz[:, n % 2, 0, :, :]).then_inc(og_hi, 1)

            def low(m):
                dve.wait_ge(w_hi, m + 1)
                hi, lo = parts(m)
                dve.tensor_tensor(lo, raw_w(m), hi.bitcast(F32), ALU.subtract).then_inc(w_lo_dve, 1)

            def lows(j):
                for m in EXTRA[j]:
                    if m in DVE_TILES:
                        low(m)

            gate_o(0, 0)
            gate_o(0, 1)
            low(0)
            gate_o(0, 2)
            gate_o(0, 3)
            low(1)
            low(2)

            def body(i, first, last):
                for j in range(KD):
                    dve.wait_ge(sig_done, i * KD + j + 1)
                    if not (first and j < 2):
                        dve.wait_ge(mg_lo, i * KD + j - 1)
                    for br in range(2):
                        dve.wait_ge(b_done, (i * KD + j) * 2 + br + 1)
                        dve.tensor_tensor(tp[:, j % 2, br, :], b_ps[:, j % 2, br, 0:CT], gt[:, j % GSLOTS, br, :], ALU.mult
                                          ).then_inc(b_prod, 1)
                    if first:
                        lows(j)
                if first:
                    lows(KD)
                if not last:
                    for n in range(PIECES):
                        gate_o(i + 1, n)
                if first:
                    dve.wait_ge(gain_in, 16)
                dve.wait_ge(gate_in, (i + 1) * 16)
                for e in range(2):
                    dve.wait_ge(x_in[e], (i + 1) * 16)
                    if not first:
                        dve.wait_ge(y_out[e], i * 16)
                    for n in range(2):
                        half = slice(n * 512, (n + 1) * 512)
                        dve.wait_ge(y_mm, i * 4 + 2 * e + n + 1)
                        dve.tensor_tensor(y[:, e, half], y_ps[:, e, half], gate[:, half], ALU.mult).then_inc(gated, 1)
                        dve.wait_ge(gated, i * 4 + 2 * e + n + 1)
                        dve.tensor_tensor(y[:, e, half], y[:, e, half], x[:, e, half], ALU.add).then_inc(res, 1)
                    dve.wait_ge(rms_done, i * 2 + e + 1)
                    dve.reciprocal(rstd[:, e:e + 1], rms[:, e:e + 1]).then_inc(r_done, 1)
                    dve.wait_ge(r_done, i * 2 + e + 1)
                    dve.scalar_tensor_tensor(out=y[:, e, :], in0=y[:, e, :], scalar=rstd[:, e:e + 1], in1=gain[:, :],
                                             op0=ALU.mult, op1=ALU.mult).then_inc(y_done, 1)

            turns(dve, body)


def build(nc, io):
    before = nc.snapshot_sems()
    with ExitStack() as ctx:
        hm = ctx.enter_context(nc.sbuf_tensor("h", [P, 2, KD, TOK], F32R))
        ident = ctx.enter_context(nc.sbuf_tensor("ident_sb", [P, P], F32))
        wq = ctx.enter_context(nc.sbuf_tensor("wq", [P, 2, D], F32R))
        craw = ctx.enter_context(nc.sbuf_tensor("craw", [P, D], F32))
        with ExitStack() as first:
            wv = first.enter_context(nc.sbuf_tensor("wv", [P, 2, KD, VH * HD], F32R))
            wkb = first.enter_context(nc.sbuf_tensor("wkb", [P, 2, D], F32R))
            startup(nc, io, hm, ident, wv, wkb)
            values(nc, io, hm, wv, wkb, wq, craw)
        pairs(nc, io, hm, ident, wq, craw, "a")
        nc.clear_and_free_semaphores(nc.allocated_since(before))
        nc.all_engine_barrier()
        pairs(nc, io, hm, ident, wq, craw, "b")
    finish(nc, io)


def constants():
    c = {"ident": np.eye(P, dtype=np.float32)}
    qr, qc = np.arange(P) // QC, np.arange(P) % QC
    row = np.zeros((P, 2, KR), np.float32)
    for t in range(2):
        r, kr = QR * t + qr[:, None], 4 * t + np.arange(KR)[None]
        start = np.clip(r - NA_KH // 2, 0, ROWS - NA_KH)
        row[:, t] = np.where((kr >= start) & (kr < start + NA_KH), 0.0, BIG)
    col = np.zeros((P, 3, KC), np.float32)
    for ty, j in enumerate(TYPE_BLOCK):
        q, kc = j * QC + qc[:, None], KC0[j] + np.arange(KC)[None]
        start = np.clip(q - NA_KW // 2, 0, GRID_W - NA_KW)
        col[:, ty] = np.where((kc >= start) & (kc < start + NA_KW), 0.0, BIG)
    band = np.zeros((P, 3, NB), np.float32)
    for ty in range(3):
        off = np.arange(NB)[None] - P * ty - np.arange(P)[:, None]
        band[:, ty] = np.where(np.abs(off) <= WINDOW, 0.0, BIG)
    half = HD // 2
    inv = (np.float32(10000.0) ** (-np.arange(0, half, 2, dtype=np.float32) / np.float32(half))).astype(np.float32)
    t = np.arange(LAT)
    pos = np.stack([t // GRID_W, t % GRID_W]).astype(np.float32)
    ang = pos[:, None, :] * inv[None, :, None]
    cos, sin = np.cos(ang).astype(np.float32), np.sin(ang).astype(np.float32)
    c["cos"] = np.tile(np.concatenate([cos, cos], 1).reshape(HD, LAT), (2, 1))
    c["sin"] = np.tile(np.concatenate([-sin, sin], 1).reshape(HD, LAT), (2, 1))
    c["rowmask"], c["colmask"], c["band"] = row, col, band
    return c


def layout(x_prompt, x_sample, cache_a_k, cache_a_v, cache_b_k, cache_b_v, c, c_ctx, w_ada, b_ada, w_in, rpb_a,
           sink_b, w_br_a, w_br_b, w_out, final_norm_g):
    f = lambda a: np.asarray(a)
    a = constants()
    a["x"] = np.concatenate([f(x_sample)[0], f(x_prompt)[0]])
    a["c_col"] = np.stack([f(c)[0], f(c_ctx)], -1).reshape(KD, P, 2).transpose(1, 0, 2)
    a["b_col"] = f(b_ada)[0, :2 * D].reshape(2 * KD, P).T
    a["b_gate"] = f(b_ada)[:, 2 * D:]
    a["w_ada"] = f(w_ada)[0]
    blocks = f(w_in)[0].reshape(KD, P, -1, P).transpose(2, 1, 0, 3).reshape(-1, P, D)
    a["w_q"] = np.concatenate([blocks[0:4], blocks[16:20], np.zeros_like(blocks[0:1])])
    a["w_ka"], a["w_kb"] = blocks[4:8], blocks[20]
    a["w_gate"] = np.concatenate([blocks[12:16], blocks[22:26], blocks[26:42]])
    cols = f(w_in)[0].reshape(KD, P, -1).transpose(1, 0, 2)
    a["w_v"] = np.concatenate([cols[:, :, 1024:1536], cols[:, :, 2688:2816]], -1)
    a["w_br"] = np.concatenate([f(w)[0].reshape(4, P, KD, P).transpose(2, 1, 0, 3) for w in (w_br_a, w_br_b)], 2
                               ).reshape(KD, P, D)
    a["w_out"] = f(w_out)[0].reshape(KD, P, D).transpose(1, 0, 2)
    a["cka"] = f(cache_a_k)[0, 0].transpose(1, 2, 0).reshape(PAIRS, P, PAST)
    a["cva"] = f(cache_a_v)[0, 0].reshape(4, P, PAIRS, P).transpose(2, 1, 0, 3).reshape(PAIRS, P, 4 * P)
    kb = f(cache_b_k)[0, 0].transpose(1, 2, 0)
    a["ckb"] = np.stack([np.concatenate([kb[p // 2]] * 2) for p in range(PAIRS)])
    vb = f(cache_b_v)[0, 0].reshape(4, P, 2, HD).transpose(2, 1, 0, 3).reshape(2, P, 4 * HD)
    a["cvb"] = np.stack([vb[p // 2] for p in range(PAIRS)])
    pad = np.pad(f(rpb_a)[0], ((0, 0), (4, 4), (16, 16)))
    a["bias"] = np.stack([pad[:, QR - 1 - r:QR - 1 - r + BR, QC - 1 - q:QC - 1 - q + BC]
                          for r in range(QR) for q in range(QC)], 1)
    a["sink"] = f(sink_b)
    a["gain"] = f(final_norm_g)[None]
    return {k: np.ascontiguousarray(v) for k, v in a.items()}


SCRATCH = {"v_d": [TOK, VH * 2 * HD], "kb_d": [2, 2, HD, TOK], "gates_d": [GATE_BLOCKS, P, TOK],
           "o_d": [KD, P, TOK], "gate_d": [2, D]}
OUTS = {"y": [TOK, D], "new_ak": [PAIRS, P, PROMPT], "new_av": [PROMPT, 8 * HD], "new_bk": [P, PROMPT],
        "new_bv": [PROMPT, 2 * HD]}


def kernel(**inputs):
    import concourse.bacc as bacc
    from concourse.bass_utils import run_bass_kernel_spmd

    nc = bacc.Bacc("TRN2", target_bir_lowering=False, num_devices=1)
    arrays = {f"in_{k}": v for k, v in layout(**inputs).items()}
    io = {}
    for name, a in arrays.items():
        io[name[3:]] = nc.dram_tensor(name, list(a.shape), mybir.dt.from_np(a.dtype), kind="ExternalInput").ap()
    for name, shape in SCRATCH.items():
        io[name] = nc.dram_tensor(name, shape, F32, kind="Internal").ap()
    for name, shape in OUTS.items():
        io[name] = nc.dram_tensor(name, shape, F32, kind="ExternalOutput").ap()
    build(nc, io)
    got = run_bass_kernel_spmd(nc, [arrays], core_ids=[0]).results[0]
    y = got["y"]
    to_tok = lambda k, h: k.reshape(h, HD, PROMPT).transpose(2, 0, 1)[None, None]
    return (y[LAT:][None], y[:LAT][None], to_tok(got["new_ak"], NA_HEADS),
            got["new_av"].reshape(1, 1, PROMPT, NA_HEADS, HD), to_tok(got["new_bk"], 2),
            got["new_bv"].reshape(1, 1, PROMPT, 2, HD))
```
